# Optimizing a Trainium2 kernel written in Bass

```python
import math
import jax
import jax.numpy as jnp
from jax import lax
import numpy as np
import jax, jax.numpy as jnp

D_MODEL = 1024
BATCH = 1
SEQ = 256
DEPTH = 1

HEAD_DIM = 64
N_HEADS_FOX = 8
N_HEADS_MOBA = 8
FOX_WIDTH = N_HEADS_FOX * HEAD_DIM
MOBA_WIDTH = N_HEADS_MOBA * HEAD_DIM
MIX_WIDTH = FOX_WIDTH + MOBA_WIDTH
IN_WIDTH = 3 * FOX_WIDTH + 3 * MOBA_WIDTH + N_HEADS_FOX
Q_BLOCK = 128
MOBA_BLOCK = 256
MOBA_TOPK = 3
MOBA_Q_CHUNK = 64
NUM_BUCKETS = 32
MAX_DISTANCE = 128
N_EXPERTS = 32
TOP_K = 4
D_EXPERT = D_MODEL
SWIGLU_LIMIT = 7.0
SWIGLU_ALPHA = 1.702
EXPERT_ROW_BLOCK = 128
RMS_EPS = 1e-6


def rms_norm(x, g):
    x32 = x.astype(jnp.float32)
    y = x32 * lax.rsqrt(jnp.mean(x32 * x32, axis=-1, keepdims=True) + RMS_EPS)
    return (y * g.astype(jnp.float32)).astype(x.dtype)

def t5_bucket(dist):
    dist = jnp.maximum(dist, 0)
    max_exact = NUM_BUCKETS // 2
    d = jnp.maximum(dist, 1).astype(jnp.float32)
    large = max_exact + (jnp.log(d / max_exact) / math.log(MAX_DISTANCE / max_exact)
                         * (NUM_BUCKETS - max_exact)).astype(jnp.int32)
    large = jnp.minimum(large, NUM_BUCKETS - 1)
    return jnp.where(dist < max_exact, dist, large)

def fox_attention(q, k, v, log_f):
    B, S, H, Dh = q.shape
    scale = Dh ** -0.5
    cum = jnp.cumsum(log_f, axis=1)
    cum_h = cum.transpose(0, 2, 1)
    kh = k.transpose(0, 2, 1, 3)
    vh = v.transpose(0, 2, 1, 3)
    nq = S // Q_BLOCK
    qb = q.reshape(B, nq, Q_BLOCK, H, Dh).transpose(1, 0, 3, 2, 4)
    cb = cum.reshape(B, nq, Q_BLOCK, H).transpose(1, 0, 3, 2)
    key_pos = jnp.arange(S)

    def block(args):
        i, qi, ci = args
        s = jnp.einsum('bhqd,bhkd->bhqk', qi, kh).astype(jnp.float32) * scale
        s = s + ci[..., None] - cum_h[:, :, None, :]
        qpos = i * Q_BLOCK + jnp.arange(Q_BLOCK)
        s = jnp.where(key_pos[None, :] <= qpos[:, None], s, -jnp.inf)
        p = jax.nn.softmax(s, axis=-1)
        return jnp.einsum('bhqk,bhkd->bhqd', p.astype(vh.dtype), vh)

    out = lax.map(block, (jnp.arange(nq), qb, cb))
    return out.transpose(1, 0, 3, 2, 4).reshape(B, S, H, Dh)

def moba_attention(q, k, v, rel_bias):
    B, S, H, Dh = q.shape
    scale = Dh ** -0.5
    s_pad = -(-S // MOBA_BLOCK) * MOBA_BLOCK
    pad = ((0, 0), (0, s_pad - S), (0, 0), (0, 0))
    q, k, v = jnp.pad(q, pad), jnp.pad(k, pad), jnp.pad(v, pad)
    nb = s_pad // MOBA_BLOCK
    k_sel_n = min(MOBA_TOPK, nb)
    kb = k.reshape(B, nb, MOBA_BLOCK, H, Dh).transpose(0, 3, 1, 2, 4)
    vb = v.reshape(B, nb, MOBA_BLOCK, H, Dh).transpose(0, 3, 1, 2, 4)
    kmean = jnp.mean(kb.astype(jnp.float32), axis=3)
    nq = s_pad // MOBA_Q_CHUNK
    qc = q.reshape(B, nq, MOBA_Q_CHUNK, H, Dh).transpose(1, 0, 2, 3, 4)
    bi = jnp.arange(B)[:, None, None, None]
    hi = jnp.arange(H)[None, None, :, None]
    hi5 = jnp.arange(H)[None, None, :, None, None]
    blk_pos = jnp.arange(MOBA_BLOCK)

    def chunk(args):
        i, qi = args
        qpos = i * MOBA_Q_CHUNK + jnp.arange(MOBA_Q_CHUNK)
        own = (i * MOBA_Q_CHUNK) // MOBA_BLOCK
        gate = jnp.einsum('bqhd,bhnd->bqhn', qi.astype(jnp.float32), kmean)
        gate = jnp.where(jnp.arange(nb) < own, gate, -jnp.inf)
        _, idx = lax.top_k(gate, k_sel_n)
        valid = jnp.arange(k_sel_n) < own
        ksel = kb[bi, hi, idx]
        vsel = vb[bi, hi, idx]
        s_sel = jnp.einsum('bqhd,bqhjpd->bqhjp', qi, ksel).astype(jnp.float32) * scale
        kpos_sel = idx[..., None] * MOBA_BLOCK + blk_pos
        dist_sel = qpos[None, :, None, None, None] - kpos_sel
        s_sel = s_sel + rel_bias[t5_bucket(dist_sel), hi5].astype(jnp.float32)
        s_sel = jnp.where(valid[None, None, None, :, None], s_sel, -jnp.inf)
        k_own = lax.dynamic_index_in_dim(kb, own, axis=2, keepdims=False)
        v_own = lax.dynamic_index_in_dim(vb, own, axis=2, keepdims=False)
        s_own = jnp.einsum('bqhd,bhpd->bqhp', qi, k_own).astype(jnp.float32) * scale
        dist_own = qpos[:, None] - (own * MOBA_BLOCK + blk_pos)[None, :]
        bias_own = rel_bias[t5_bucket(dist_own)].transpose(0, 2, 1)
        s_own = s_own + bias_own[None].astype(jnp.float32)
        s_own = jnp.where((dist_own >= 0)[None, :, None, :], s_own, -jnp.inf)
        logits = jnp.concatenate(
            [s_sel.reshape(B, MOBA_Q_CHUNK, H, k_sel_n * MOBA_BLOCK), s_own], axis=-1)
        p = jax.nn.softmax(logits, axis=-1).astype(vb.dtype)
        p_sel = p[..., :k_sel_n * MOBA_BLOCK].reshape(B, MOBA_Q_CHUNK, H, k_sel_n, MOBA_BLOCK)
        p_own = p[..., k_sel_n * MOBA_BLOCK:]
        return (jnp.einsum('bqhjp,bqhjpd->bqhd', p_sel, vsel)
                + jnp.einsum('bqhp,bhpd->bqhd', p_own, v_own))

    out = lax.map(chunk, (jnp.arange(nq), qc))
    return out.transpose(1, 0, 2, 3, 4).reshape(B, s_pad, H, Dh)[:, :S]

def clamped_swiglu(hdn):
    x_glu = jnp.minimum(hdn[..., :D_EXPERT], SWIGLU_LIMIT)
    x_lin = jnp.clip(hdn[..., D_EXPERT:], -SWIGLU_LIMIT, SWIGLU_LIMIT)
    return x_glu * jax.nn.sigmoid(SWIGLU_ALPHA * x_glu) * (x_lin + 1)

def moe_ffn(h, w_router, b_router, w_gate_up, b_gate_up, w_down, b_down):
    B, S, D = h.shape
    T = B * S
    xt = h.reshape(T, D)
    logits = (xt @ w_router).astype(jnp.float32) + b_router.astype(jnp.float32)
    top_v, top_i = lax.top_k(logits, TOP_K)
    gates = jax.nn.softmax(top_v, axis=-1)
    A = T * TOP_K
    e_flat = top_i.reshape(A)
    tok_flat = jnp.arange(A) // TOP_K
    g_flat = gates.reshape(A)
    order = jnp.argsort(e_flat)
    e_sorted, tok_sorted, g_sorted = e_flat[order], tok_flat[order], g_flat[order]
    counts = jnp.bincount(e_flat, length=N_EXPERTS)
    padded = ((counts + EXPERT_ROW_BLOCK - 1) // EXPERT_ROW_BLOCK) * EXPERT_ROW_BLOCK
    starts = jnp.cumsum(counts) - counts
    pends = jnp.cumsum(padded)
    pstarts = pends - padded
    dest = pstarts[e_sorted] + jnp.arange(A) - starts[e_sorted]
    n_rows = A + N_EXPERTS * EXPERT_ROW_BLOCK
    n_blk = n_rows // EXPERT_ROW_BLOCK
    rows = jnp.zeros((n_rows, D), xt.dtype).at[dest].set(xt[tok_sorted])
    block_e = jnp.minimum(
        jnp.searchsorted(pends, jnp.arange(n_blk) * EXPERT_ROW_BLOCK, side='right'), N_EXPERTS - 1)

    def expert_block(args):
        xb, e = args
        hdn = xb @ w_gate_up[e] + b_gate_up[e]
        return clamped_swiglu(hdn) @ w_down[e] + b_down[e]

    y = lax.map(expert_block, (rows.reshape(n_blk, EXPERT_ROW_BLOCK, D), block_e)).reshape(n_rows, D)
    out = jnp.zeros((T, D), y.dtype).at[tok_sorted].add(y[dest] * g_sorted[:, None].astype(y.dtype))
    return out.reshape(B, S, D)

def first_inputs(seed: int = 0) -> dict:
    key = jax.random.key(seed)
    ks = jax.random.split(key, 20)
    nrm = jax.random.normal
    f32 = jnp.float32
    return {
        "x": nrm(ks[0], (BATCH, SEQ, D_MODEL), f32),
        "c": nrm(ks[1], (BATCH, D_MODEL), f32),
        "w_ada": nrm(ks[2], (DEPTH, D_MODEL, 6 * D_MODEL), f32) * (0.5 * D_MODEL ** -0.5),
        "b_ada": nrm(ks[3], (DEPTH, 6 * D_MODEL), f32) * 0.01,
        "g_pre_mix": 1.0 + 0.05 * nrm(ks[4], (DEPTH, D_MODEL), f32),
        "g_post_mix": 1.0 + 0.05 * nrm(ks[5], (DEPTH, D_MODEL), f32),
        "w_in": nrm(ks[6], (DEPTH, D_MODEL, IN_WIDTH), f32) * D_MODEL ** -0.5,
        "b_forget": nrm(ks[7], (DEPTH, N_HEADS_FOX), f32) * 0.1,
        "rel_bias": nrm(ks[8], (NUM_BUCKETS, N_HEADS_MOBA), f32) * 0.5,
        "w_out": nrm(ks[9], (DEPTH, MIX_WIDTH, D_MODEL), f32) * MIX_WIDTH ** -0.5,
        "g_pre_ffn": 1.0 + 0.05 * nrm(ks[10], (DEPTH, D_MODEL), f32),
        "g_post_ffn": 1.0 + 0.05 * nrm(ks[11], (DEPTH, D_MODEL), f32),
        "w_router": nrm(ks[12], (DEPTH, D_MODEL, N_EXPERTS), f32) * D_MODEL ** -0.5,
        "b_router": nrm(ks[13], (DEPTH, N_EXPERTS), f32) * 0.01,
        "w_gate_up": nrm(ks[14], (DEPTH, N_EXPERTS, D_MODEL, 2 * D_EXPERT), f32) * D_MODEL ** -0.5,
        "b_gate_up": nrm(ks[15], (DEPTH, N_EXPERTS, 2 * D_EXPERT), f32) * 0.01,
        "w_down": nrm(ks[16], (DEPTH, N_EXPERTS, D_EXPERT, D_MODEL), f32) * D_EXPERT ** -0.5,
        "b_down": nrm(ks[17], (DEPTH, N_EXPERTS, D_MODEL), f32) * 0.01,
    }

def first_block(x, c, w_ada, b_ada, g_pre_mix, g_post_mix, w_in, b_forget, rel_bias, w_out,
              g_pre_ffn, g_post_ffn, w_router, b_router, w_gate_up, b_gate_up, w_down, b_down):
    B, S, D = x.shape
    cond = jax.nn.silu(c)
    for l in range(DEPTH):
        mod = cond @ w_ada[l] + b_ada[l]
        sh_m, sc_m, gt_m, sh_f, sc_f, gt_f = jnp.split(mod, 6, axis=-1)
        h = rms_norm(x, g_pre_mix[l]) * (1 + sc_m[:, None, :]) + sh_m[:, None, :]
        proj = h @ w_in[l]
        o = np.cumsum([FOX_WIDTH] * 3 + [MOBA_WIDTH] * 3)
        q_a, k_a, v_a = proj[..., :o[0]], proj[..., o[0]:o[1]], proj[..., o[1]:o[2]]
        q_b, k_b, v_b = proj[..., o[2]:o[3]], proj[..., o[3]:o[4]], proj[..., o[4]:o[5]]
        f_logit = proj[..., o[5]:]
        log_f = jax.nn.log_sigmoid(f_logit.astype(jnp.float32) + b_forget[l].astype(jnp.float32))
        hs_a = (B, S, N_HEADS_FOX, HEAD_DIM)
        hs_b = (B, S, N_HEADS_MOBA, HEAD_DIM)
        y_a = fox_attention(q_a.reshape(hs_a), k_a.reshape(hs_a), v_a.reshape(hs_a), log_f)
        y_b = moba_attention(q_b.reshape(hs_b), k_b.reshape(hs_b), v_b.reshape(hs_b), rel_bias)
        mix = jnp.concatenate([y_a.reshape(B, S, FOX_WIDTH), y_b.reshape(B, S, MOBA_WIDTH)], axis=-1)
        x = x + gt_m[:, None, :] * rms_norm(mix @ w_out[l], g_post_mix[l])
        h = rms_norm(x, g_pre_ffn[l]) * (1 + sc_f[:, None, :]) + sh_f[:, None, :]
        y = moe_ffn(h, w_router[l], b_router[l], w_gate_up[l], b_gate_up[l], w_down[l], b_down[l])
        x = x + gt_f[:, None, :] * rms_norm(y, g_post_ffn[l])
    return x


DEPTH_2 = 2

GRID_W = 64
A_HEADS = 8
A_KV_HEADS = 2
A_GROUPS = A_HEADS // A_KV_HEADS
ROPE_THETA = 10000.0
POOL_WINDOWS = (2, 4, 8, 16)
POOL_GROUP = 128
POOL_WIDTH = POOL_GROUP * len(POOL_WINDOWS)
C_HEADS = 8
NA_ROWS = 8
NA_COLS = 16
A_Q = A_HEADS * HEAD_DIM
A_KV = A_KV_HEADS * HEAD_DIM
C_W = C_HEADS * HEAD_DIM
N_BRANCH = 3
BRANCH_WIDTH = 512
IN_WIDTHS = (A_Q, A_KV, A_KV, POOL_WIDTH, C_W, C_W, C_W, N_BRANCH * D_MODEL)
D_IN = sum(IN_WIDTHS)
D_FF = 2816
CONV_W = 3
EPS = 1e-6


def rmsnorm(x, g):
    xf = x.astype(jnp.float32)
    y = xf * lax.rsqrt(jnp.mean(xf * xf, axis=-1, keepdims=True) + EPS)
    return (y * g.astype(jnp.float32)).astype(x.dtype)

def rope_axis(x, pos):
    dim = x.shape[-1]
    half = dim // 2
    freqs = ROPE_THETA ** (-jnp.arange(0, dim, 2, dtype=jnp.float32) / dim)
    ang = pos.astype(jnp.float32)[:, None] * freqs[None, :]
    cos = jnp.cos(ang)[:, None, :]
    sin = jnp.sin(ang)[:, None, :]
    xf = x.astype(jnp.float32)
    x1, x2 = xf[..., :half], xf[..., half:]
    out = jnp.concatenate([x1 * cos - x2 * sin, x1 * sin + x2 * cos], axis=-1)
    return out.astype(x.dtype)

def rope_2d(x, row, col):
    half = x.shape[-1] // 2
    return jnp.concatenate([rope_axis(x[..., :half], row), rope_axis(x[..., half:], col)], axis=-1)

def global_axial_attention(q, k, v, gq, gk):
    B, S = q.shape[0], q.shape[1]
    t = jnp.arange(S)
    row, col = t // GRID_W, t % GRID_W
    q = rmsnorm(q.reshape(B, S, A_HEADS, HEAD_DIM), gq)
    k = rmsnorm(k.reshape(B, S, A_KV_HEADS, HEAD_DIM), gk)
    v = v.reshape(B, S, A_KV_HEADS, HEAD_DIM)
    q = rope_2d(q, row, col) * (HEAD_DIM ** -0.5)
    k = rope_2d(k, row, col)
    nb = S // Q_BLOCK
    qb = q.reshape(B, nb, Q_BLOCK, A_KV_HEADS, A_GROUPS, HEAD_DIM).transpose(1, 0, 2, 3, 4, 5)

    def block(qi):
        s = jnp.einsum('bqkgd,bskd->bkgqs', qi, k).astype(jnp.float32)
        p = jax.nn.softmax(s, axis=-1)
        return jnp.einsum('bkgqs,bskd->bqkgd', p.astype(v.dtype), v)

    o = lax.map(block, qb)
    return o.transpose(1, 0, 2, 3, 4, 5).reshape(B, S, A_Q)

def pool_mixer(u, w_pool, pool_scale):
    B, S = u.shape[0], u.shape[1]
    uf = u.astype(jnp.float32)
    cs = jnp.concatenate([jnp.zeros((B, 1, POOL_WIDTH), jnp.float32), jnp.cumsum(uf, axis=1)], axis=1)
    t = jnp.arange(S)
    outs = []
    for g, w in enumerate(POOL_WINDOWS):
        sl = slice(g * POOL_GROUP, (g + 1) * POOL_GROUP)
        lo = jnp.clip(t - w // 2, 0, S)
        hi = jnp.clip(t + w - w // 2, 0, S)
        csg = cs[..., sl]
        mean = (csg[:, hi] - csg[:, lo]) / (hi - lo).astype(jnp.float32)[None, :, None]
        diff = (mean - uf[..., sl]).astype(u.dtype)
        outs.append(jnp.einsum('bsc,cd->bsd', diff, w_pool[g]))
    return jnp.concatenate(outs, axis=-1) * pool_scale

def neighbourhood_attention(q, k, v, rpb):
    B, S = q.shape[0], q.shape[1]
    rows = S // GRID_W
    win_r = min(NA_ROWS, rows)
    qg = q.reshape(B, rows, GRID_W, C_HEADS, HEAD_DIM) * (HEAD_DIM ** -0.5)
    kg = k.reshape(B, rows, GRID_W, C_HEADS, HEAD_DIM)
    vg = v.reshape(B, rows, GRID_W, C_HEADS, HEAD_DIM)
    col = jnp.arange(GRID_W)
    col_start = jnp.clip(col - NA_COLS // 2, 0, GRID_W - NA_COLS)
    col_idx = col_start[:, None] + jnp.arange(NA_COLS)[None, :]
    dc = col_idx - col[:, None] + (NA_COLS - 1)

    def row_block(args):
        r, q_row = args
        rs = jnp.clip(r - win_r // 2, 0, rows - win_r)
        k_rows = lax.dynamic_slice_in_dim(kg, rs, win_r, axis=1)
        v_rows = lax.dynamic_slice_in_dim(vg, rs, win_r, axis=1)
        k_nb = k_rows[:, :, col_idx]
        v_nb = v_rows[:, :, col_idx]
        dr = rs + jnp.arange(win_r) - r + (NA_ROWS - 1)
        bias = rpb[:, dr[None, :, None], dc[:, None, :]]
        s = jnp.einsum('bqhd,brqjhd->bhqrj', q_row, k_nb).astype(jnp.float32)
        s = s + bias.astype(jnp.float32)[None]
        p = jax.nn.softmax(s.reshape(B, C_HEADS, GRID_W, win_r * NA_COLS), axis=-1)
        p = p.reshape(B, C_HEADS, GRID_W, win_r, NA_COLS).astype(v.dtype)
        return jnp.einsum('bhqrj,brqjhd->bqhd', p, v_nb)

    o = lax.map(row_block, (jnp.arange(rows), qg.transpose(1, 0, 2, 3, 4)))
    return o.transpose(1, 0, 2, 3, 4).reshape(B, S, C_W)

def conv_gated_mlp(h, w_up, conv_w, conv_b, w_down):
    up = jnp.einsum('bsd,df->bsf', h, w_up)
    pad = jnp.pad(up, ((0, 0), (1, 1), (0, 0)))
    up = pad[:, :-2] * conv_w[0] + pad[:, 1:-1] * conv_w[1] + pad[:, 2:] * conv_w[2] + conv_b
    val, gate = up[..., :D_FF], up[..., D_FF:]
    return jnp.einsum('bsf,fd->bsd', jax.nn.gelu(gate, approximate=True) * val, w_down)

def second_inputs(seed: int = 0) -> dict:
    key = jax.random.key(seed)
    ks = jax.random.split(key, 20)
    n = lambda k, shape, s: jax.random.normal(k, shape, jnp.float32) * s
    L, D = DEPTH_2, D_MODEL
    return {
        "x": n(ks[0], (BATCH, SEQ, D), 1.0),
        "norm_mix_pre": 1.0 + n(ks[1], (L, D), 0.1),
        "norm_mix_post": 1.0 + n(ks[2], (L, D), 0.1),
        "norm_ffn_pre": 1.0 + n(ks[3], (L, D), 0.1),
        "norm_ffn_post": 1.0 + n(ks[4], (L, D), 0.1),
        "w_in": n(ks[5], (L, D, D_IN), D ** -0.5),
        "b_gate": n(ks[6], (L, N_BRANCH * D), 0.1),
        "qk_norm_q": 1.0 + n(ks[7], (L, HEAD_DIM), 0.1),
        "qk_norm_k": 1.0 + n(ks[8], (L, HEAD_DIM), 0.1),
        "w_pool": n(ks[9], (L, len(POOL_WINDOWS), POOL_GROUP, POOL_GROUP), POOL_GROUP ** -0.5),
        "pool_scale": 1.0 + n(ks[10], (L, POOL_WIDTH), 0.1),
        "rpb": n(ks[11], (L, C_HEADS, 2 * NA_ROWS - 1, 2 * NA_COLS - 1), 0.5),
        "w_branch": n(ks[12], (L, N_BRANCH, BRANCH_WIDTH, D), BRANCH_WIDTH ** -0.5),
        "w_out": n(ks[13], (L, D, D), D ** -0.5),
        "w_up": n(ks[14], (L, D, 2 * D_FF), D ** -0.5),
        "conv_w": n(ks[15], (L, CONV_W, 2 * D_FF), CONV_W ** -0.5),
        "conv_b": n(ks[16], (L, 2 * D_FF), 0.01),
        "w_down": n(ks[17], (L, D_FF, D), D_FF ** -0.5),
    }

def second_block(x, norm_mix_pre, norm_mix_post, norm_ffn_pre, norm_ffn_post, w_in, b_gate,
              qk_norm_q, qk_norm_k, w_pool, pool_scale, rpb, w_branch, w_out,
              w_up, conv_w, conv_b, w_down):
    B, S = x.shape[0], x.shape[1]
    splits = [int(s) for s in np.cumsum(IN_WIDTHS)[:-1]]
    for l in range(DEPTH_2):
        h = rmsnorm(x, norm_mix_pre[l])
        proj = jnp.einsum('bsd,de->bse', h, w_in[l])
        qa, ka, va, pu, qc, kc, vc, gl = jnp.split(proj, splits, axis=-1)
        ya = global_axial_attention(qa, ka, va, qk_norm_q[l], qk_norm_k[l])
        yb = pool_mixer(pu, w_pool[l], pool_scale[l])
        yc = neighbourhood_attention(qc, kc, vc, rpb[l])
        ys = jnp.stack([ya, yb, yc], axis=2)
        z = jnp.einsum('bsnc,ncd->bsnd', ys, w_branch[l])
        gates = jax.nn.sigmoid(gl + b_gate[l]).reshape(B, S, N_BRANCH, D_MODEL)
        merged = jnp.sum(gates * z, axis=2)
        mix = jnp.einsum('bsd,de->bse', merged, w_out[l])
        x = x + rmsnorm(mix, norm_mix_post[l])
        h = rmsnorm(x, norm_ffn_pre[l])
        f = conv_gated_mlp(h, w_up[l], conv_w[l], conv_b[l], w_down[l])
        x = x + rmsnorm(f, norm_ffn_post[l])
    return x


def setup_inputs(seed=0):
    out = dict(first_inputs(seed))
    for name, value in second_inputs(seed + 1).items():
        if name != "x":
            out[name + "_2"] = value
    return out


def reference(
    x, c, w_ada, b_ada, g_pre_mix, g_post_mix, w_in, b_forget, rel_bias, w_out, g_pre_ffn,
    g_post_ffn, w_router, b_router, w_gate_up, b_gate_up, w_down, b_down, norm_mix_pre_2,
    norm_mix_post_2, norm_ffn_pre_2, norm_ffn_post_2, w_in_2, b_gate_2, qk_norm_q_2,
    qk_norm_k_2, w_pool_2, pool_scale_2, rpb_2, w_branch_2, w_out_2, w_up_2, conv_w_2, conv_b_2,
    w_down_2,
):
    x = first_block(
        x, c, w_ada, b_ada, g_pre_mix, g_post_mix, w_in, b_forget, rel_bias, w_out, g_pre_ffn,
        g_post_ffn, w_router, b_router, w_gate_up, b_gate_up, w_down, b_down,
    )
    return second_block(
        x, norm_mix_pre_2, norm_mix_post_2, norm_ffn_pre_2, norm_ffn_post_2, w_in_2, b_gate_2,
        qk_norm_q_2, qk_norm_k_2, w_pool_2, pool_scale_2, rpb_2, w_branch_2, w_out_2, w_up_2,
        conv_w_2, conv_b_2, w_down_2,
    )


_drawn_inputs = setup_inputs


def setup_inputs(seed=0):
    import zlib

    import numpy as np

    out = dict(_drawn_inputs(seed))
    spreads = {}
    factors = {'g_post_ffn': 2.857,
     'b_gate_up': 8.0,
     'b_down': 8.0,
     'qk_norm_q_2': 5.612,
     'qk_norm_k_2': 5.384,
     'conv_b_2': 5.023}
    for name, (base, spread) in spreads.items():
        noise = np.random.default_rng([zlib.crc32(name.encode()), seed]).standard_normal(out[name].shape)
        drawn = base * np.exp(spread * noise) if base else spread * noise
        out[name] = jnp.asarray(drawn.astype(out[name].dtype))
    for name, factor in factors.items():
        out[name] = (out[name] * factor).astype(out[name].dtype)
    return out
```

```python
import math

import concourse.bass as bass
import numpy as np
from concourse import mybir
from contextlib import ExitStack

F32 = mybir.dt.float32
I32 = mybir.dt.int32
U32 = mybir.dt.uint32
ALU = mybir.AluOpType
ACT = mybir.ActivationFunctionType
AX_X = mybir.AxisListType.X

P = 128
T = 256
TT = T // P
D = 1024
KC = D // P
UNIT = 2048
HEADS, DH = 8, 64
PAIRS = HEADS // 2
MIX = HEADS * DH
EPS = 1e-6
MASKED = -1e30
LEAST = -3e38
QK_SCALE = DH ** -0.5

RING = 6
MOE_UNITS = 12
EXPERTS, TOPK = 32, 4
CAP = 64
BLOCKS = EXPERTS + T * TOPK // (CAP + 1)
SWIGLU_LIMIT, SWIGLU_ALPHA = 7.0, 1.702
BUCKETS, MAX_DISTANCE = 32, 128
NOT_CHOSEN = 1000.0

LAYERS = 2
A_KV = 2
GRID_W, GRID_H = 64, T // 64
NA_ROWS, NA_COLS = 8, 16
RPB_ROW = 2 * NA_COLS - 1
RPB_HEAD = (2 * NA_ROWS - 1) * RPB_ROW
WINDOWS = (2, 4, 8, 16)
D_FF = 2816
FT = D_FF // P
D_IN2 = 5888
UPAIRS = D_FF // 256

SMALL_IN = 16 * 12
PARAMS_IN = 12
DVE_LAYER = 36


def shape_tables():
    parts = {}
    parts["ident"] = np.eye(P)
    parts["ones"] = np.ones((P, P))
    q, k = np.arange(T)[:, None], np.arange(T)[None, :]
    causal = np.where(k <= q, 0.0, MASKED)
    parts["causal"] = np.concatenate([causal[:P], causal[P:]], 1)
    col = np.arange(P) % GRID_W
    first = np.clip(col - NA_COLS // 2, 0, GRID_W - NA_COLS)
    key = np.arange(GRID_W)[None, :]
    inside = (key >= first[:, None]) & (key < first[:, None] + NA_COLS)
    parts["window"] = np.where(inside, 0.0, MASKED)
    t = np.arange(T)
    bands = []
    for st in range(TT):
        for w in WINDOWS:
            lo, hi = np.clip(t - w // 2, 0, T), np.clip(t + w - w // 2, 0, T)
            s = (st * P + np.arange(P))[:, None]
            mean = np.where((s >= lo) & (s < hi), np.float32(1.0) / (hi - lo).astype(np.float32), 0.0)
            bands.append(mean - (s == t))
    parts["bands"] = np.concatenate(bands, 1)
    freqs = np.float32(10000.0) ** (-np.arange(0, 32, 2, dtype=np.float32) / np.float32(32))
    cos, sin = [], []
    for st in range(TT):
        tok = st * P + np.arange(P)
        for pos in (tok // GRID_W, tok % GRID_W):
            ang = pos.astype(np.float32)[:, None] * freqs[None, :]
            cos += [np.cos(ang), np.cos(ang)]
            sin += [-np.sin(ang), np.sin(ang)]
    parts["cos"], parts["sin"] = np.concatenate(cos, 1), np.concatenate(sin, 1)
    parts["before"] = (np.arange(P)[:, None] < np.arange(P)[None, :])
    parts["upto"] = (np.arange(P)[:, None] <= np.arange(EXPERTS)[None, :])
    parts["slots"] = np.tile(np.arange(CAP), (P, 2))
    parts["blocks"] = np.tile(np.arange(BLOCKS + 1), (P, 1))
    parts["experts"] = np.tile(np.arange(EXPERTS), (P, 1))
    d = T - 1 - np.arange(2 * T)
    exact = BUCKETS // 2
    far = np.maximum(d, 1).astype(np.float32)
    large = exact + (np.log(far / np.float32(exact)) / np.float32(math.log(MAX_DISTANCE / exact))
                     * np.float32(BUCKETS - exact)).astype(np.int32)
    bucket = np.where(d < exact, d, np.minimum(large, BUCKETS - 1))
    onehot = np.zeros((P, 2 * T))
    onehot[:BUCKETS] = (bucket[None, :] == np.arange(BUCKETS)[:, None]) & (d >= 0)
    onehot[BUCKETS] = np.where(d >= 0, 0.0, MASKED)
    onehot[64:76, :12 * 32] = np.arange(12)[:, None] == np.repeat(np.arange(12), 32)[None, :]
    onehot[96:100, :4 * CAP] = np.arange(4)[:, None] == np.repeat(np.arange(4), CAP)[None, :]
    parts["picks"] = onehot
    at, offset = {}, 0
    for name, a in parts.items():
        at[name] = (offset, a.shape[1])
        offset += a.shape[1]
    table = np.concatenate([np.asarray(a, np.float32) for a in parts.values()], 1)
    fox = np.zeros((40, HEADS, T), np.float32)
    for h in range(HEADS):
        fox[h, h], fox[32 + h, h] = 1.0, -1.0
    return np.ascontiguousarray(table), at, fox.reshape(40, HEADS * T)


class Plan:

    def __init__(self):
        self.tiles, self.units, self.jobs, self.uses, self.at = 0, 0, {}, [0] * 8, 0

    def bank(self, name):
        b = self.at % 8
        self.at += 1
        self.jobs[name] = [b, self.uses[b], 0]
        self.uses[b] += 1

    def tile(self, name):
        self.bank(name)
        self.tiles += 1
        self.jobs[name][2] = self.tiles

    def unit(self, *names):
        self.units += 1
        for n in names:
            self.jobs[n][2] = self.units

    def attention(self, s, after_scores, after=None):
        for tt in range(TT):
            for h in range(HEADS):
                self.tile(f"{s}score{tt}{h}")
        after_scores()
        for h in range(HEADS):
            self.tile(f"{s}turn{h}")
        for p in range(PAIRS):
            self.tile(f"{s}out{p}")


IN1 = [f"{n}{i}" for n in ("qa", "ka", "va", "qb", "kb", "vb") for i in range(2)]
IN2 = ["qa0", "qa1", "kv", "pu0", "pu1", "qc0", "qc1", "kc0", "kc1", "vc0", "vc1"] + [f"gl{i}" for i in range(12)]


def plan_first():
    p = Plan()
    p.tile("cond")
    p.tile("table")

    def ada(r):
        p.bank(f"ada{r}")
        for k in range(KC):
            p.unit(f"ada{r}")
        for j in range(4):
            p.tile(f"mod{4 * r + j}")

    def project(names):
        for n in names:
            p.bank(n)
            p.unit(n)

    ada(0)
    for j in range(4):
        p.tile(f"h{j}")
    p.tile("forget")
    project(IN1[:6])
    p.attention("a", lambda: project(IN1[6:]))
    p.attention("b", lambda: (ada(1), ada(2)))
    for j in range(4):
        p.bank(f"mix{j}")
    for u in range(4):
        p.unit(*[f"mix{j}" for j in range(4)])
    for j in range(4):
        p.tile(f"g{j}")
    for n in ("logits", "places", "counts", "ends", "turned", "list", "spread0", "spread1"):
        p.tile(n)
    return p


def plan_layer():
    p = Plan()

    def project(names):
        for n in names:
            p.bank(n)
            p.unit(n)

    p.tile("params")
    for j in range(4):
        p.tile(f"h{j}")
    project(IN2[0:5])
    for g in range(4):
        p.tile(f"diff{g}")
    for g in range(4):
        p.tile(f"pool{g}")
    for n in ("qturn0", "qturn1", "kturn"):
        p.tile(n)
    p.attention("a", lambda: project(IN2[5:11]))
    p.attention("c", lambda: project(IN2[11:]))
    for u in range(6):
        p.bank(f"branch{u}0")
        p.bank(f"branch{u}1")
        p.unit(f"branch{u}0", f"branch{u}1")
    for j in range(4):
        p.bank(f"mix{j}")
    for u in range(4):
        p.unit(*[f"mix{j}" for j in range(4)])
    for j in range(4):
        p.tile(f"g{j}")
    for c in range(UPAIRS):
        for n in ("val", "gate"):
            p.bank(f"{n}{c}")
            p.unit(f"{n}{c}")
    for j in range(4):
        p.bank(f"down{j}")
    for u in range(FT // 2):
        p.unit(*[f"down{j}" for j in range(4)])
    return p


class Chain:

    def __init__(self, engine, semaphore):
        self.engine, self.semaphore, self.base, self.n = engine, semaphore, 0, 0

    def __call__(self, instruction):
        self.n += 1
        instruction.then_inc(self.semaphore, 1)
        self.engine.wait_ge(self.semaphore, self.base + self.n)

    def loop(self, i, per_turn):
        self.before, self.per_turn = (self.base + self.n if i is not None else 0), per_turn
        self.base, self.n = self.before + i * per_turn, 0

    def loop_end(self, turns):
        assert self.n == self.per_turn, (self.n, self.per_turn)
        self.base, self.n = self.before + turns * self.per_turn, 0


def build(nc, x_in, c_in, w_ada, b_ada, g_pre_mix, g_post_mix, w_in, b_forget, rel_bias, w_out, g_pre_ffn,
          g_post_ffn, w_router, b_router, w_gate_up, b_gate_up, w_down, b_down, norm_mix_pre, norm_mix_post,
          norm_ffn_pre, norm_ffn_post, w_in2, b_gate2, qk_q, qk_k, w_pool, pool_scale, rpb, w_branch, w_out2,
          w_up, conv_w, conv_b, w_down2, shape_table, fox_table, out, table_at):
    first, layer = plan_first(), plan_layer()
    JF, JL = first.jobs, layer.jobs
    N_UNITS, N_TILES = layer.units, layer.tiles

    with ExitStack() as ctx:
        def sb(name, width, dt=F32, parts=P):
            return ctx.enter_context(nc.sbuf_tensor(name, [parts, width], dt))

        def sem(name):
            return ctx.enter_context(nc.semaphore(name))

        ring = sb("ring", MOE_UNITS * UNIT)
        x = sb("x", TT * D)[:, :].rearrange("p (t d) -> p t d", t=TT)
        htok_t = sb("htok", TT * D)
        htok = htok_t[:, :].rearrange("p (t d) -> p t d", t=TT)
        hT = sb("hT", KC * T)[:, :].rearrange("p (k t) -> p k t", k=KC)
        probs_t = sb("probs", TT * HEADS * T)
        probs = probs_t[:, :].rearrange("p (t h k) -> p t h k", t=TT, h=HEADS)
        mixT_t = sb("mixT", 12 * T)
        mixT = mixT_t[:, :].rearrange("p (c t) -> p c t", c=12)
        qkv = sb("qkv", 6 * 1024)
        consts = sb("consts", shape_table.shape[1])
        side = sb("side", 2048)
        small = sb("small", 2040)
        lists = sb("lists", 64, I32, parts=1)
        picked = sb("picked", TT * 8, U32)

        def const(name, parts=slice(0, P)):
            a, n = table_at[name]
            return consts[parts, a:a + n]

        def scratch(at, n):
            return ring[:, RING * UNIT + at:RING * UNIT + at + n]

        used = [0]

        def little(n):
            a = used[0]
            used[0] += n
            return small[:, a:a + n]

        def by_tile(a):
            return a.rearrange("p (t e) -> p t e", t=TT)

        ident, ones = const("ident"), const("ones")
        causal, bands = by_tile(const("causal")), const("bands").rearrange("p (s g t) -> p s g t", s=TT, g=4)
        eps, meansq, root, rstd, halves = little(1), little(TT), little(TT), little(TT), little(4)
        top, negtop, total, scale = (little(TT * HEADS) for _ in range(4))
        zeros = little(T)

        def q4(a):
            return qkv[:, a:a + 1024].rearrange("p (c t) -> p c t", c=4)

        def v2(a, n=512):
            return qkv[:, a:a + TT * n].rearrange("p (t n) -> p t n", t=TT)

        proj1 = dict(qa=q4(0), ka=q4(1024), va=v2(2048), qb=q4(3072), kb=q4(4096), vb=v2(5120))
        gain_m, shift_m = probs_t[:, 0:1024], probs_t[:, 1024:2048]
        modrows = [probs_t[:, 2048:2560], htok_t[:, 0:512], htok_t[:, 512:1024]]
        tables = scratch(0, 4096).rearrange("p (t h k) -> p t h k", t=TT, h=HEADS)
        turned = scratch(4096, 4096).rearrange("p (h c q) -> p h c q", h=HEADS, c=TT)
        gpre_m, gpost_m, gpre_f, gpost_f = (scratch(8192 + 1024 * i, 1024) for i in range(4))
        gate_m, gain_f, shift_f, gate_f = gpost_m, gpre_f, gpre_m, mixT_t[:, 2048:3072]
        fox_rhs = side[0:40, :].rearrange("p (h k) -> p h k", h=HEADS)
        bada, trow, crow = side[64:76, 0:512], side[96:96 + HEADS, 0:512], side[96:96 + KC, 512:512 + P]
        pick12 = const("picks", slice(64, 76))[:, 0:12 * 32].rearrange("p (c m) -> p c m", c=12)
        buckets = const("picks", slice(0, BUCKETS + 1))
        condrep = little(KC * 32).rearrange("p (k m) -> p k m", k=KC)
        wf = little(KC * HEADS).rearrange("p (k n) -> p k n", k=KC)
        wfdup = little(KC * 40).rearrange("p (k n) -> p k n", k=KC)
        bforget, rel33 = little(1), little(HEADS)
        fcum = little(T)[0:40, :]
        fz, fa, fe, fm = (probs_t[0:40, 2560 + T * i:2560 + T * i + T] for i in range(4))

        wrt = sb("wrt", KC * EXPERTS)[:, :].rearrange("p (k e) -> p k e", k=KC)
        brt, logits = little(EXPERTS), by_tile(little(TT * EXPERTS))
        best, bestf, gate4 = (by_tile(little(TT * n)) for n in (8, 8, TOPK))
        gsum = little(TT)
        gates_te, chosen, place = (by_tile(little(TT * EXPERTS)) for _ in range(3))
        nblk, ends, starts = (little(1)[0:EXPERTS, :] for _ in range(3))
        blkpos, blkgate = (by_tile(little(TT * (BLOCKS + 1))) for _ in range(2))
        assert used[0] <= 2040, used

        at = [0]

        def moe(n, memory=qkv):
            a = at[0]
            at[0] += n
            return memory[:, a:a + n]

        xgT = moe(512).rearrange("p (b j s) -> p b j s", b=4, j=2)
        actT = moe(512).rearrange("p (b j s) -> p b j s", b=4, j=2)
        xrow, yblk, glu, lin, lin1, sig, act_row = (moe(512) for _ in range(7))
        brows = moe(512)[96:100, :]
        assert at[0] <= 6144
        at[0] = 0
        sel, selg = by_tile(moe(TT * CAP, probs_t)), by_tile(moe(TT * 2 * CAP, probs_t))
        selgT, bdown = moe(T, probs_t), moe(D, probs_t)[0:EXPERTS, :]
        posT, gateT = (moe(T, probs_t)[0:EXPERTS, :] for _ in range(2))
        done_e, begun_e, onehot = (moe(BLOCKS + 1, probs_t)[0:EXPERTS, :] for _ in range(3))
        equal4, equalg = (moe(TOPK * EXPERTS, probs_t).rearrange("p (k e) -> p k e", k=TOPK) for _ in range(2))
        pick4 = const("picks", slice(96, 100))[:, 0:4 * CAP].rearrange("p (r s) -> p r s", r=4)
        slots, blocks, experts = const("slots"), const("blocks"), const("experts")

        qk = qkv[:, 0:1280].rearrange("p (t n) -> p t n", t=TT)
        qTa, kTa, va2 = q4(1280), qkv[:, 2304:2816].rearrange("p (g t) -> p g t", g=A_KV), v2(2816, P)
        pu = vc = v2(3072)
        qTc, kTc = q4(4096), q4(5120)
        params = scratch(4096, 256).rearrange("p (i n) -> p i n", i=2)
        gqk = scratch(4352, 640)
        wpool = scratch(4992, 512).rearrange("p (g d) -> p g d", g=4)
        diffT = scratch(5504, 1024).rearrange("p (c t) -> p c t", c=4)
        qksq = scratch(6528, 1280).rearrange("p (t n) -> p t n", t=TT)
        rope1 = probs_t[:, 0:1280].rearrange("p (t n) -> p t n", t=TT)
        rope2 = probs_t[:, 1280:2560].rearrange("p (t n) -> p t n", t=TT)
        kdup = probs_t[:, 2560:3072].rearrange("p (t g c d) -> p t g c d", t=TT, g=A_KV, c=2)
        gpost2 = [side[:, 0:1024], side[:, 1024:2048]]
        gates = [scratch(8192, 2048), scratch(10240, 2048), htok_t[:, :]]
        gates = [g.rearrange("p (c t) -> p c t", c=KC) for g in gates]
        merged = gates[0]
        gated = scratch(0, FT * T).rearrange("p (c t) -> p c t", c=FT)
        conv = [probs_t[:, 512 * i:512 * i + 512].rearrange("p (m t) -> p m t", m=2) for i in range(4)]
        columns = sb("columns", 220)
        qkms, qkr = sb("qkms", TT * (HEADS + A_KV))[:, :], sb("qkr", TT * (HEADS + A_KV))[:, :]

        def tap(first_column):
            return lambda f: columns[:, first_column + f:first_column + f + 1]

        c_conv0, c_conv1, c_conv2 = tap(0), tap(44), tap(128)
        c_gate, c_pre, c_ffn = columns[:, 88:112], columns[:, 112:120], columns[:, 120:128]
        c_bias, c_pool = columns[:, 172:216], columns[:, 216:220]

        distances = nc.dram_tensor("distances", (P, HEADS, 2 * T), F32, kind="Internal").ap()
        rpb_copies = nc.dram_tensor("rpb_copies", (LAYERS, GRID_W, HEADS * RPB_HEAD), F32, kind="Internal").ap()
        neighbours = nc.dram_tensor("neighbours", (LAYERS, P, TT, HEADS, T), F32, kind="Internal").ap()
        banks = [ctx.enter_context(nc.psum_tensor(f"bank{b}", [P, 512], F32)) for b in range(8)]

        consts_in, small_in, x_in_sem = sem("consts_in"), sem("small_in"), sem("x_in")
        cleared, cond_rows, cond_ready = sem("cleared"), sem("cond_rows"), sem("cond_ready")
        landed = [sem(f"landed{s}") for s in range(RING)]
        landed_moe = [sem(f"landed_moe{s}") for s in range(MOE_UNITS)]
        landed_l = [sem(f"landed_l{s}") for s in range(RING)]
        unit_done, tile_done = sem("unit_done"), sem("tile_done")
        unit_done_l, tile_done_l = sem("unit_done_l"), sem("tile_done_l")
        bank_free = [sem(f"bank_free{b}") for b in range(8)]
        bank_free_l = [sem(f"bank_free_l{b}") for b in range(8)]
        dve_own, act_own, pool_own = sem("dve_own"), sem("act_own"), sem("pool_own")
        scores_kept, negmax_ready, exp_done, prob_ready = (sem(n) for n in ("scores_kept", "negmax_ready", "exp_done", "prob_ready"))
        squares, means, roots = sem("squares"), sem("means"), sem("roots")
        h_ready, fox_ready, scan_in, log_in = sem("h_ready"), sem("fox_ready"), sem("scan_in"), sem("log_in")
        table_out, rpb_out, table_in, x_mid = sem("table_out"), sem("rpb_out"), sem("table_in"), sem("x_mid")
        gates_in, gates_exp, route_ready, list_ready = sem("gates_in"), sem("gates_exp"), sem("route_ready"), sem("list_ready")
        scratch_dead, bias_in = sem("scratch_dead"), sem("bias_in")
        moe_used = [sem(f"moe_used{s}") for s in range(MOE_UNITS)]
        sel_ready, gathered, xrow_ready, xg_turned, xg_ready = (sem(n) for n in ("sel_ready", "gathered", "xrow_ready", "xg_turned", "xg_ready"))
        selg_ready, selg_turned, selgT_ready = sem("selg_ready"), sem("selg_turned"), sem("selgT_ready")
        clamped, sig_ready, act_ready, act_turned, actT_ready = (sem(n) for n in ("clamped", "sig_ready", "act_ready", "act_turned", "actT_ready"))
        y_ready, moe_done = sem("y_ready"), sem("moe_done")
        layer_in, params_in, bias_l_in, bias_masked = sem("layer_in"), sem("params_in"), sem("bias_l_in"), sem("bias_masked")
        qk_means, rope_ready, branch_ready, gated_ready = sem("qk_means"), sem("rope_ready"), sem("branch_ready"), sem("gated_ready")
        conv_in, conv_ready, gelu_ready = sem("conv_in"), sem("conv_ready"), sem("gelu_ready")
        odd_scores, out_done, cond_in, bdown_in, neighbours_out = (sem(n) for n in ("odd_scores", "out_done", "cond_in", "bdown_in", "neighbours_out"))

        hidden_done, down_done = moe_used[KC - 1], moe_used[MOE_UNITS - 1]
        block = ctx.enter_context(nc.Block())

        per_layer = {id(s): n for s, n in (
            (negmax_ready, 4), (exp_done, 4), (prob_ready, 4), (roots, 5), (squares, 2), (means, 2), (h_ready, 4),
            (x_mid, 1), (qk_means, 1), (rope_ready, 1), (branch_ready, 1), (gated_ready, 1), (conv_in, 2 * UPAIRS),
            (conv_ready, UPAIRS - 1), (gelu_ready, UPAIRS))}

        class Seen:

            def __init__(self):
                self.base, self.n = {}, {}

            def __call__(self, s):
                self.n[id(s)] = self.n.get(id(s), 0) + 1
                return self.base.get(id(s), 0) + self.n[id(s)]

            def loop(self, i):
                self.base = {k: self.n.get(k, 0) + i * per for k, per in per_layer.items()}
                self.n = {}

            def loop_end(self):
                assert all(per_layer[k] == n for k, n in self.n.items()), self.n

        def full(name):
            job = JF[name]
            return (unit_done if name in UNIT_TILES else tile_done), job[2]

        def full_l(name, l):
            job = JL[name]
            if name in UNIT_TILES_L:
                return unit_done_l, l * N_UNITS + (job[2] + RING)
            return tile_done_l, l * N_TILES + job[2]

        def emptied(name):
            return bank_free[JF[name][0]], JF[name][1] + 1

        def emptied_l(name, l):
            b, use, _ = JL[name]
            return bank_free_l[b], l * layer.uses[b] + (use + 2)

        UNIT_TILES = {f"ada{r}" for r in range(3)} | set(IN1) | {f"mix{j}" for j in range(4)}
        UNIT_TILES_L = set(IN2) | {f"branch{u}{i}" for u in range(6) for i in range(2)}
        UNIT_TILES_L |= {f"{n}{j}" for n in ("mix", "down") for j in range(4)}
        UNIT_TILES_L |= {f"{n}{c}" for n in ("val", "gate") for c in range(UPAIRS)}

        def unit_at(slot):
            return ring[:, slot * UNIT:(slot + 1) * UNIT]

        def columns_unit(slot):
            return unit_at(slot).rearrange("p (k n) -> p k n", k=KC)

        def rows_unit(slot):
            return unit_at(slot).rearrange("p (k n) -> p k n", k=2)

        @block.sync
        def _(sp):
            sp.dma_start(x, x_in[0].rearrange("(t p) d -> p t d", p=P)).then_inc(x_in_sem, 16)
            w_in_v = w_in[0].rearrange("(k p) n -> p k n", p=P)
            w_out_v = w_out[0].rearrange("(k p) n -> p k n", p=P)
            sources = [w_ada[0, P * k:P * k + P, 0:UNIT] for k in range(KC)]
            sources += [w_in_v[:, :, 256 * u:256 * u + 256] for u in range(len(IN1))]
            sources += [w_ada[0, P * k:P * k + P, UNIT * r:UNIT * r + UNIT] for r in (1, 2) for k in range(KC)]
            sources += [w_out_v[:, 2 * u:2 * u + 2, :] for u in range(4)]
            for u, source in enumerate(sources):
                s = u % RING
                if u >= RING:
                    sp.wait_ge(unit_done, u - RING + 1)
                shape = unit_at(s) if len(source.shape) == 2 else unit_at(s).rearrange(
                    "p (k n) -> p k n", k=source.shape[1])
                sp.dma_start(shape, source).then_inc(landed[s], 16)

            def load_expert(e, wait):
                wgu = w_gate_up[0, bass.ds(e, 1)].rearrange("e (k p) n -> (e p) k n", p=P)
                wdn = w_down[0, bass.ds(e, 1)].rearrange("e (k p) n -> (e p) k n", p=P)
                for u in range(MOE_UNITS):
                    wait(u)
                    if u == 0:
                        sp.dma_start(brows, b_gate_up[0, bass.ds(e, 1)].rearrange("e (r n) -> (e r) n", r=4))\
                            .then_inc(bias_in, 16)
                    if u < KC:
                        sp.dma_start(unit_at(u), wgu[:, u, :]).then_inc(landed_moe[u], 16)
                    else:
                        v = u - KC
                        sp.dma_start(rows_unit(u), wdn[:, 2 * v:2 * v + 2, :]).then_inc(landed_moe[u], 16)

            def first_wait(u):
                if u == 0:
                    sp.wait_ge(unit_done, first.units)
                if u == RING:
                    sp.wait_ge(h_ready, 4)

            load_expert(0, first_wait)
            sp.wait_ge(*emptied("list"))
            n_blocks = sp.value_load(lists[0:1, BLOCKS + 1:BLOCKS + 2], min_val=EXPERTS, max_val=BLOCKS)
            with sp.Fori(1, n_blocks) as i:
                e = sp.value_load(lists[0:1, bass.ds(i, 1)], min_val=0, max_val=EXPERTS - 1)
                load_expert(e, lambda u: sp.wait_ge(moe_used[u], i))

            with sp.Fori(0, LAYERS) as l:
                def w(a, k):
                    return a[bass.ds(l, 1)].rearrange("l (k p) n -> (l p) k n", p=P)

                in_v, out_v = w(w_in2, KC), w(w_out2, KC)
                up_v, down_v = w(w_up, KC), w(w_down2, FT)
                branch_v = w_branch[bass.ds(l, 1)].rearrange("l b (k p) n -> (l p) b k n", p=P)
                order = [in_v[:, :, 256 * u:256 * u + 256] for u in range(len(IN2))]
                order += [branch_v[:, u // 2, :, 512 * (u % 2):512 * (u % 2) + 512] for u in range(6)]
                order += [out_v[:, 2 * u:2 * u + 2, :] for u in range(4)]
                for c in range(UPAIRS):
                    order += [up_v[:, :, D_FF * half + 256 * c:D_FF * half + 256 * c + 256] for half in range(2)]
                order += [down_v[:, 2 * u:2 * u + 2, :] for u in range(FT // 2)]
                assert len(order) == N_UNITS and N_UNITS % RING == 0
                for u, source in enumerate(order):
                    sp.wait_ge(unit_done_l, l * N_UNITS + (u + 1))
                    sp.dma_start(unit_at(u % RING).rearrange("p (k n) -> p k n", k=source.shape[1]), source)\
                        .then_inc(landed_l[u % RING], 16)
            sp.wait_ge(layer_in, LAYERS + 1)
            sp.dma_start(out[0].rearrange("(t p) d -> p t d", p=P), x).then_inc(out_done, 16)
            sp.wait_ge(out_done, 16)

        @block.tensor
        def _(pe):
            seen = Seen()
            state = dict(unit=0, l=None, emptied=[0] * 8)

            def bank_emptied(b, times):
                if times > state["emptied"][b]:
                    state["emptied"][b] = times
                    if state["l"] is None:
                        pe.wait_ge(bank_free[b], times)
                    else:
                        pe.wait_ge(bank_free_l[b], state["l"] * layer.uses[b] + (times + 1))

            def take(name):
                b, use, _ = (JF if state["l"] is None else JL)[name]
                bank_emptied(b, use)
                return banks[b]

            def read(*names):
                jobs, last = JF if state["l"] is None else JL, {}
                for n in names:
                    b, use, _ = jobs[n]
                    last[b] = max(use + 1, last.get(b, 0))
                for b, times in last.items():
                    bank_emptied(b, times)

            def tile(last):
                last.then_inc(tile_done if state["l"] is None else tile_done_l, 1)

            def next_unit():
                u = state["unit"]
                state["unit"] += 1
                s = u % RING
                if state["l"] is None:
                    pe.wait_ge(landed[s], 16 * (u // RING + 1))
                else:
                    pe.wait_ge(landed_l[s], state["l"] * (16 * N_UNITS // RING) + 16 * (u // RING + 1))
                return s

            def used(last):
                last.then_inc(unit_done if state["l"] is None else unit_done_l, 1)

            def turn_h(names, src):
                for j, n in enumerate(names):
                    b = take(n)
                    for kk in range(2):
                        for tt in range(TT):
                            c = (2 * j + kk) * P
                            last = pe.transpose(b[:, kk * T + tt * P:kk * T + tt * P + P], src[:, tt, c:c + P], ident)
                    tile(last)

            def project_T(name):
                b, s = take(name), next_unit()
                for i in range(2):
                    for k in range(KC):
                        last = pe.matmul(b[:, i * T:i * T + T], columns_unit(s)[:, k, i * P:i * P + P], hT[:, k, :],
                                         start=(k == 0), stop=(k == KC - 1))
                used(last)

            def project(name):
                b, s = take(name), next_unit()
                for tt in range(TT):
                    for k in range(KC):
                        last = pe.matmul(b[:, tt * 256:tt * 256 + 256], hT[:, k, tt * P:tt * P + P],
                                         columns_unit(s)[:, k, :], start=(k == 0), stop=(k == KC - 1))
                used(last)

            def rows_product(names, lhsT, chunks):
                bs = [take(n) for n in names]
                for u in range(chunks // 2):
                    s = next_unit()
                    for c in range(2):
                        kc = 2 * u + c
                        for j in range(4):
                            tt, half = j // 2, j % 2
                            last = pe.matmul(bs[j][:, :], lhsT[:, kc, tt * P:tt * P + P],
                                             rows_unit(s)[:, c, half * 512:half * 512 + 512],
                                             start=(kc == 0), stop=(kc == chunks - 1))
                    used(last)

            def scores(s, qT, key, extra=None):
                for tt in range(TT):
                    for h in range(HEADS):
                        b, o = take(f"{s}score{tt}{h}"), DH * (h % 2)
                        last = pe.matmul(b[:, 0:T], qT[o:o + DH, h // 2, tt * P:tt * P + P], key(h, o), start=True,
                                         stop=extra is None)
                        if extra is not None:
                            if o:
                                last.then_inc(odd_scores, 1)
                                pe.wait_ge(odd_scores, tt * PAIRS + h // 2 + 1)
                            last = extra(b, tt, h)
                        tile(last)

            def values(s, value):
                for tt in range(TT):
                    pe.wait_ge(prob_ready, seen(prob_ready))
                for h in range(HEADS):
                    b = take(f"{s}turn{h}")
                    for c in range(TT):
                        for tt in range(TT):
                            last = pe.transpose(b[:, c * T + tt * P:c * T + tt * P + P],
                                                probs[:, tt, h, c * P:c * P + P], ident)
                    tile(last)
                for p in range(PAIRS):
                    b = take(f"{s}out{p}")
                    for h in (2 * p, 2 * p + 1):
                        read(f"{s}turn{h}")
                        o = DH * (h % 2)
                        for c in range(TT):
                            last = pe.matmul(b[o:o + DH, 0:T], value(h, c), turned[:, h, c, :], start=(c == 0),
                                             stop=(c == TT - 1))
                    tile(last)

            pe.wait_ge(consts_in, 16)
            pe.wait_ge(cond_rows, 1)
            tile(pe.transpose(take("cond")[:, 0:KC], crow, const("ident", slice(96, 96 + KC))[:, 96:96 + KC]))
            pe.wait_ge(small_in, SMALL_IN)
            pe.wait_ge(cleared, 1)
            tile(pe.matmul(take("table")[0:HEADS, :], rel33[0:BUCKETS + 1, :], buckets, start=True, stop=True))

            def ada(r):
                b = take(f"ada{r}")
                for j in range(4):
                    pe.matmul(b[32 * j:32 * j + 32, :], pick12[:, 4 * r + j, :], bada, start=True, stop=False)
                for k in range(KC):
                    s = next_unit()
                    for j in range(4):
                        last = pe.matmul(b[32 * j:32 * j + 32, :], condrep[:, k, :],
                                         unit_at(s)[:, 512 * j:512 * j + 512], start=False, stop=(k == KC - 1))
                    used(last)
                read(f"ada{r}")
                for j in range(4):
                    tile(pe.matmul(take(f"mod{4 * r + j}")[:, :], ones[32 * j:32 * j + 1, :],
                                   modrows[r][32 * j:32 * j + 1, :], start=True, stop=True))

            read("cond")
            ada(0)
            for tt in range(TT):
                pe.wait_ge(h_ready, seen(h_ready))
            turn_h([f"h{j}" for j in range(4)], htok)
            read(*[f"h{j}" for j in range(4)])
            b = take("forget")
            for k in range(KC):
                last = pe.matmul(b[0:40, 0:T], wfdup[:, k, :], hT[:, k, :], start=(k == 0), stop=(k == KC - 1))
            tile(last)

            def project_set(names):
                for n in names:
                    (project if n[0] == "v" else project_T)(n)

            project_set(IN1[0:6])
            read(*IN1[0:6])
            pe.wait_ge(fox_ready, 1)

            def fox_bias(b, tt, h):
                return pe.matmul(b[:, 0:T], fcum[:, tt * P:tt * P + P], fox_rhs[:, h, :], start=False, stop=True)

            scores("a", proj1["qa"], lambda h, o: proj1["ka"][o:o + DH, h // 2, :], fox_bias)
            project_set(IN1[6:])
            values("a", lambda h, c: proj1["va"][:, c, h * DH:h * DH + DH])
            read(*IN1[6:])
            scores("b", proj1["qb"], lambda h, o: proj1["kb"][o:o + DH, h // 2, :])
            ada(1)
            ada(2)
            values("b", lambda h, c: proj1["vb"][:, c, h * DH:h * DH + DH])
            read(*[f"{s}out{p}" for s in "ab" for p in range(PAIRS)])
            rows_product([f"mix{j}" for j in range(4)], mixT, KC)
            for tt in range(TT):
                pe.wait_ge(h_ready, seen(h_ready))
            turn_h([f"g{j}" for j in range(4)], htok)
            read(*[f"g{j}" for j in range(4)])
            b = take("logits")
            for tt in range(TT):
                for k in range(KC):
                    last = pe.matmul(b[:, tt * EXPERTS:tt * EXPERTS + EXPERTS], hT[:, k, tt * P:tt * P + P],
                                     wrt[:, k, :], start=(k == 0), stop=(k == KC - 1))
            tile(last)
            pe.wait_ge(route_ready, 1)
            b = take("places")
            before = const("before")
            pe.matmul(b[:, 0:EXPERTS], before, chosen[:, 0, :], start=True, stop=True)
            pe.matmul(b[:, EXPERTS:2 * EXPERTS], ones, chosen[:, 0, :], start=True, stop=False)
            tile(pe.matmul(b[:, EXPERTS:2 * EXPERTS], before, chosen[:, 1, :], start=False, stop=True))
            b = take("counts")
            for tt in range(TT):
                last = pe.matmul(b[0:EXPERTS, 0:1], chosen[:, tt, :], ones[:, 0:1], start=(tt == 0), stop=(tt == 1))
            tile(last)
            pe.wait_ge(route_ready, 2)
            tile(pe.matmul(take("ends")[0:EXPERTS, 0:1], const("upto", slice(0, EXPERTS)), nblk, start=True, stop=True))
            pe.wait_ge(route_ready, 3)
            b = take("turned")
            for tt in range(TT):
                pe.transpose(b[0:EXPERTS, tt * P:tt * P + P], place[:, tt, :], ident)
            for tt in range(TT):
                last = pe.transpose(b[0:EXPERTS, T + tt * P:T + tt * P + P], gates_te[:, tt, :], ident)
            tile(last)
            pe.wait_ge(route_ready, 4)
            b = take("list")
            pe.matmul(b[0:1, 0:BLOCKS + 1], ones[0:EXPERTS, 0:1], done_e, start=True, stop=True)
            tile(pe.matmul(b[0:1, BLOCKS + 1:BLOCKS + 2], nblk, ones[0:EXPERTS, 0:1], start=True, stop=True))
            read("turned")
            for tt in range(TT):
                b = take(f"spread{tt}")
                pe.matmul(b[:, 0:BLOCKS + 1], posT[:, tt * P:tt * P + P], onehot, start=True, stop=True)
                tile(pe.matmul(b[:, 64:64 + BLOCKS + 1], gateT[:, tt * P:tt * P + P], onehot, start=True, stop=True))

            for b in range(8):
                pe.wait_ge(bank_free[b], first.uses[b])
            sums, hidden, rows_bank, turn_bank = banks[0:4], banks[4:6], banks[6], banks[7]
            y_bank = hidden[0]
            for j in range(4):
                pe.matmul(sums[j][:, :], zeros[:, 0:P], consts[:, 0:512], start=True, stop=False, skip_group_check=True)

            def gather():
                for tt in range(TT):
                    for j in range(2):
                        last = pe.matmul(rows_bank[CAP * j:CAP * j + CAP, :], sel[:, tt, :],
                                         htok[:, tt, 512 * j:512 * j + 512], start=(tt == 0), stop=(tt == TT - 1))
                last.then_inc(gathered, 1)

            def turn_rows():
                for b in range(4):
                    last = pe.transpose(rows_bank[:, P * b:P * b + P], xrow[:, P * b:P * b + P], ident)
                last.then_inc(xg_turned, 1)

            def scatter(signal):
                for j in range(4):
                    tt, half = j // 2, j % 2
                    p0 = CAP * half
                    last = pe.matmul(sums[j][:, :], selgT[p0:p0 + CAP, tt * P:tt * P + P], yblk[p0:p0 + CAP, :],
                                     start=False, stop=False, skip_group_check=True)
                    if signal is not None:
                        last.then_inc(signal, 1)

            pe.wait_ge(sel_ready, 1)
            gather()
            pe.wait_ge(xrow_ready, 1)
            turn_rows()
            read("list")
            n_blocks = pe.value_load(lists[0:1, BLOCKS + 1:BLOCKS + 2], min_val=EXPERTS, max_val=BLOCKS)
            with pe.Fori(0, n_blocks) as i:
                pe.wait_ge(xg_ready, i + 1)
                pe.wait_ge(y_ready, i + 1)
                pe.wait_ge(bias_in, 16 * i + 16)
                for q in range(2):
                    for j in range(2):
                        pe.matmul(hidden[q][CAP * j:CAP * j + CAP, :], pick4[:, 2 * q + j, :], brows, start=True,
                                  stop=False)
                for k in range(KC):
                    pe.wait_ge(landed_moe[k], 16 * i + 16)
                    for q in range(2):
                        for j in range(2):
                            c = q * D + j * 512
                            last = pe.matmul(hidden[q][CAP * j:CAP * j + CAP, :], xgT[:, k % 4, k // 4, :],
                                             unit_at(k)[:, c:c + 512], start=False, stop=(k == KC - 1))
                    last.then_inc(moe_used[k], 1)
                pe.wait_ge(selgT_ready, i + 1)
                scatter(None)
                pe.wait_ge(selg_ready, i + 1)
                for tt in range(TT):
                    last = pe.transpose(turn_bank[:, tt * P:tt * P + P], selg[:, tt, :], ident)
                last.then_inc(selg_turned, 1)
                pe.wait_ge(sel_ready, i + 2)
                gather()
                pe.wait_ge(act_ready, i + 1)
                pe.wait_ge(selgT_ready, i + 2)
                for b in range(4):
                    last = pe.transpose(turn_bank[:, P * b:P * b + P], act_row[:, P * b:P * b + P], ident)
                last.then_inc(act_turned, 1)
                pe.wait_ge(actT_ready, i + 1)
                for v in range(KC // 2):
                    pe.wait_ge(landed_moe[KC + v], 16 * i + 16)
                    for c in range(2):
                        f = 2 * v + c
                        for half in range(2):
                            last = pe.matmul(y_bank[CAP * half:CAP * half + CAP, :], actT[:, f % 4, f // 4, :],
                                             rows_unit(KC + v)[:, c, 512 * half:512 * half + 512], start=(f == 0),
                                             stop=(f == KC - 1))
                    last.then_inc(moe_used[KC + v], 1)
                pe.wait_ge(xrow_ready, i + 2)
                turn_rows()
            pe.wait_ge(y_ready, n_blocks + 1)
            pe.wait_ge(selgT_ready, n_blocks + 1)
            scatter(unit_done_l)
            pe.wait_ge(bdown_in, 16)
            for j in range(4):
                tt, half = j // 2, j % 2
                last = pe.matmul(sums[j][:, :], gateT[:, tt * P:tt * P + P], bdown[:, 512 * half:512 * half + 512],
                                 start=False, stop=True, skip_group_check=True)
                last.then_inc(unit_done_l if j < RING - 4 else moe_done, 1)

            with pe.Fori(0, LAYERS) as l:
                state.update(unit=0, l=l, emptied=[-1] * 8)
                seen.loop(l)
                pe.wait_ge(params_in, 16 * PARAMS_IN * (l + 1))
                b = take("params")
                pe.transpose(b[:, 0:P], params[:, 0, :], ident)
                tile(pe.transpose(b[:, P:P + 92], params[0:92, 1, :], ident[0:92, 0:92]))
                for tt in range(TT):
                    pe.wait_ge(h_ready, seen(h_ready))
                turn_h([f"h{j}" for j in range(4)], htok)
                read(*[f"h{j}" for j in range(4)])
                for n in IN2[0:5]:
                    project(n)
                read("pu0", "pu1")
                for g in range(4):
                    b = take(f"diff{g}")
                    for st in range(TT):
                        last = pe.matmul(b[:, 0:T], pu[:, st, g * P:g * P + P], bands[:, st, g, :], start=(st == 0),
                                         stop=(st == TT - 1))
                    tile(last)
                for g in range(4):
                    b = take(f"pool{g}")
                    read(f"diff{g}")
                    tile(pe.matmul(b[:, 0:T], wpool[:, g, :], diffT[:, g, :], start=True, stop=True))
                pe.wait_ge(rope_ready, seen(rope_ready))
                for i in range(2):
                    b = take(f"qturn{i}")
                    for c in range(2):
                        for tt in range(TT):
                            a = (2 * i + c) * P
                            last = pe.transpose(b[:, c * T + tt * P:c * T + tt * P + P], qk[:, tt, a:a + P], ident)
                    tile(last)
                b = take("kturn")
                for g in range(A_KV):
                    for tt in range(TT):
                        last = pe.transpose(b[:, g * T + tt * P:g * T + tt * P + P],
                                            kdup[:, tt, g, :, :].rearrange("p c d -> p (c d)"), ident)
                tile(last)
                read("qturn0", "qturn1", "kturn")
                group = HEADS // A_KV
                scores("a", qTa, lambda h, o: kTa[o:o + DH, h // group, :])
                for n in IN2[5:11]:
                    (project if n[0] == "v" else project_T)(n)
                values("a", lambda h, c: va2[:, c, (h // group) * DH:(h // group) * DH + DH])
                read(*IN2[5:11])
                scores("c", qTc, lambda h, o: kTc[o:o + DH, h // 2, :])
                for n in IN2[11:]:
                    project_T(n)
                values("c", lambda h, c: vc[:, c, h * DH:h * DH + DH])
                read(*[f"pool{g}" for g in range(4)], *[f"{s}out{p}" for s in "ac" for p in range(PAIRS)])
                for u in range(6):
                    bs = [take(f"branch{u}{i}") for i in range(2)]
                    wv = unit_at(next_unit()).rearrange("p (k n) -> p k n", k=4)
                    for i in range(2):
                        for c in range(2):
                            n0 = (2 * i + c) * P
                            for k in range(4):
                                last = pe.matmul(bs[i][:, c * T:c * T + T], wv[:, k, n0:n0 + P],
                                                 mixT[:, 4 * (u // 2) + k, :], start=(k == 0), stop=(k == 3))
                    used(last)
                pe.wait_ge(branch_ready, seen(branch_ready))
                rows_product([f"mix{j}" for j in range(4)], merged, KC)
                for tt in range(TT):
                    pe.wait_ge(h_ready, seen(h_ready))
                turn_h([f"g{j}" for j in range(4)], htok)
                read(*[f"g{j}" for j in range(4)])
                for c in range(UPAIRS):
                    project_T(f"val{c}")
                    project_T(f"gate{c}")
                pe.wait_ge(gated_ready, seen(gated_ready))
                rows_product([f"down{j}" for j in range(4)], gated, FT)
                seen.loop_end()

        @block.vector
        def _(dve):
            own, seen = Chain(dve, dve_own), Seen()
            state = dict(l=None)

            def await_full(name):
                dve.wait_ge(*(full(name) if state["l"] is None else full_l(name, state["l"])))

            def await_own(name):
                dve.wait_ge(*(emptied(name) if state["l"] is None else emptied_l(name, state["l"])))

            def leave(last, name):
                job, free = (JF, bank_free) if state["l"] is None else (JL, bank_free_l)
                last.then_inc(free[job[name][0]], 1)

            def bank(name):
                return banks[(JF if state["l"] is None else JL)[name][0]]

            def keep_scores(s, table):
                for tt in range(TT):
                    for h in range(HEADS):
                        n, r = f"{s}score{tt}{h}", tt * HEADS + h
                        await_full(n)
                        if state["l"] is not None:
                            dve.memset(negtop[:, r:r + 1], 0.0)
                        leave(dve.tensor_tensor_reduce(probs[:, tt, h, :], bank(n)[:, 0:T], table(tt, h), 1.0, LEAST,
                                                       ALU.add, ALU.max, top[:, r:r + 1]), n)
                    await_own(n)
                    r = slice(tt * HEADS, (tt + 1) * HEADS)
                    dve.tensor_scalar(negtop[:, r], top[:, r], -1.0, None, ALU.mult).then_inc(negmax_ready, 1)

            def normalise():
                for tt in range(TT):
                    dve.wait_ge(exp_done, seen(exp_done))
                    r = slice(tt * HEADS, (tt + 1) * HEADS)
                    own(dve.reciprocal(scale[:, r], total[:, r]))
                    for h in range(HEADS):
                        a = tt * HEADS + h
                        last = dve.tensor_scalar(probs[:, tt, h, :], probs[:, tt, h, :], scale[:, a:a + 1], None,
                                                 ALU.mult)
                    last.then_inc(prob_ready, 1)

            def row_scale():
                dve.wait_ge(roots, seen(roots))
                own(dve.reciprocal(rstd, root))

            def post_norm(names, gate, signal):
                dve.wait_ge(squares, seen(squares))
                pair = halves.rearrange("p (t a) -> p t a", t=TT)
                dve.tensor_tensor(meansq, pair[:, :, 0], pair[:, :, 1], ALU.add).then_inc(means, 1)
                row_scale()
                for j, n in enumerate(names):
                    tt, half = j // 2, j % 2
                    leave(dve.scalar_tensor_tensor(out=htok[:, tt, 512 * half:512 * half + 512], in0=bank(n)[:, :],
                                                   scalar=rstd[:, tt:tt + 1], in1=gate[:, 512 * half:512 * half + 512],
                                                   op0=ALU.mult, op1=ALU.mult), n)
                await_own(names[-1])
                dve.tensor_tensor(x, x, htok, ALU.add).then_inc(signal, 1)

            dve.memset(eps, EPS)
            dve.memset(zeros, 0.0)
            dve.memset(wfdup, 0.0)
            dve.memset(bforget, 0.0)
            dve.memset(rel33[BUCKETS:BUCKETS + 1, :], 1.0).then_inc(cleared, 1)
            await_full("cond")
            leave(dve.tensor_copy(condrep, bank("cond")[:, 0:KC].unsqueeze(2).broadcast_to([P, KC, 32])), "cond")
            dve.wait_ge(small_in, SMALL_IN)
            dve.wait_ge(cleared, 1)
            for a in (0, 32):
                dve.tensor_copy(wfdup[:, :, a:a + HEADS], wf)

            def ada(r, takes):
                await_full(f"ada{r}")
                leave(dve.tensor_copy(modrows[r], bank(f"ada{r}")[:, :]), f"ada{r}")
                for j, what in enumerate(takes):
                    n, half = f"mod{4 * r + j}", slice(512 * (j % 2), 512 * (j % 2) + 512)
                    await_full(n)
                    leave(what(bank(n)[:, :], half), n)

            def shift(to):
                return lambda row, half: dve.tensor_copy(to[:, half], row)

            def gain(to, g):
                return lambda row, half: dve.scalar_tensor_tensor(out=to[:, half], in0=row, scalar=1.0,
                                                                  in1=g[:, half], op0=ALU.add, op1=ALU.mult)

            def gate(to, g):
                return lambda row, half: dve.tensor_tensor(to[:, half], row, g[:, half], ALU.mult)

            def modulated(gain_row, shift_row):
                for tt in range(TT):
                    own(dve.scalar_tensor_tensor(out=htok[:, tt, :], in0=x[:, tt, :], scalar=rstd[:, tt:tt + 1],
                                                 in1=gain_row, op0=ALU.mult, op1=ALU.mult))
                    dve.tensor_tensor(htok[:, tt, :], htok[:, tt, :], shift_row, ALU.add).then_inc(h_ready, 1)

            row_scale()
            ada(0, 2 * [shift(shift_m)] + 2 * [gain(gain_m, gpre_m)])
            await_own("mod1")
            await_own("mod3")
            modulated(gain_m, shift_m)
            await_full("forget")
            leave(dve.tensor_scalar(fz, bank("forget")[0:40, 0:T], bforget[0:40, :], None, ALU.add), "forget")
            await_own("forget")
            dve.scalar_tensor_tensor(out=fa, in0=fz, scalar=-1.0, in1=fz, op0=ALU.mult, op1=ALU.max)\
                .then_inc(log_in, 1)
            own(dve.tensor_scalar(fm, fz, 0.0, None, ALU.min))
            dve.wait_ge(scan_in, 1)
            own(dve.tensor_tensor(fm, fm, fe, ALU.subtract))
            own(dve.tensor_tensor_scan(fcum, ones[0:40, 0:1].broadcast_to([40, T]), fm, 0.0, ALU.mult, ALU.add))
            own(dve.tensor_tensor(fox_rhs[32:40], fox_rhs[32:40], fcum[32:40].unsqueeze(1).broadcast_to([8, HEADS, T]),
                                  ALU.mult))
            dve.memset(fcum[32:40, :], 1.0).then_inc(fox_ready, 1)
            keep_scores("a", lambda tt, h: causal[:, tt, :])
            normalise()
            dve.wait_ge(table_in, 32)
            keep_scores("b", lambda tt, h: tables[:, tt, h, :])
            ada(1, 2 * [gate(gate_m, gpost_m)] + 2 * [shift(shift_f)])
            ada(2, 2 * [gain(gain_f, gpre_f)] + 2 * [gate(gate_f, gpost_f)])
            normalise()
            post_norm([f"mix{j}" for j in range(4)], gate_m, x_mid)
            dve.wait_ge(x_mid, seen(x_mid))
            row_scale()
            modulated(gain_f, shift_f)
            await_full("logits")
            leave(dve.tensor_tensor(logits, by_tile(bank("logits")[:, 0:TT * EXPERTS]),
                                    brt.unsqueeze(1).broadcast_to([P, TT, EXPERTS]), ALU.add), "logits")
            await_own("logits")
            for tt in range(TT):
                own(dve.max(best[:, tt, :], logits[:, tt, :]))
                own(dve.max_index(picked[:, 8 * tt:8 * tt + 8], best[:, tt, :], logits[:, tt, :]))
            own(dve.tensor_copy(bestf.rearrange("p t k -> p (t k)"), picked[:, :]))
            for tt in range(TT):
                last = dve.tensor_scalar(gate4[:, tt, :], best[:, tt, 0:TOPK], best[:, tt, 0:1], None, ALU.subtract)
            last.then_inc(gates_in, 1)
            for tt in range(TT):
                for k in range(TOPK):
                    last = dve.tensor_scalar(equal4[:, k, :], experts, bestf[:, tt, k:k + 1], None, ALU.is_equal)
                own(last)
                last = dve.tensor_reduce(chosen[:, tt, :], equal4.rearrange("p k e -> p e k"), AX_X, ALU.add)
                if tt < TT - 1:
                    own(last)
            last.then_inc(route_ready, 1)
            await_full("counts")
            leave(dve.tensor_copy(starts, bank("counts")[0:EXPERTS, 0:1]), "counts")
            await_own("counts")
            own(dve.tensor_scalar(nblk, starts, float(CAP), 1.0, ALU.is_gt, ALU.add))
            for p in range(2, T // CAP):
                last = dve.scalar_tensor_tensor(out=nblk, in0=starts, scalar=float(CAP * p), in1=nblk, op0=ALU.is_gt,
                                                op1=ALU.add)
                if p < T // CAP - 1:
                    own(last)
            last.then_inc(route_ready, 1)
            dve.wait_ge(gates_exp, 1)
            own(dve.reciprocal(gsum, gsum))
            for tt in range(TT):
                own(dve.tensor_scalar(gate4[:, tt, :], gate4[:, tt, :], gsum[:, tt:tt + 1], None, ALU.mult))
            for tt in range(TT):
                for k in range(TOPK):
                    last = dve.tensor_scalar(equalg[:, k, :], experts, bestf[:, tt, k:k + 1], gate4[:, tt, k:k + 1],
                                             ALU.is_equal, ALU.mult)
                own(last)
                own(dve.tensor_reduce(gates_te[:, tt, :], equalg.rearrange("p k e -> p e k"), AX_X, ALU.add))
            await_full("places")
            leave(dve.scalar_tensor_tensor(out=place, in0=by_tile(bank("places")[:, 0:TT * EXPERTS]), scalar=NOT_CHOSEN,
                                           in1=chosen, op0=ALU.add, op1=ALU.mult), "places")
            await_own("places")
            dve.tensor_scalar(place, place, -NOT_CHOSEN, None, ALU.add).then_inc(route_ready, 1)
            await_full("ends")
            leave(dve.tensor_copy(ends, bank("ends")[0:EXPERTS, 0:1]), "ends")
            await_own("ends")
            own(dve.tensor_tensor(starts, ends, nblk, ALU.subtract))
            dve.tensor_scalar(done_e, blocks[0:EXPERTS, :], ends, None, ALU.is_ge)
            own(dve.tensor_scalar(begun_e, blocks[0:EXPERTS, :], starts, None, ALU.is_ge))
            dve.tensor_tensor(onehot, begun_e, done_e, ALU.subtract).then_inc(route_ready, 1)
            own(dve.tensor_scalar(starts, starts, float(CAP), None, ALU.mult))
            await_full("turned")
            dve.tensor_scalar(posT, bank("turned")[0:EXPERTS, 0:T], starts, None, ALU.add)
            leave(dve.tensor_copy(gateT, bank("turned")[0:EXPERTS, T:2 * T]), "turned")
            await_full("list")
            leave(dve.tensor_copy(lists[0:1, 0:BLOCKS + 2], bank("list")[0:1, 0:BLOCKS + 2]), "list")
            for tt in range(TT):
                await_full(f"spread{tt}")
                dve.scalar_tensor_tensor(out=blkpos[:, tt, :], in0=blocks, scalar=-float(CAP),
                                         in1=bank(f"spread{tt}")[:, 0:BLOCKS + 1], op0=ALU.mult, op1=ALU.add)
                leave(dve.tensor_copy(blkgate[:, tt, :], bank(f"spread{tt}")[:, 64:64 + BLOCKS + 1]), f"spread{tt}")
            dve.memset(yblk, 0.0).then_inc(y_ready, 1)
            for tt in range(TT):
                await_own(f"spread{tt}")

            def select(at):
                for tt in range(TT):
                    last = dve.tensor_scalar(sel[:, tt, :], slots[:, 0:CAP], blkpos[:, tt, at], None, ALU.is_equal)
                last.then_inc(sel_ready, 1)

            select(slice(0, 1))
            await_own("list")
            n_blocks = dve.value_load(lists[0:1, BLOCKS + 1:BLOCKS + 2], min_val=EXPERTS, max_val=BLOCKS)
            with dve.Fori(0, n_blocks) as i:
                own.loop(i, 2)
                for tt in range(TT):
                    last = dve.tensor_scalar(selg[:, tt, :], slots, blkpos[:, tt, bass.ds(i, 1)],
                                             blkgate[:, tt, bass.ds(i, 1)], ALU.is_equal, ALU.mult)
                last.then_inc(selg_ready, 1)
                dve.wait_ge(gathered, i + 1)
                select(bass.ds(i + 1, 1))
                dve.wait_ge(hidden_done, i + 1)
                dve.tensor_scalar(glu, banks[4][:, :], SWIGLU_LIMIT, None, ALU.min).then_inc(clamped, 1)
                own(dve.tensor_scalar(lin, banks[5][:, :], -SWIGLU_LIMIT, SWIGLU_LIMIT, ALU.max, ALU.min))
                dve.wait_ge(clamped, i + 1)
                own(dve.scalar_tensor_tensor(out=lin1, in0=lin, scalar=1.0, in1=glu, op0=ALU.add, op1=ALU.mult))
                dve.wait_ge(sig_ready, i + 1)
                dve.tensor_tensor(act_row, lin1, sig, ALU.mult).then_inc(act_ready, 1)
                dve.wait_ge(down_done, i + 1)
                dve.tensor_copy(yblk, banks[4][:, :]).then_inc(y_ready, 1)
            own.loop_end(n_blocks)
            dve.wait_ge(squares, seen(squares))
            pair = halves.rearrange("p (t a) -> p t a", t=TT)
            dve.tensor_tensor(meansq, pair[:, :, 0], pair[:, :, 1], ALU.add).then_inc(means, 1)
            dve.wait_ge(roots, seen(roots))
            dve.reciprocal(rstd, root).then_inc(bank_free_l[7], 1)
            dve.wait_ge(bank_free_l[7], 1)
            quarters = [(j // 2, slice(512 * (j % 2), 512 * (j % 2) + 512)) for j in range(4)]
            for j, (tt, half) in enumerate(quarters):
                dve.scalar_tensor_tensor(out=htok[:, tt, half], in0=banks[j][:, :], scalar=rstd[:, tt:tt + 1],
                                         in1=gate_f[:, half], op0=ALU.mult, op1=ALU.mult).then_inc(bank_free_l[j], 1)
            for j, (tt, half) in enumerate(quarters):
                dve.wait_ge(bank_free_l[j], 1)
                dve.tensor_tensor(x[:, tt, half], x[:, tt, half], htok[:, tt, half], ALU.add)\
                    .then_inc(bank_free_l[4 + j] if j < 3 else layer_in, 1)

            with dve.Fori(0, LAYERS) as l:
                state["l"] = l
                own.loop(l, DVE_LAYER)
                seen.loop(l)
                await_full("params")
                leave(dve.tensor_copy(columns[:, 0:220], bank("params")[:, 0:220]), "params")
                dve.wait_ge(layer_in, l + 1)

                def normed():
                    row_scale()
                    for tt in range(TT):
                        dve.tensor_scalar(htok[:, tt, :], x[:, tt, :], rstd[:, tt:tt + 1], None, ALU.mult)\
                            .then_inc(h_ready, 1)

                normed()
                await_own("kv")
                own(dve.tensor_tensor(qksq, qk, qk, ALU.mult))
                dve.tensor_reduce(qkms, qksq.rearrange("p t (h d) -> p (t h) d", d=DH), AX_X, ALU.add)\
                    .then_inc(qk_means, 1)
                dve.wait_ge(roots, seen(roots))
                own(dve.reciprocal(qkr, qkms))
                n_heads = HEADS + A_KV
                qk_heads = qk.rearrange("p t (h d) -> p (t h) d", d=DH)
                own(dve.tensor_tensor(qk_heads, qk_heads, qkr.unsqueeze(2).broadcast_to([P, TT * n_heads, DH]), ALU.mult))
                dve.wait_ge(params_in, 16 * PARAMS_IN * (l + 1))
                own(dve.tensor_tensor(qk, qk, gqk.unsqueeze(1).broadcast_to([P, TT, n_heads * DH]), ALU.mult))
                for tt in range(TT):
                    def heads(a):
                        return a[:, tt, :].rearrange("p (h d) -> p h d", d=DH)

                    def angle(name):
                        return by_tile(const(name))[:, tt, :]

                    dve.tensor_tensor(heads(rope1), heads(qk), angle("cos").unsqueeze(1).broadcast_to([P, n_heads, DH]),
                                      ALU.mult)
                    sin = angle("sin").rearrange("p (a b d) -> p a b d", a=2, b=2)
                    q5 = heads(qk).rearrange("p h (a b d) -> p h a b d", a=2, b=2)
                    r5 = heads(rope2).rearrange("p h (a b d) -> p h a b d", a=2, b=2)
                    for b in range(2):
                        last = dve.tensor_tensor(r5[:, :, :, b, :], q5[:, :, :, 1 - b, :],
                                                 sin[:, :, b, :].unsqueeze(1).broadcast_to([P, n_heads, 2, 16]), ALU.mult)
                own(last)
                dve.tensor_tensor(qk[:, :, 0:MIX], rope1[:, :, 0:MIX], rope2[:, :, 0:MIX], ALU.add)
                for tt in range(TT):
                    for c in range(2):
                        k1, k2 = (r[:, tt, MIX:].rearrange("p (g d) -> p g d", d=DH) for r in (rope1, rope2))
                        last = dve.tensor_tensor(kdup[:, tt, :, c, :], k1, k2, ALU.add)
                last.then_inc(rope_ready, 1)
                keep_scores("a", lambda tt, h: zeros)
                normalise()
                dve.wait_ge(bias_masked, l + 1)
                keep_scores("c", lambda tt, h: tables[:, tt, h, :])
                normalise()
                await_own("gl11")
                for u in range(6):
                    for i in range(2):
                        n, c = f"branch{u}{i}", 4 * (u % 2) + 2 * i
                        await_full(n)
                        part = gates[u // 2][:, c:c + 2, :]
                        leave(dve.tensor_tensor(part, bank(n)[:, :].rearrange("p (c t) -> p c t", c=2), part, ALU.mult), n)
                await_own("branch51")
                own(dve.tensor_tensor(merged, gates[0], gates[1], ALU.add))
                dve.tensor_tensor(merged, merged, gates[2], ALU.add).then_inc(branch_ready, 1)
                post_norm([f"mix{j}" for j in range(4)], gpost2[0], x_mid)
                dve.wait_ge(x_mid, seen(x_mid))
                normed()

                def product(c):
                    dve.wait_ge(gelu_ready, seen(gelu_ready))
                    last = dve.tensor_tensor(gated[:, 2 * c:2 * c + 2, :], conv[2 * (c % 2)], conv[2 * (c % 2) + 1], ALU.mult)
                    last.then_inc(conv_ready if c < UPAIRS - 1 else gated_ready, 1)

                for c in range(UPAIRS):
                    for half, name in enumerate(("val", "gate")):
                        n, cv = f"{name}{c}", conv[2 * (c % 2) + half]
                        up = bank(n)[:, :].rearrange("p (m t) -> p m t", m=2)
                        dve.wait_ge(conv_in, seen(conv_in))
                        for m in range(2):
                            f = FT * half + 2 * c + m
                            last = dve.scalar_tensor_tensor(out=cv[:, m, 1:T], in0=up[:, m, 0:T - 1],
                                                            scalar=c_conv0(f), in1=cv[:, m, 1:T], op0=ALU.mult, op1=ALU.add)
                        own(last)
                        for m in range(2):
                            f = FT * half + 2 * c + m
                            last = dve.scalar_tensor_tensor(out=cv[:, m, 0:T - 1], in0=up[:, m, 1:T],
                                                            scalar=c_conv2(f), in1=cv[:, m, 0:T - 1], op0=ALU.mult, op1=ALU.add)
                        leave(last, n)
                    if c:
                        product(c - 1)
                await_own(f"val{UPAIRS - 1}")
                product(UPAIRS - 1)
                post_norm([f"down{j}" for j in range(4)], gpost2[1], layer_in)
                own.loop_end(LAYERS)
                seen.loop_end()

        @block.scalar
        def _(act):
            own, seen = Chain(act, act_own), Seen()
            state = dict(l=None)

            def await_full(name):
                act.wait_ge(*(full(name) if state["l"] is None else full_l(name, state["l"])))

            def bank(name):
                return banks[(JF if state["l"] is None else JL)[name][0]]

            def leave(last, name):
                job, free = (JF, bank_free) if state["l"] is None else (JL, bank_free_l)
                last.then_inc(free[job[name][0]], 1)

            def copy(name, to, scale=1.0, width=512):
                await_full(name)
                source = bank(name)[0:to.shape[0], 0:width]
                if len(to.shape) == 3:
                    source = source.rearrange("p (a b) -> p a b", a=to.shape[1])
                leave(act.activation(to, source, ACT.Copy, scale=scale), name)

            def exps(tables=None):
                for tt in range(TT):
                    act.wait_ge(negmax_ready, seen(negmax_ready))
                    for h in range(HEADS):
                        r = slice(tt * HEADS + h, tt * HEADS + h + 1)
                        last = act.activation(probs[:, tt, h, :], probs[:, tt, h, :], ACT.Exp, bias=negtop[:, r],
                                              accum_out=total[:, r])
                    last.then_inc(exp_done, 1)

            def turn_and_out(s, chunk):
                for h in range(HEADS):
                    copy(f"{s}turn{h}", turned[:, h, :, :])
                for p in range(PAIRS):
                    copy(f"{s}out{p}", mixT[:, chunk + p, :], width=T)

            def take_root():
                act.activation(root, meansq, ACT.Sqrt, bias=eps).then_inc(roots, 1)

            def square_x():
                for tt in range(TT):
                    last = act.activation(htok[:, tt, :], x[:, tt, :], ACT.Square, scale=D ** -0.5,
                                          accum_out=meansq[:, tt:tt + 1])
                own(last)
                take_root()

            def square_banks(sources):
                for j, b in enumerate(sources):
                    last = act.activation(htok[:, j // 2, 512 * (j % 2):512 * (j % 2) + 512], b, ACT.Square,
                                          scale=D ** -0.5, accum_out=halves[:, j:j + 1])
                last.then_inc(squares, 1)
                act.wait_ge(means, seen(means))
                take_root()

            act.dma_start(crow, c_in[0].rearrange("(k p) -> k p", p=P)).then_inc(cond_in, 16)
            act.dma_start(consts[:, :], shape_table).then_inc(consts_in, 16)
            act.wait_ge(cond_in, 16)
            act.activation(crow, crow, ACT.Silu).then_inc(cond_rows, 1)
            act.wait_ge(cleared, 1)
            w_f = w_in[0].rearrange("(k p) n -> p k n", p=P)[:, :, 6 * MIX:6 * MIX + HEADS]
            loads = [(bada, b_ada[0].rearrange("(r n) -> r n", n=512)), (wf, w_f), (rel33[0:BUCKETS, :], rel_bias),
                     (bforget[0:HEADS, :], b_forget[0].rearrange("(h a) -> h a", a=1)),
                     (bforget[32:32 + HEADS, :], b_forget[0].rearrange("(h a) -> h a", a=1)),
                     (side[0:40, :], fox_table), (gpre_m, g_pre_mix[0].partition_broadcast(P)),
                     (gpost_m, g_post_mix[0].partition_broadcast(P)), (gpre_f, g_pre_ffn[0].partition_broadcast(P)),
                     (gpost_f, g_post_ffn[0].partition_broadcast(P)),
                     (wrt, w_router[0].rearrange("(k p) e -> p k e", p=P)), (brt, b_router[0].partition_broadcast(P))]
            assert 16 * len(loads) == SMALL_IN
            for to, source in loads:
                act.dma_start(to, source).then_inc(small_in, 16)
            act.wait_ge(x_in_sem, 16)
            square_x()
            copy("table", trow)
            for j in range(4):
                copy(f"h{j}", hT[:, 2 * j:2 * j + 2, :])
            act.wait_ge(log_in, 1)
            own(act.activation(fe, fa, ACT.Exp, scale=-1.0))
            act.activation(fe, fe, ACT.Ln, bias=ones[0:40, 0:1]).then_inc(scan_in, 1)

            def projections(names, views):
                for n in names:
                    i = int(n[-1])
                    to = views[n[:-1]]
                    if n[0] == "v":
                        copy(n, to[:, :, 256 * i:256 * i + 256])
                    else:
                        copy(n, to[:, 2 * i:2 * i + 2, :], scale=QK_SCALE if n[0] == "q" else 1.0)

            projections(IN1[0:6], proj1)
            exps()
            projections(IN1[6:], proj1)
            turn_and_out("a", 0)
            exps()
            turn_and_out("b", 4)
            await_full("mix3")
            square_banks([bank(f"mix{j}")[:, :] for j in range(4)])
            act.wait_ge(x_mid, seen(x_mid))
            square_x()
            for j in range(4):
                copy(f"g{j}", hT[:, 2 * j:2 * j + 2, :])
            act.wait_ge(gates_in, 1)
            for tt in range(TT):
                last = act.activation(gate4[:, tt, :], gate4[:, tt, :], ACT.Exp, accum_out=gsum[:, tt:tt + 1])
            last.then_inc(gates_exp, 1)
            act.wait_ge(*emptied("list"))
            n_blocks = act.value_load(lists[0:1, BLOCKS + 1:BLOCKS + 2], min_val=EXPERTS, max_val=BLOCKS)
            act.activation(selgT, zeros, ACT.Copy).then_inc(selgT_ready, 1)

            def rows_out(n):
                act.wait_ge(gathered, n)
                act.activation(xrow, banks[6][:, :], ACT.Copy).then_inc(xrow_ready, 1)

            def rows_turned(n):
                act.wait_ge(xg_turned, n)
                act.activation(xgT.rearrange("p b j s -> p (b j s)"), banks[6][:, :], ACT.Copy).then_inc(xg_ready, 1)

            rows_out(1)
            rows_turned(1)
            with act.Fori(0, n_blocks) as i:
                act.wait_ge(clamped, i + 1)
                act.activation(sig, glu, ACT.Sigmoid, scale=SWIGLU_ALPHA).then_inc(sig_ready, 1)
                act.wait_ge(selg_turned, i + 1)
                act.activation(selgT, banks[7][:, 0:T], ACT.Copy).then_inc(selgT_ready, 1)
                rows_out(i + 2)
                act.wait_ge(act_turned, i + 1)
                act.activation(actT.rearrange("p b j s -> p (b j s)"), banks[7][:, :], ACT.Copy).then_inc(actT_ready, 1)
                rows_turned(i + 2)
            act.wait_ge(moe_done, 4 + 4 - RING)
            square_banks([banks[j][:, :] for j in range(4)])

            with act.Fori(0, LAYERS) as l:
                state["l"] = l
                own.loop(l, 2)
                seen.loop(l)
                act.wait_ge(layer_in, l + 1)
                square_x()
                act.wait_ge(*emptied_l("params", l))

                def turn_h(prefix, column):
                    for j in range(4):
                        await_full(f"{prefix}{j}")
                        for kk in range(2):
                            k = 2 * j + kk
                            last = act.activation(hT[:, k, :], bank(f"{prefix}{j}")[:, kk * T:kk * T + T], ACT.Copy,
                                                  scale=column[:, k:k + 1])
                        leave(last, f"{prefix}{j}")

                turn_h("h", c_pre)
                for i in range(2):
                    copy(f"qa{i}", qk[:, :, 256 * i:256 * i + 256])
                await_full("kv")
                kv = bank("kv")[:, :].rearrange("p (t n) -> p t n", t=TT)
                act.activation(qk[:, :, MIX:MIX + P], kv[:, :, 0:P], ACT.Copy)
                leave(act.activation(va2, kv[:, :, P:2 * P], ACT.Copy), "kv")
                for i in range(2):
                    copy(f"pu{i}", pu[:, :, 256 * i:256 * i + 256])
                act.wait_ge(qk_means, seen(qk_means))
                act.activation(qkms, qkms, ACT.Sqrt, scale=1.0 / DH, bias=eps).then_inc(roots, 1)
                for g in range(4):
                    copy(f"diff{g}", diffT[:, g, :], width=T)
                for g in range(4):
                    n = f"pool{g}"
                    await_full(n)
                    leave(act.activation(mixT[:, 4 + g, :], bank(n)[:, 0:T], ACT.Copy, scale=c_pool[:, g:g + 1]), n)
                for i in range(2):
                    copy(f"qturn{i}", qTa[:, 2 * i:2 * i + 2, :], scale=QK_SCALE)
                copy("kturn", kTa)
                exps()
                projections(IN2[5:11], dict(qc=qTc, kc=kTc, vc=vc))
                turn_and_out("a", 0)
                exps()
                for i in range(12):
                    n = f"gl{i}"
                    await_full(n)
                    for m in range(2):
                        f = 2 * i + m
                        last = act.activation(gates[f // KC][:, f % KC, :], bank(n)[:, m * T:m * T + T], ACT.Sigmoid,
                                              bias=c_gate[:, f:f + 1])
                    leave(last, n)
                turn_and_out("c", 8)
                await_full("mix3")
                square_banks([bank(f"mix{j}")[:, :] for j in range(4)])
                act.wait_ge(x_mid, seen(x_mid))
                square_x()
                turn_h("g", c_ffn)

                def gelu(c):
                    act.wait_ge(*emptied_l(f"gate{c}", l))
                    cv = conv[2 * (c % 2) + 1]
                    act.activation(cv, cv, ACT.Gelu_apprx_tanh).then_inc(gelu_ready, 1)

                for c in range(UPAIRS):
                    if c >= 2:
                        act.wait_ge(conv_ready, l * (UPAIRS - 1) + (c - 1))
                    for half, name in enumerate(("val", "gate")):
                        n = f"{name}{c}"
                        await_full(n)
                        for m in range(2):
                            f = FT * half + 2 * c + m
                            last = act.activation(conv[2 * (c % 2) + half][:, m, :], bank(n)[:, m * T:m * T + T],
                                                  ACT.Identity, scale=c_conv1(f), bias=c_bias[:, f:f + 1])
                        last.then_inc(conv_in, 1)
                    if c:
                        gelu(c - 1)
                gelu(UPAIRS - 1)
                await_full("down3")
                square_banks([bank(f"down{j}")[:, :] for j in range(4)])
                own.loop_end(LAYERS)
                seen.loop_end()

        @block.gpsimd
        def _(pool):
            for layer_ in range(LAYERS):
                pool.dma_start(rpb_copies[layer_], rpb[layer_].rearrange("h r c -> (h r c)").partition_broadcast(GRID_W))\
                    .then_inc(rpb_out, 16)
            pool.wait_ge(*emptied("table"))
            pool.dma_start(distances.rearrange("q h d -> h q d"), trow.unsqueeze(1).broadcast_to([HEADS, P, 2 * T]))\
                .then_inc(table_out, 16)
            pool.wait_ge(table_out, 16)
            for tt in range(TT):
                pitch = HEADS * 2 * T
                shifted = bass.AP(distances.tensor, T - 1 - P * tt, [[pitch - 1, P], [2 * T, HEADS], [1, T]])
                pool.dma_start(tables[:, tt, :, :], shifted).then_inc(table_in, 16)
            pool.wait_ge(rpb_out, 16 * LAYERS)
            pitch = HEADS * RPB_HEAD
            for layer_ in range(LAYERS):
                for r in range(GRID_H):
                    for rk in range(GRID_H):
                        start = layer_ * GRID_W * pitch + (rk - r + NA_ROWS - 1) * RPB_ROW + NA_COLS - 1
                        source = bass.AP(rpb_copies.tensor, start, [[pitch - 1, GRID_W], [RPB_HEAD, HEADS], [1, GRID_W]])
                        to = neighbours[layer_, GRID_W * (r % 2):GRID_W * (r % 2) + GRID_W, r // 2, :,
                                        GRID_W * rk:GRID_W * rk + GRID_W]
                        pool.dma_start(to, source).then_inc(neighbours_out, 16)
            pool.wait_ge(h_ready, 4)
            pool.dma_start(bdown, b_down[0]).then_inc(bdown_in, 16)
            pool.wait_ge(neighbours_out, 16 * LAYERS * GRID_H * GRID_H)
            with pool.Fori(0, LAYERS) as l:
                one = bass.ds(l, 1)
                pool.wait_ge(layer_in, l + 1)

                def over_heads(a, n):
                    return a[one].rearrange("l d -> (l d)").unsqueeze(0).broadcast_to([n, DH]).partition_broadcast(P)

                conv_rows = conv_w[one].rearrange("l c (f p) -> (l c f) p", p=P)
                loads = [(params[0:88, 0, :], conv_rows[0:88, :]), (params[0:44, 1, :], conv_rows[88:132, :]),
                         (params[88:112, 0, :], b_gate2[one].rearrange("l (f p) -> (l f) p", p=P)),
                         (params[112:120, 0, :], norm_mix_pre[one].rearrange("l (f p) -> (l f) p", p=P)),
                         (params[120:128, 0, :], norm_ffn_pre[one].rearrange("l (f p) -> (l f) p", p=P)),
                         (params[44:88, 1, :], conv_b[one].rearrange("l (f p) -> (l f) p", p=P)),
                         (params[88:92, 1, :], pool_scale[one].rearrange("l (f p) -> (l f) p", p=P)),
                         (gqk[:, 0:MIX].rearrange("p (h d) -> p h d", d=DH), over_heads(qk_q, HEADS)),
                         (gqk[:, MIX:].rearrange("p (h d) -> p h d", d=DH), over_heads(qk_k, A_KV)),
                         (wpool, w_pool[one].rearrange("l g c d -> (l c) g d")),
                         (gpost2[0], norm_mix_post[one].rearrange("l d -> (l d)").partition_broadcast(P)),
                         (gpost2[1], norm_ffn_post[one].rearrange("l d -> (l d)").partition_broadcast(P))]
                assert len(loads) == PARAMS_IN
                for to, source in loads:
                    pool.dma_start(to, source).then_inc(params_in, 16)
                pool.dma_start(tables.rearrange("p t h k -> p (t h k)"),
                               neighbours[one].rearrange("l p t h k -> (l p) (t h k)")).then_inc(bias_l_in, 16)
                pool.wait_ge(bias_l_in, 16 * (l + 1))
                groups = tables.rearrange("p t h (r c) -> p (t h r) c", c=GRID_W)
                pool.tensor_tensor(groups, groups, const("window").unsqueeze(1).broadcast_to(
                    [P, TT * HEADS * GRID_H, GRID_W]), ALU.add).then_inc(bias_masked, 1)


_INS = ["x", "c", "w_ada", "b_ada", "g_pre_mix", "g_post_mix", "w_in", "b_forget", "rel_bias", "w_out", "g_pre_ffn",
        "g_post_ffn", "w_router", "b_router", "w_gate_up", "b_gate_up", "w_down", "b_down", "norm_mix_pre_2",
        "norm_mix_post_2", "norm_ffn_pre_2", "norm_ffn_post_2", "w_in_2", "b_gate_2", "qk_norm_q_2", "qk_norm_k_2",
        "w_pool_2", "pool_scale_2", "rpb_2", "w_branch_2", "w_out_2", "w_up_2", "conv_w_2", "conv_b_2", "w_down_2"]


def kernel(**inputs):
    import concourse.bacc as bacc
    from concourse.bass_utils import run_bass_kernel_spmd

    nc = bacc.Bacc("TRN2", target_bir_lowering=False, num_devices=1)
    table, table_at, fox = shape_tables()
    arrays, args = {}, []
    for name in _INS:
        arrays[f"in_{name}"] = np.ascontiguousarray(inputs[name])
    arrays["shape_table"], arrays["fox_table"] = table, fox
    for name, a in arrays.items():
        args.append(nc.dram_tensor(name, a.shape, mybir.dt.from_np(a.dtype), kind="ExternalInput").ap())
    args.append(nc.dram_tensor("out_x", (1, T, D), F32, kind="ExternalOutput").ap())
    build(nc, *args, table_at)
    return run_bass_kernel_spmd(nc, [arrays], core_ids=[0]).results[0]["out_x"]
```

```python
import math

import concourse.bass as bass
import numpy as np
from concourse import mybir
from contextlib import ExitStack

F32 = mybir.dt.float32
F32R = mybir.dt.float32r
I32 = mybir.dt.int32
U32 = mybir.dt.uint32
ALU = mybir.AluOpType
ACT = mybir.ActivationFunctionType
AX_X = mybir.AxisListType.X

P = 128
T = 256
TT = T // P
D = 1024
KC = D // P
UNIT = 2048
HEADS, DH = 8, 64
PAIRS = HEADS // 2
MIX = HEADS * DH
EPS = 1e-6
MASKED = -1e30
LEAST = -3e38
QK_SCALE = DH ** -0.5

RING = 6
RING_L = 3
HALVES = 2
MOE_UNITS = 12
EXPERTS, TOPK = 32, 4
CAP = 64
BLOCKS = EXPERTS + T * TOPK // (CAP + 1)
SWIGLU_LIMIT, SWIGLU_ALPHA = 7.0, 1.702
BUCKETS, MAX_DISTANCE = 32, 128
NOT_CHOSEN = 1000.0

LAYERS = 2
A_KV = 2
GRID_W, GRID_H = 64, T // 64
NA_ROWS, NA_COLS = 8, 16
RPB_ROW = 2 * NA_COLS - 1
RPB_HEAD = (2 * NA_ROWS - 1) * RPB_ROW
WINDOWS = (2, 4, 8, 16)
D_FF = 2816
FT = D_FF // P
D_IN2 = 5888
UPAIRS = D_FF // 256

SMALL_IN = 16 * 12
PARAMS_IN = 12
DVE_LAYER = 36


def shape_tables():
    parts = {}
    parts["ident"] = np.eye(P)
    parts["ones"] = np.ones((P, P))
    q, k = np.arange(T)[:, None], np.arange(T)[None, :]
    causal = np.where(k <= q, 0.0, MASKED)
    parts["causal"] = np.concatenate([causal[:P], causal[P:]], 1)
    col = np.arange(P) % GRID_W
    first = np.clip(col - NA_COLS // 2, 0, GRID_W - NA_COLS)
    key = np.arange(GRID_W)[None, :]
    inside = (key >= first[:, None]) & (key < first[:, None] + NA_COLS)
    parts["window"] = np.where(inside, 0.0, MASKED)
    t = np.arange(T)
    bands = []
    for st in range(TT):
        for w in WINDOWS:
            lo, hi = np.clip(t - w // 2, 0, T), np.clip(t + w - w // 2, 0, T)
            s = (st * P + np.arange(P))[:, None]
            mean = np.where((s >= lo) & (s < hi), np.float32(1.0) / (hi - lo).astype(np.float32), 0.0)
            bands.append(mean - (s == t))
    parts["bands"] = np.concatenate(bands, 1)
    freqs = np.float32(10000.0) ** (-np.arange(0, 32, 2, dtype=np.float32) / np.float32(32))
    cos, sin = [], []
    for st in range(TT):
        tok = st * P + np.arange(P)
        for pos in (tok // GRID_W, tok % GRID_W):
            ang = pos.astype(np.float32)[:, None] * freqs[None, :]
            cos += [np.cos(ang), np.cos(ang)]
            sin += [-np.sin(ang), np.sin(ang)]
    parts["cos"], parts["sin"] = np.concatenate(cos, 1), np.concatenate(sin, 1)
    parts["before"] = (np.arange(P)[:, None] < np.arange(P)[None, :])
    parts["upto"] = (np.arange(P)[:, None] <= np.arange(EXPERTS)[None, :])
    parts["slots"] = np.tile(np.arange(CAP), (P, 2))
    parts["blocks"] = np.tile(np.arange(BLOCKS + 1), (P, 1))
    parts["experts"] = np.tile(np.arange(EXPERTS), (P, 1))
    d = T - 1 - np.arange(2 * T)
    exact = BUCKETS // 2
    far = np.maximum(d, 1).astype(np.float32)
    large = exact + (np.log(far / np.float32(exact)) / np.float32(math.log(MAX_DISTANCE / exact))
                     * np.float32(BUCKETS - exact)).astype(np.int32)
    bucket = np.where(d < exact, d, np.minimum(large, BUCKETS - 1))
    onehot = np.zeros((P, 2 * T))
    onehot[:BUCKETS] = (bucket[None, :] == np.arange(BUCKETS)[:, None]) & (d >= 0)
    onehot[BUCKETS] = np.where(d >= 0, 0.0, MASKED)
    onehot[64:76, :12 * 32] = np.arange(12)[:, None] == np.repeat(np.arange(12), 32)[None, :]
    onehot[96:100, :4 * CAP] = np.arange(4)[:, None] == np.repeat(np.arange(4), CAP)[None, :]
    parts["picks"] = onehot
    at, offset = {}, 0
    for name, a in parts.items():
        at[name] = (offset, a.shape[1])
        offset += a.shape[1]
    table = np.concatenate([np.asarray(a, np.float32) for a in parts.values()], 1)
    fox = np.zeros((40, HEADS, T), np.float32)
    for h in range(HEADS):
        fox[h, h], fox[32 + h, h] = 1.0, -1.0
    return np.ascontiguousarray(table), at, fox.reshape(40, HEADS * T)


class Plan:

    def __init__(self):
        self.tiles, self.units, self.jobs, self.uses, self.at = 0, 0, {}, [0] * 8, 0

    def bank(self, name):
        b = self.at % 8
        self.at += 1
        self.jobs[name] = [b, self.uses[b], 0]
        self.uses[b] += 1

    def tile(self, name):
        self.bank(name)
        self.tiles += 1
        self.jobs[name][2] = self.tiles

    def unit(self, *names):
        self.units += 1
        for n in names:
            self.jobs[n][2] = self.units

    def attention(self, s, after_scores, after=None):
        for tt in range(TT):
            for h in range(HEADS):
                self.tile(f"{s}score{tt}{h}")
        after_scores()
        for h in range(HEADS):
            self.tile(f"{s}turn{h}")
        for p in range(PAIRS):
            self.tile(f"{s}out{p}")


IN1 = [f"{n}{i}" for n in ("qa", "ka", "va", "qb", "kb", "vb") for i in range(2)]
IN2 = ["qa0", "qa1", "kv", "pu0", "pu1", "qc0", "qc1", "kc0", "kc1", "vc0", "vc1"] + [f"gl{i}" for i in range(12)]


BRANCH_UNITS, OUT_UNITS = 6, D // 256
FIRST_UP = len(IN2) + BRANCH_UNITS + OUT_UNITS
SPLIT = list(range(len(IN2))) + list(range(FIRST_UP, FIRST_UP + 2 * UPAIRS))
POOL_LOW = [5, 6, 7, 8]
DVE_LOW = [u for u in SPLIT if u not in POOL_LOW]
EARLY = 7


def plan_first():
    p = Plan()
    p.tile("cond")
    p.tile("table")

    def ada(r):
        p.bank(f"ada{r}")
        for k in range(KC):
            p.unit(f"ada{r}")
        for j in range(4):
            p.tile(f"mod{4 * r + j}")

    def project(names):
        for n in names:
            p.bank(n)
            p.unit(n)

    ada(0)
    for j in range(4):
        p.tile(f"h{j}")
    p.tile("forget")
    project(IN1[:6])
    p.attention("a", lambda: project(IN1[6:]))
    p.attention("b", lambda: (ada(1), ada(2)))
    for j in range(4):
        p.bank(f"mix{j}")
    for u in range(4):
        p.unit(*[f"mix{j}" for j in range(4)])
    for j in range(4):
        p.tile(f"g{j}")
    for n in ("logits", "places", "counts", "ends", "turned", "list", "spread0", "spread1"):
        p.tile(n)
    return p


def plan_layer():
    p = Plan()

    def project(names):
        for n in names:
            p.bank(n)
            p.unit(n)

    p.tile("params")
    for j in range(4):
        p.tile(f"h{j}")
    project(IN2[0:EARLY])
    for g in range(4):
        p.tile(f"diff{g}")
    for g in range(4):
        p.tile(f"pool{g}")
    for n in ("qturn0", "qturn1", "kturn"):
        p.tile(n)
    p.attention("a", lambda: project(IN2[EARLY:11]))
    p.attention("c", lambda: project(IN2[11:]))
    for u in range(BRANCH_UNITS):
        p.bank(f"branch{u}0")
        p.bank(f"branch{u}1")
        p.unit(f"branch{u}0", f"branch{u}1")
    for j in range(4):
        p.bank(f"mix{j}")
    for u in range(4):
        p.unit(*[f"mix{j}" for j in range(4)])
    for j in range(4):
        p.tile(f"g{j}")
    for c in range(UPAIRS):
        for n in ("val", "gate"):
            p.bank(f"{n}{c}")
            p.unit(f"{n}{c}")
    for j in range(4):
        p.bank(f"down{j}")
    for u in range(FT // 2):
        p.unit(*[f"down{j}" for j in range(4)])
    return p


class Chain:

    def __init__(self, engine, semaphore):
        self.engine, self.semaphore, self.base, self.n = engine, semaphore, 0, 0

    def __call__(self, instruction):
        self.n += 1
        instruction.then_inc(self.semaphore, 1)
        self.engine.wait_ge(self.semaphore, self.base + self.n)

    def loop(self, i, per_turn):
        self.before, self.per_turn = (self.base + self.n if i is not None else 0), per_turn
        self.base, self.n = self.before + i * per_turn, 0

    def loop_end(self, turns):
        assert self.n == self.per_turn, (self.n, self.per_turn)
        self.base, self.n = self.before + turns * self.per_turn, 0


def build(nc, x_in, c_in, w_ada, b_ada, g_pre_mix, g_post_mix, w_in, b_forget, rel_bias, w_out, g_pre_ffn,
          g_post_ffn, w_router, b_router, w_gate_up, b_gate_up, w_down, b_down, norm_mix_pre, norm_mix_post,
          norm_ffn_pre, norm_ffn_post, w_in2, b_gate2, qk_q, qk_k, w_pool, pool_scale, rpb, w_branch, w_out2,
          w_up, conv_w, conv_b, w_down2, shape_table, fox_table, out, table_at):
    first, layer = plan_first(), plan_layer()
    JF, JL = first.jobs, layer.jobs
    N_UNITS, N_TILES = layer.units, layer.tiles

    with ExitStack() as ctx:
        def sb(name, width, dt=F32, parts=P):
            return ctx.enter_context(nc.sbuf_tensor(name, [parts, width], dt))

        def sem(name):
            return ctx.enter_context(nc.semaphore(name))

        with ExitStack() as over:
            def beside(name, width, dt=F32R):
                return over.enter_context(nc.sbuf_tensor(name, [P, width], dt))

            beside("layer_ring", RING_L * UNIT, F32)
            split_t, hT_lo_t = beside("split", 2 * HALVES * UNIT), beside("hT_lo", KC * T)
        ring = sb("ring", MOE_UNITS * UNIT)
        x = sb("x", TT * D)[:, :].rearrange("p (t d) -> p t d", t=TT)
        htok_t = sb("htok", TT * D)
        htok = htok_t[:, :].rearrange("p (t d) -> p t d", t=TT)
        with nc.sbuf_tensor("hT_hi", [P, KC * T], F32R) as hT_hi_t:
            pass
        hT = sb("hT", KC * T)[:, :].rearrange("p (k t) -> p k t", k=KC)
        probs_t = sb("probs", TT * HEADS * T)
        probs = probs_t[:, :].rearrange("p (t h k) -> p t h k", t=TT, h=HEADS)
        with nc.sbuf_tensor("out_halves", [P, 1024 + T], F32R) as out_r:
            pass
        mixT_t = sb("mixT", 12 * T)
        mixT = mixT_t[:, :].rearrange("p (c t) -> p c t", c=12)
        qkv = sb("qkv", 6 * 1024)
        consts = sb("consts", shape_table.shape[1])
        with nc.sbuf_tensor("bias_halves", [P, 1024 + 4 * CAP], F32R) as bias_r:
            pass
        side = sb("side", 2048)
        small = sb("small", 2040)
        lists = sb("lists", 96, I32, parts=1)
        picked = sb("picked", TT * 8, U32)

        def const(name, parts=slice(0, P)):
            a, n = table_at[name]
            return consts[parts, a:a + n]

        def scratch(at, n):
            return ring[:, RING * UNIT + at:RING * UNIT + at + n]

        used = [0]

        def little(n):
            a = used[0]
            used[0] += n
            return small[:, a:a + n]

        def by_tile(a):
            return a.rearrange("p (t e) -> p t e", t=TT)

        ident, ones = const("ident"), const("ones")
        causal, bands = by_tile(const("causal")), const("bands").rearrange("p (s g t) -> p s g t", s=TT, g=4)
        eps, meansq, root, rstd, halves = little(1), little(TT), little(TT), little(TT), little(4)
        top, negtop, total, scale = (little(TT * HEADS) for _ in range(4))
        zeros = little(T)

        def q4(a):
            return qkv[:, a:a + 1024].rearrange("p (c t) -> p c t", c=4)

        def v2(a, n=512):
            return qkv[:, a:a + TT * n].rearrange("p (t n) -> p t n", t=TT)

        proj1 = dict(qa=q4(0), ka=q4(1024), va=v2(2048), qb=q4(3072), kb=q4(4096), vb=v2(5120))
        gain_m, shift_m = probs_t[:, 0:1024], probs_t[:, 1024:2048]
        modrows = [probs_t[:, 2048:2560], htok_t[:, 0:512], htok_t[:, 512:1024]]
        tables = scratch(4096, 4096).rearrange("p (t h k) -> p t h k", t=TT, h=HEADS)
        turned = scratch(8192, 4096).rearrange("p (h c q) -> p h c q", h=HEADS, c=TT)
        gpre_m, gpost_m, gpre_f, gpost_f = (scratch(1024 * i, 1024) for i in range(4))
        gate_m, gain_f, shift_f, gate_f = gpost_m, gpre_f, gpre_m, mixT_t[:, 2048:3072]
        fox_rhs = side[0:40, :].rearrange("p (h k) -> p h k", h=HEADS)
        bada, trow, crow = side[64:76, 0:512], side[96:96 + HEADS, 0:512], side[96:96 + KC, 512:512 + P]
        pick12 = const("picks", slice(64, 76))[:, 0:12 * 32].rearrange("p (c m) -> p c m", c=12)
        buckets = const("picks", slice(0, BUCKETS + 1))
        condrep = little(KC * 32).rearrange("p (k m) -> p k m", k=KC)
        wf = little(KC * HEADS).rearrange("p (k n) -> p k n", k=KC)
        wfdup = little(KC * 40).rearrange("p (k n) -> p k n", k=KC)
        bforget, rel33 = little(1), little(HEADS)
        fcum = little(T)[0:40, :]
        fz, fa, fe, fm = (probs_t[0:40, 2560 + T * i:2560 + T * i + T] for i in range(4))

        wrt = sb("wrt", KC * EXPERTS)[:, :].rearrange("p (k e) -> p k e", k=KC)
        brt, logits = little(EXPERTS), by_tile(little(TT * EXPERTS))
        best, bestf, gate4 = (by_tile(little(TT * n)) for n in (8, 8, TOPK))
        gsum = little(TT)
        gates_te, chosen, place = (by_tile(little(TT * EXPERTS)) for _ in range(3))
        nblk, ends, starts = (little(1)[0:EXPERTS, :] for _ in range(3))
        blkpos, blkgate = (by_tile(little(TT * (BLOCKS + 1))) for _ in range(2))
        assert used[0] <= 2040, used

        at = [0]

        def moe(n, memory=qkv):
            a = at[0]
            at[0] += n
            return memory[:, a:a + n]

        xgT = moe(512).rearrange("p (b j s) -> p b j s", b=4, j=2)
        actT = moe(512).rearrange("p (b j s) -> p b j s", b=4, j=2)
        xrow, glu, lin, lin1, sig, act_row = (moe(512) for _ in range(6))
        brows = moe(512)[96:100, :]
        assert at[0] <= 6144
        at[0] = 0
        sel, sel2 = by_tile(moe(TT * CAP, probs_t)), by_tile(moe(TT * 2 * CAP, probs_t))
        bdown = moe(D, probs_t)[0:EXPERTS, :]
        slot_gate, gate_now = moe(1, probs_t), moe(TT, probs_t)
        posT, gateT = (moe(T, probs_t)[0:EXPERTS, :] for _ in range(2))
        done_e, begun_e, onehot = (moe(BLOCKS + 1, probs_t)[0:EXPERTS, :] for _ in range(3))
        equal4, equalg = (moe(TOPK * EXPERTS, probs_t).rearrange("p (k e) -> p k e", k=TOPK) for _ in range(2))
        pick4 = const("picks", slice(96, 100))[:, 0:4 * CAP]
        bias_halves = [bias_r[96:100, 512 * i:512 * i + 512] for i in range(2)]
        pick4_r = bias_r[96:100, 1024:1024 + 4 * CAP].rearrange("p (q m) -> p q m", q=2)
        y_halves = out_r[:, 0:2 * 512].rearrange("p (a n) -> p a n", a=2)
        selT = out_r[:, 1024:1024 + T]
        slots, blocks, experts = const("slots"), const("blocks"), const("experts")

        qk = qkv[:, 0:1280].rearrange("p (t n) -> p t n", t=TT)
        qTa, kTa, va2 = q4(1280), qkv[:, 2304:2816].rearrange("p (g t) -> p g t", g=A_KV), v2(2816, P)
        pu = vc = v2(3072)
        qTc, kTc = q4(4096), q4(5120)
        params = scratch(8192, 256).rearrange("p (i n) -> p i n", i=2)
        gqk = scratch(8448, 640)
        wpool = scratch(9088, 512).rearrange("p (g d) -> p g d", g=4)
        diffT = scratch(9600, 1024).rearrange("p (c t) -> p c t", c=4)
        qksq = scratch(10624, 1280).rearrange("p (t n) -> p t n", t=TT)
        rope1 = probs_t[:, 0:1280].rearrange("p (t n) -> p t n", t=TT)
        rope2 = probs_t[:, 1280:2560].rearrange("p (t n) -> p t n", t=TT)
        kdup = probs_t[:, 2560:3072].rearrange("p (t g c d) -> p t g c d", t=TT, g=A_KV, c=2)
        gpost2 = [side[:, 0:1024], side[:, 1024:2048]]
        gates = [qkv[:, 4096:6144], qkv[:, 0:2048], htok_t[:, :]]
        gates = [g.rearrange("p (c t) -> p c t", c=KC) for g in gates]
        merged = gates[0]
        gated = scratch(4096, FT * T).rearrange("p (c t) -> p c t", c=FT)
        conv = [probs_t[:, 512 * i:512 * i + 512].rearrange("p (m t) -> p m t", m=2) for i in range(4)]
        hT_hi, hT_lo = (a[:, :].rearrange("p (k t) -> p k t", k=KC) for a in (hT_hi_t, hT_lo_t))
        halves_of = [[split_t[:, (2 * i + j) * UNIT:(2 * i + j + 1) * UNIT] for j in range(2)] for i in range(HALVES)]
        columns = sb("columns", 220)
        qkms, qkr = sb("qkms", TT * (HEADS + A_KV))[:, :], sb("qkr", TT * (HEADS + A_KV))[:, :]

        def tap(first_column):
            return lambda f: columns[:, first_column + f:first_column + f + 1]

        c_conv0, c_conv1, c_conv2 = tap(0), tap(44), tap(128)
        c_gate, c_pre, c_ffn = columns[:, 88:112], columns[:, 112:120], columns[:, 120:128]
        c_bias, c_pool = columns[:, 172:216], columns[:, 216:220]

        distances = nc.dram_tensor("distances", (P, HEADS, 2 * T), F32, kind="Internal").ap()
        rpb_copies = nc.dram_tensor("rpb_copies", (LAYERS, GRID_W, HEADS * RPB_HEAD), F32, kind="Internal").ap()
        neighbours = nc.dram_tensor("neighbours", (LAYERS, P, TT, HEADS, T), F32, kind="Internal").ap()
        banks = [ctx.enter_context(nc.psum_tensor(f"bank{b}", [P, 512], F32)) for b in range(8)]

        consts_in, small_in, x_in_sem = sem("consts_in"), sem("small_in"), sem("x_in")
        cleared, cond_rows, cond_ready = sem("cleared"), sem("cond_rows"), sem("cond_ready")
        landed = [sem(f"landed{s}") for s in range(RING)]
        landed_moe = [sem(f"landed_moe{s}") for s in range(MOE_UNITS)]
        landed_l = [sem(f"landed_l{s}") for s in range(RING_L)]
        high_done, low_done, low_done_pool, hT_high = (sem(n) for n in ("high_done", "low_done", "low_done_pool", "hT_high"))
        unit_done, tile_done = sem("unit_done"), sem("tile_done")
        unit_done_l, tile_done_l = sem("unit_done_l"), sem("tile_done_l")
        bank_free = [sem(f"bank_free{b}") for b in range(8)]
        bank_free_l = [sem(f"bank_free_l{b}") for b in range(8)]
        dve_own, act_own, pool_own = sem("dve_own"), sem("act_own"), sem("pool_own")
        scores_kept, negmax_ready, exp_done, prob_ready = (sem(n) for n in ("scores_kept", "negmax_ready", "exp_done", "prob_ready"))
        squares, means, roots = sem("squares"), sem("means"), sem("roots")
        h_ready, fox_ready, scan_in, log_in = sem("h_ready"), sem("fox_ready"), sem("scan_in"), sem("log_in")
        table_out, rpb_out, table_in, x_mid = sem("table_out"), sem("rpb_out"), sem("table_in"), sem("x_mid")
        gates_in, gates_exp, route_ready, list_ready = sem("gates_in"), sem("gates_exp"), sem("route_ready"), sem("list_ready")
        scratch_dead, bias_in = sem("scratch_dead"), sem("bias_in")
        moe_used = [sem(f"moe_used{s}") for s in range(MOE_UNITS)]
        sel_ready, gathered, xrow_ready, xg_turned, xg_ready = (sem(n) for n in ("sel_ready", "gathered", "xrow_ready", "xg_turned", "xg_ready"))
        sel2_ready, sel2_turned, selT_ready = sem("sel2_ready"), sem("sel2_turned"), sem("selT_ready")
        bias_high, bias_ready, y_high = sem("bias_high"), sem("bias_ready"), sem("y_high")
        clamped, sig_ready, act_ready, act_turned, actT_ready = (sem(n) for n in ("clamped", "sig_ready", "act_ready", "act_turned", "actT_ready"))
        y_ready, moe_done = sem("y_ready"), sem("moe_done")
        layer_in, params_in, bias_l_in, bias_masked = sem("layer_in"), sem("params_in"), sem("bias_l_in"), sem("bias_masked")
        qk_means, rope_ready, branch_ready, gated_ready = sem("qk_means"), sem("rope_ready"), sem("branch_ready"), sem("gated_ready")
        conv_in, conv_ready, gelu_ready = sem("conv_in"), sem("conv_ready"), sem("gelu_ready")
        odd_scores, out_done, cond_in, bdown_in, neighbours_out = (sem(n) for n in ("odd_scores", "out_done", "cond_in", "bdown_in", "neighbours_out"))

        hidden_done, down_done = moe_used[KC - 1], moe_used[MOE_UNITS - 1]
        block = ctx.enter_context(nc.Block())

        per_layer = {id(s): n for s, n in (
            (negmax_ready, 4), (exp_done, 4), (hT_high, 8), (prob_ready, 4), (roots, 5), (squares, 2), (means, 2), (h_ready, 4),
            (x_mid, 1), (qk_means, 1), (rope_ready, 1), (branch_ready, 1), (gated_ready, 1), (conv_in, 2 * UPAIRS),
            (conv_ready, UPAIRS - 1), (gelu_ready, UPAIRS))}

        class Seen:

            def __init__(self):
                self.base, self.n = {}, {}

            def __call__(self, s):
                self.n[id(s)] = self.n.get(id(s), 0) + 1
                return self.base.get(id(s), 0) + self.n[id(s)]

            def loop(self, i):
                self.base = {k: self.n.get(k, 0) + i * per for k, per in per_layer.items()}
                self.n = {}

            def loop_end(self):
                assert all(per_layer[k] == n for k, n in self.n.items()), self.n

        def full(name):
            job = JF[name]
            return (unit_done if name in UNIT_TILES else tile_done), job[2]

        def full_l(name, l):
            job = JL[name]
            if name in UNIT_TILES_L:
                return unit_done_l, l * N_UNITS + (job[2] + RING_L)
            return tile_done_l, l * N_TILES + job[2]

        def emptied(name):
            return bank_free[JF[name][0]], JF[name][1] + 1

        def emptied_l(name, l):
            b, use, _ = JL[name]
            return bank_free_l[b], l * layer.uses[b] + (use + 2)

        UNIT_TILES = {f"ada{r}" for r in range(3)} | set(IN1) | {f"mix{j}" for j in range(4)}
        UNIT_TILES_L = set(IN2) | {f"branch{u}{i}" for u in range(6) for i in range(2)}
        UNIT_TILES_L |= {f"{n}{j}" for n in ("mix", "down") for j in range(4)}
        UNIT_TILES_L |= {f"{n}{c}" for n in ("val", "gate") for c in range(UPAIRS)}

        def unit_at(slot):
            return ring[:, slot * UNIT:(slot + 1) * UNIT]

        def landed_unit(u, l):
            return landed_l[u % RING_L], l * (16 * N_UNITS // RING_L) + 16 * (u // RING_L + 1)

        def low_half_done(u, l):
            mine, done = (POOL_LOW, low_done_pool) if u in POOL_LOW else (DVE_LOW, low_done)
            return done, l * len(mine) + (mine.index(u) + 1)

        def split_halves(u):
            return halves_of[SPLIT.index(u) % HALVES]

        def columns_unit(slot):
            return unit_at(slot).rearrange("p (k n) -> p k n", k=KC)

        def rows_unit(slot):
            return unit_at(slot).rearrange("p (k n) -> p k n", k=2)

        @block.sync
        def _(sp):
            sp.dma_start(x, x_in[0].rearrange("(t p) d -> p t d", p=P)).then_inc(x_in_sem, 16)
            w_in_v = w_in[0].rearrange("(k p) n -> p k n", p=P)
            w_out_v = w_out[0].rearrange("(k p) n -> p k n", p=P)
            sources = [w_ada[0, P * k:P * k + P, 0:UNIT] for k in range(KC)]
            sources += [w_in_v[:, :, 256 * u:256 * u + 256] for u in range(len(IN1))]
            sources += [w_ada[0, P * k:P * k + P, UNIT * r:UNIT * r + UNIT] for r in (1, 2) for k in range(KC)]
            sources += [w_out_v[:, 2 * u:2 * u + 2, :] for u in range(4)]
            for u, source in enumerate(sources):
                s = u % RING
                if u >= RING:
                    sp.wait_ge(unit_done, u - RING + 1)
                shape = unit_at(s) if len(source.shape) == 2 else unit_at(s).rearrange(
                    "p (k n) -> p k n", k=source.shape[1])
                sp.dma_start(shape, source).then_inc(landed[s], 16)

            def load_expert(e, wait):
                wgu = w_gate_up[0, bass.ds(e, 1)].rearrange("e (k p) n -> (e p) k n", p=P)
                wdn = w_down[0, bass.ds(e, 1)].rearrange("e (k p) n -> (e p) k n", p=P)
                for u in range(MOE_UNITS):
                    wait(u)
                    if u == 0:
                        sp.dma_start(brows, b_gate_up[0, bass.ds(e, 1)].rearrange("e (r n) -> (e r) n", r=4))\
                            .then_inc(bias_in, 16)
                    if u < KC:
                        sp.dma_start(unit_at(u), wgu[:, u, :]).then_inc(landed_moe[u], 16)
                    else:
                        v = u - KC
                        sp.dma_start(rows_unit(u), wdn[:, 2 * v:2 * v + 2, :]).then_inc(landed_moe[u], 16)

            def first_wait(u):
                if u == 0:
                    sp.wait_ge(unit_done, first.units)
                if u == RING:
                    sp.wait_ge(h_ready, 4)

            load_expert(0, first_wait)
            sp.wait_ge(*emptied("list"))
            with sp.Fori(1, EXPERTS) as e:
                blocks_before = sp.value_load(lists[0:1, bass.ds(BLOCKS + e, 1)], min_val=1, max_val=BLOCKS)
                load_expert(e, lambda u: sp.wait_ge(moe_used[u], blocks_before))

            with sp.Fori(0, LAYERS) as l:
                def w(a, k):
                    return a[bass.ds(l, 1)].rearrange("l (k p) n -> (l p) k n", p=P)

                in_v, out_v = w(w_in2, KC), w(w_out2, KC)
                up_v, down_v = w(w_up, KC), w(w_down2, FT)
                branch_v = w_branch[bass.ds(l, 1)].rearrange("l b (k p) n -> (l p) b k n", p=P)
                order = [in_v[:, :, 256 * u:256 * u + 256] for u in range(len(IN2))]
                order += [branch_v[:, u // 2, :, 512 * (u % 2):512 * (u % 2) + 512] for u in range(6)]
                order += [out_v[:, 2 * u:2 * u + 2, :] for u in range(4)]
                for c in range(UPAIRS):
                    order += [up_v[:, :, D_FF * half + 256 * c:D_FF * half + 256 * c + 256] for half in range(2)]
                order += [down_v[:, 2 * u:2 * u + 2, :] for u in range(FT // 2)]
                assert len(order) == N_UNITS and N_UNITS % RING_L == 0 and N_UNITS - 1 not in SPLIT
                for u, source in enumerate(order):
                    if u - RING_L in SPLIT:
                        sp.wait_ge(*low_half_done(u - RING_L, l))
                    else:
                        sp.wait_ge(unit_done_l, l * N_UNITS + (u + 1))
                    sp.dma_start(unit_at(u % RING_L).rearrange("p (k n) -> p k n", k=source.shape[1]), source)\
                        .then_inc(landed_l[u % RING_L], 16)
            sp.wait_ge(layer_in, LAYERS + 1)
            sp.dma_start(out[0].rearrange("(t p) d -> p t d", p=P), x).then_inc(out_done, 16)
            sp.wait_ge(out_done, 16)

        @block.tensor
        def _(pe):
            seen = Seen()
            state = dict(unit=0, l=None, emptied=[0] * 8)

            def bank_emptied(b, times):
                if times > state["emptied"][b]:
                    state["emptied"][b] = times
                    if state["l"] is None:
                        pe.wait_ge(bank_free[b], times)
                    else:
                        pe.wait_ge(bank_free_l[b], state["l"] * layer.uses[b] + (times + 1))

            def take(name):
                b, use, _ = (JF if state["l"] is None else JL)[name]
                bank_emptied(b, use)
                return banks[b]

            def read(*names):
                jobs, last = JF if state["l"] is None else JL, {}
                for n in names:
                    b, use, _ = jobs[n]
                    last[b] = max(use + 1, last.get(b, 0))
                for b, times in last.items():
                    bank_emptied(b, times)

            def tile(last):
                last.then_inc(tile_done if state["l"] is None else tile_done_l, 1)

            def next_unit():
                u = state["unit"]
                state["unit"] += 1
                if state["l"] is None:
                    pe.wait_ge(landed[u % RING], 16 * (u // RING + 1))
                    return u % RING
                pe.wait_ge(*landed_unit(u, state["l"]))
                return u % RING_L

            def used(last):
                last.then_inc(unit_done if state["l"] is None else unit_done_l, 1)

            def turn_h(names, src):
                for j, n in enumerate(names):
                    b = take(n)
                    for kk in range(2):
                        for tt in range(TT):
                            c = (2 * j + kk) * P
                            last = pe.transpose(b[:, kk * T + tt * P:kk * T + tt * P + P], src[:, tt, c:c + P], ident)
                    tile(last)

            def next_halves():
                u = state["unit"]
                state["unit"] += 1
                pe.wait_ge(*low_half_done(u, state["l"]))
                return [a.rearrange("p (k n) -> p k n", k=KC) for a in split_halves(u)]

            def split_product(out, a, b, start, stop):
                for i, (a_half, b_half) in enumerate(((0, 0), (1, 0), (0, 1))):
                    last = pe.matmul(out, a[a_half], b[b_half], start=start and i == 0, stop=stop and i == 2)
                return last

            def split_project_T(name):
                b, w_halves = take(name), next_halves()
                for i in range(2):
                    for k in range(KC):
                        last = split_product(b[:, i * T:i * T + T], [a[:, k, i * P:i * P + P] for a in w_halves],
                                             [a[:, k, :] for a in (hT_hi, hT_lo)], k == 0, k == KC - 1)
                used(last)

            def split_project(name):
                b, w_halves = take(name), next_halves()
                for tt in range(TT):
                    for k in range(KC):
                        last = split_product(b[:, tt * 256:tt * 256 + 256],
                                             [a[:, k, tt * P:tt * P + P] for a in (hT_hi, hT_lo)],
                                             [a[:, k, :] for a in w_halves], k == 0, k == KC - 1)
                used(last)

            def project_T(name):
                b, s = take(name), next_unit()
                for i in range(2):
                    for k in range(KC):
                        last = pe.matmul(b[:, i * T:i * T + T], columns_unit(s)[:, k, i * P:i * P + P], hT[:, k, :],
                                         start=(k == 0), stop=(k == KC - 1))
                used(last)

            def project(name):
                b, s = take(name), next_unit()
                for tt in range(TT):
                    for k in range(KC):
                        last = pe.matmul(b[:, tt * 256:tt * 256 + 256], hT[:, k, tt * P:tt * P + P],
                                         columns_unit(s)[:, k, :], start=(k == 0), stop=(k == KC - 1))
                used(last)

            def rows_product(names, lhsT, chunks):
                bs = [take(n) for n in names]
                for u in range(chunks // 2):
                    s = next_unit()
                    for c in range(2):
                        kc = 2 * u + c
                        for j in range(4):
                            tt, half = j // 2, j % 2
                            last = pe.matmul(bs[j][:, :], lhsT[:, kc, tt * P:tt * P + P],
                                             rows_unit(s)[:, c, half * 512:half * 512 + 512],
                                             start=(kc == 0), stop=(kc == chunks - 1))
                    used(last)

            def scores(s, qT, key, extra=None):
                for tt in range(TT):
                    for h in range(HEADS):
                        b, o = take(f"{s}score{tt}{h}"), DH * (h % 2)
                        last = pe.matmul(b[:, 0:T], qT[o:o + DH, h // 2, tt * P:tt * P + P], key(h, o), start=True,
                                         stop=extra is None)
                        if extra is not None:
                            if o:
                                last.then_inc(odd_scores, 1)
                                pe.wait_ge(odd_scores, tt * PAIRS + h // 2 + 1)
                            last = extra(b, tt, h)
                        tile(last)

            def values(s, value):
                for tt in range(TT):
                    pe.wait_ge(prob_ready, seen(prob_ready))
                for h in range(HEADS):
                    b = take(f"{s}turn{h}")
                    for c in range(TT):
                        for tt in range(TT):
                            last = pe.transpose(b[:, c * T + tt * P:c * T + tt * P + P],
                                                probs[:, tt, h, c * P:c * P + P], ident)
                    tile(last)
                for p in range(PAIRS):
                    b = take(f"{s}out{p}")
                    for h in (2 * p, 2 * p + 1):
                        read(f"{s}turn{h}")
                        o = DH * (h % 2)
                        for c in range(TT):
                            last = pe.matmul(b[o:o + DH, 0:T], value(h, c), turned[:, h, c, :], start=(c == 0),
                                             stop=(c == TT - 1))
                    tile(last)

            pe.wait_ge(consts_in, 16)
            pe.wait_ge(cond_rows, 1)
            tile(pe.transpose(take("cond")[:, 0:KC], crow, const("ident", slice(96, 96 + KC))[:, 96:96 + KC]))
            pe.wait_ge(small_in, SMALL_IN)
            pe.wait_ge(cleared, 1)
            tile(pe.matmul(take("table")[0:HEADS, :], rel33[0:BUCKETS + 1, :], buckets, start=True, stop=True))

            def ada(r):
                b = take(f"ada{r}")
                for j in range(4):
                    pe.matmul(b[32 * j:32 * j + 32, :], pick12[:, 4 * r + j, :], bada, start=True, stop=False)
                for k in range(KC):
                    s = next_unit()
                    for j in range(4):
                        last = pe.matmul(b[32 * j:32 * j + 32, :], condrep[:, k, :],
                                         unit_at(s)[:, 512 * j:512 * j + 512], start=False, stop=(k == KC - 1))
                    used(last)
                read(f"ada{r}")
                for j in range(4):
                    tile(pe.matmul(take(f"mod{4 * r + j}")[:, :], ones[32 * j:32 * j + 1, :],
                                   modrows[r][32 * j:32 * j + 1, :], start=True, stop=True))

            read("cond")
            ada(0)
            for tt in range(TT):
                pe.wait_ge(h_ready, seen(h_ready))
            turn_h([f"h{j}" for j in range(4)], htok)
            read(*[f"h{j}" for j in range(4)])
            b = take("forget")
            for k in range(KC):
                last = pe.matmul(b[0:40, 0:T], wfdup[:, k, :], hT[:, k, :], start=(k == 0), stop=(k == KC - 1))
            tile(last)

            def project_set(names):
                for n in names:
                    (project if n[0] == "v" else project_T)(n)

            project_set(IN1[0:6])
            read(*IN1[0:6])
            pe.wait_ge(fox_ready, 1)

            def fox_bias(b, tt, h):
                return pe.matmul(b[:, 0:T], fcum[:, tt * P:tt * P + P], fox_rhs[:, h, :], start=False, stop=True)

            scores("a", proj1["qa"], lambda h, o: proj1["ka"][o:o + DH, h // 2, :], fox_bias)
            project_set(IN1[6:])
            values("a", lambda h, c: proj1["va"][:, c, h * DH:h * DH + DH])
            read(*IN1[6:])
            scores("b", proj1["qb"], lambda h, o: proj1["kb"][o:o + DH, h // 2, :])
            ada(1)
            ada(2)
            values("b", lambda h, c: proj1["vb"][:, c, h * DH:h * DH + DH])
            read(*[f"{s}out{p}" for s in "ab" for p in range(PAIRS)])
            rows_product([f"mix{j}" for j in range(4)], mixT, KC)
            for tt in range(TT):
                pe.wait_ge(h_ready, seen(h_ready))
            turn_h([f"g{j}" for j in range(4)], htok)
            read(*[f"g{j}" for j in range(4)])
            b = take("logits")
            for tt in range(TT):
                for k in range(KC):
                    last = pe.matmul(b[:, tt * EXPERTS:tt * EXPERTS + EXPERTS], hT[:, k, tt * P:tt * P + P],
                                     wrt[:, k, :], start=(k == 0), stop=(k == KC - 1))
            tile(last)
            pe.wait_ge(route_ready, 1)
            b = take("places")
            before = const("before")
            pe.matmul(b[:, 0:EXPERTS], before, chosen[:, 0, :], start=True, stop=True)
            pe.matmul(b[:, EXPERTS:2 * EXPERTS], ones, chosen[:, 0, :], start=True, stop=False)
            tile(pe.matmul(b[:, EXPERTS:2 * EXPERTS], before, chosen[:, 1, :], start=False, stop=True))
            b = take("counts")
            for tt in range(TT):
                last = pe.matmul(b[0:EXPERTS, 0:1], chosen[:, tt, :], ones[:, 0:1], start=(tt == 0), stop=(tt == 1))
            tile(last)
            pe.wait_ge(route_ready, 2)
            tile(pe.matmul(take("ends")[0:EXPERTS, 0:1], const("upto", slice(0, EXPERTS)), nblk, start=True, stop=True))
            pe.wait_ge(route_ready, 3)
            b = take("turned")
            for tt in range(TT):
                pe.transpose(b[0:EXPERTS, tt * P:tt * P + P], place[:, tt, :], ident)
            for tt in range(TT):
                last = pe.transpose(b[0:EXPERTS, T + tt * P:T + tt * P + P], gates_te[:, tt, :], ident)
            tile(last)
            pe.wait_ge(route_ready, 4)
            b = take("list")
            pe.matmul(b[0:1, 0:BLOCKS + 1], ones[0:EXPERTS, 0:1], done_e, start=True, stop=True)
            tile(pe.matmul(b[0:1, BLOCKS + 1:BLOCKS + 1 + EXPERTS], nblk, const("upto", slice(0, EXPERTS)), start=True,
                           stop=True))
            read("turned")
            for tt in range(TT):
                b = take(f"spread{tt}")
                pe.matmul(b[:, 0:BLOCKS + 1], posT[:, tt * P:tt * P + P], onehot, start=True, stop=True)
                tile(pe.matmul(b[:, 64:64 + BLOCKS + 1], gateT[:, tt * P:tt * P + P], onehot, start=True, stop=True))

            for b in range(8):
                pe.wait_ge(bank_free[b], first.uses[b])
            sums, hidden, rows_bank, turn_bank = banks[0:4], banks[4:6], banks[6], banks[7]
            for j in range(4):
                pe.matmul(sums[j][:, :], zeros[:, 0:P], consts[:, 0:512], start=True, stop=False, skip_group_check=True)

            def gather():
                for tt in range(TT):
                    for j in range(2):
                        last = pe.matmul(rows_bank[CAP * j:CAP * j + CAP, :], sel[:, tt, :],
                                         htok[:, tt, 512 * j:512 * j + 512], start=(tt == 0), stop=(tt == TT - 1))
                last.then_inc(gathered, 1)

            def turn_rows():
                for b in range(4):
                    last = pe.transpose(turn_bank[:, P * b:P * b + P], xrow[:, P * b:P * b + P], ident)
                last.then_inc(xg_turned, 1)

            def scatter(signal):
                for j in range(4):
                    tt, half = j // 2, j % 2
                    last = pe.matmul(sums[j][:, :], selT[:, tt * P:tt * P + P], y_halves[:, half, :], start=False,
                                     stop=False, skip_group_check=True)
                    if signal is not None and j < RING_L:
                        last.then_inc(signal, 1)

            pe.wait_ge(sel_ready, 1)
            gather()
            pe.wait_ge(xrow_ready, 1)
            turn_rows()
            read("list")
            n_blocks = pe.value_load(lists[0:1, BLOCKS + EXPERTS:BLOCKS + EXPERTS + 1], min_val=EXPERTS, max_val=BLOCKS)
            with pe.Fori(0, n_blocks) as i:
                e = pe.value_load(lists[0:1, bass.ds(i, 1)], min_val=0, max_val=EXPERTS - 1)
                pe.wait_ge(bias_ready, e + 1)
                for q in range(2):
                    for half in range(2):
                        pe.matmul(hidden[q][:, :], pick4_r[:, q, :], bias_halves[half], start=(half == 0), stop=False)
                pe.wait_ge(xg_ready, i + 1)
                for k in range(KC):
                    pe.wait_ge(landed_moe[k], 16 * e + 16)
                    for q in range(2):
                        for j in range(2):
                            c = q * D + j * 512
                            last = pe.matmul(hidden[q][CAP * j:CAP * j + CAP, :], xgT[:, k % 4, k // 4, :],
                                             unit_at(k)[:, c:c + 512], start=False, stop=(k == KC - 1))
                    last.then_inc(moe_used[k], 1)
                pe.wait_ge(selT_ready, i + 1)
                pe.wait_ge(y_ready, i + 1)
                scatter(None)
                pe.wait_ge(sel2_ready, i + 1)
                for tt in range(TT):
                    pe.transpose(turn_bank[:, tt * P:tt * P + P], sel2[:, tt, :], ident)
                for tt in range(TT):
                    last = pe.matmul(turn_bank[:, T:T + 1], sel2[:, tt, :], gate_now[:, tt:tt + 1], start=(tt == 0),
                                     stop=(tt == TT - 1))
                last.then_inc(sel2_turned, 1)
                pe.wait_ge(sel_ready, i + 2)
                gather()
                pe.wait_ge(act_ready, i + 1)
                pe.wait_ge(selT_ready, i + 2)
                for b in range(4):
                    last = pe.transpose(turn_bank[:, P * b:P * b + P], act_row[:, P * b:P * b + P], ident)
                last.then_inc(act_turned, 1)
                pe.wait_ge(xrow_ready, i + 2)
                pe.wait_ge(actT_ready, i + 1)
                for v in range(KC // 2):
                    if v == KC // 2 - 1:
                        turn_rows()
                    pe.wait_ge(landed_moe[KC + v], 16 * e + 16)
                    for c in range(2):
                        f = 2 * v + c
                        for half in range(2):
                            last = pe.matmul(rows_bank[CAP * half:CAP * half + CAP, :], actT[:, f % 4, f // 4, :],
                                             rows_unit(KC + v)[:, c, 512 * half:512 * half + 512], start=(f == 0),
                                             stop=(f == KC - 1))
                    last.then_inc(moe_used[KC + v], 1)
            pe.wait_ge(y_ready, n_blocks + 1)
            pe.wait_ge(selT_ready, n_blocks + 1)
            scatter(unit_done_l)
            pe.wait_ge(bdown_in, 16)
            for j in range(4):
                tt, half = j // 2, j % 2
                last = pe.matmul(sums[j][:, :], gateT[:, tt * P:tt * P + P], bdown[:, 512 * half:512 * half + 512],
                                 start=False, stop=True, skip_group_check=True)
                last.then_inc(moe_done, 1)

            with pe.Fori(0, LAYERS) as l:
                state.update(unit=0, l=l, emptied=[-1] * 8)
                seen.loop(l)
                pe.wait_ge(params_in, 16 * PARAMS_IN * (l + 1))
                b = take("params")
                pe.transpose(b[:, 0:P], params[:, 0, :], ident)
                tile(pe.transpose(b[:, P:P + 92], params[0:92, 1, :], ident[0:92, 0:92]))
                for tt in range(TT):
                    pe.wait_ge(h_ready, seen(h_ready))
                turn_h([f"h{j}" for j in range(4)], htok)
                read(*[f"h{j}" for j in range(4)])
                for n in IN2[0:EARLY]:
                    (split_project_T if n[0:2] == "qc" else split_project)(n)
                read("pu0", "pu1")
                for g in range(4):
                    b = take(f"diff{g}")
                    for st in range(TT):
                        last = pe.matmul(b[:, 0:T], pu[:, st, g * P:g * P + P], bands[:, st, g, :], start=(st == 0),
                                         stop=(st == TT - 1))
                    tile(last)
                for g in range(4):
                    b = take(f"pool{g}")
                    read(f"diff{g}")
                    tile(pe.matmul(b[:, 0:T], wpool[:, g, :], diffT[:, g, :], start=True, stop=True))
                pe.wait_ge(rope_ready, seen(rope_ready))
                for i in range(2):
                    b = take(f"qturn{i}")
                    for c in range(2):
                        for tt in range(TT):
                            a = (2 * i + c) * P
                            last = pe.transpose(b[:, c * T + tt * P:c * T + tt * P + P], qk[:, tt, a:a + P], ident)
                    tile(last)
                b = take("kturn")
                for g in range(A_KV):
                    for tt in range(TT):
                        last = pe.transpose(b[:, g * T + tt * P:g * T + tt * P + P],
                                            kdup[:, tt, g, :, :].rearrange("p c d -> p (c d)"), ident)
                tile(last)
                read("qturn0", "qturn1", "kturn")
                group = HEADS // A_KV
                scores("a", qTa, lambda h, o: kTa[o:o + DH, h // group, :])
                for n in IN2[EARLY:11]:
                    (split_project if n[0] == "v" else split_project_T)(n)
                values("a", lambda h, c: va2[:, c, (h // group) * DH:(h // group) * DH + DH])
                read(*IN2[5:11])
                scores("c", qTc, lambda h, o: kTc[o:o + DH, h // 2, :])
                for n in IN2[11:]:
                    split_project_T(n)
                values("c", lambda h, c: vc[:, c, h * DH:h * DH + DH])
                read(*[f"pool{g}" for g in range(4)], *[f"{s}out{p}" for s in "ac" for p in range(PAIRS)])
                for u in range(6):
                    bs = [take(f"branch{u}{i}") for i in range(2)]
                    wv = unit_at(next_unit()).rearrange("p (k n) -> p k n", k=4)
                    for i in range(2):
                        for c in range(2):
                            n0 = (2 * i + c) * P
                            for k in range(4):
                                last = pe.matmul(bs[i][:, c * T:c * T + T], wv[:, k, n0:n0 + P],
                                                 mixT[:, 4 * (u // 2) + k, :], start=(k == 0), stop=(k == 3))
                    used(last)
                pe.wait_ge(branch_ready, seen(branch_ready))
                rows_product([f"mix{j}" for j in range(4)], merged, KC)
                for tt in range(TT):
                    pe.wait_ge(h_ready, seen(h_ready))
                turn_h([f"g{j}" for j in range(4)], htok)
                read(*[f"g{j}" for j in range(4)])
                for c in range(UPAIRS):
                    split_project_T(f"val{c}")
                    split_project_T(f"gate{c}")
                pe.wait_ge(gated_ready, seen(gated_ready))
                rows_product([f"down{j}" for j in range(4)], gated, FT)
                seen.loop_end()

        @block.vector
        def _(dve):
            own, seen = Chain(dve, dve_own), Seen()
            state = dict(l=None)

            def await_full(name):
                dve.wait_ge(*(full(name) if state["l"] is None else full_l(name, state["l"])))

            def await_own(name):
                dve.wait_ge(*(emptied(name) if state["l"] is None else emptied_l(name, state["l"])))

            def leave(last, name):
                job, free = (JF, bank_free) if state["l"] is None else (JL, bank_free_l)
                last.then_inc(free[job[name][0]], 1)

            def bank(name):
                return banks[(JF if state["l"] is None else JL)[name][0]]

            def keep_scores(s, table):
                for tt in range(TT):
                    for h in range(HEADS):
                        n, r = f"{s}score{tt}{h}", tt * HEADS + h
                        await_full(n)
                        if state["l"] is not None:
                            dve.memset(negtop[:, r:r + 1], 0.0)
                        leave(dve.tensor_tensor_reduce(probs[:, tt, h, :], bank(n)[:, 0:T], table(tt, h), 1.0, LEAST,
                                                       ALU.add, ALU.max, top[:, r:r + 1]), n)
                    await_own(n)
                    r = slice(tt * HEADS, (tt + 1) * HEADS)
                    dve.tensor_scalar(negtop[:, r], top[:, r], -1.0, None, ALU.mult).then_inc(negmax_ready, 1)

            def normalise():
                for tt in range(TT):
                    dve.wait_ge(exp_done, seen(exp_done))
                    r = slice(tt * HEADS, (tt + 1) * HEADS)
                    own(dve.reciprocal(scale[:, r], total[:, r]))
                    for h in range(HEADS):
                        a = tt * HEADS + h
                        last = dve.tensor_scalar(probs[:, tt, h, :], probs[:, tt, h, :], scale[:, a:a + 1], None,
                                                 ALU.mult)
                    last.then_inc(prob_ready, 1)

            def row_scale():
                dve.wait_ge(roots, seen(roots))
                own(dve.reciprocal(rstd, root))

            def post_norm(names, gate, signal):
                dve.wait_ge(squares, seen(squares))
                pair = halves.rearrange("p (t a) -> p t a", t=TT)
                dve.tensor_tensor(meansq, pair[:, :, 0], pair[:, :, 1], ALU.add).then_inc(means, 1)
                row_scale()
                for j, n in enumerate(names):
                    tt, half = j // 2, j % 2
                    leave(dve.scalar_tensor_tensor(out=htok[:, tt, 512 * half:512 * half + 512], in0=bank(n)[:, :],
                                                   scalar=rstd[:, tt:tt + 1], in1=gate[:, 512 * half:512 * half + 512],
                                                   op0=ALU.mult, op1=ALU.mult), n)
                await_own(names[-1])
                dve.tensor_tensor(x, x, htok, ALU.add).then_inc(signal, 1)

            dve.memset(eps, EPS)
            dve.memset(zeros, 0.0)
            dve.memset(wfdup, 0.0)
            dve.memset(bforget, 0.0)
            dve.memset(rel33[BUCKETS:BUCKETS + 1, :], 1.0).then_inc(cleared, 1)
            await_full("cond")
            leave(dve.tensor_copy(condrep, bank("cond")[:, 0:KC].unsqueeze(2).broadcast_to([P, KC, 32])), "cond")
            dve.wait_ge(small_in, SMALL_IN)
            dve.wait_ge(cleared, 1)
            for a in (0, 32):
                dve.tensor_copy(wfdup[:, :, a:a + HEADS], wf)

            def ada(r, takes):
                await_full(f"ada{r}")
                leave(dve.tensor_copy(modrows[r], bank(f"ada{r}")[:, :]), f"ada{r}")
                for j, what in enumerate(takes):
                    n, half = f"mod{4 * r + j}", slice(512 * (j % 2), 512 * (j % 2) + 512)
                    await_full(n)
                    leave(what(bank(n)[:, :], half), n)

            def shift(to):
                return lambda row, half: dve.tensor_copy(to[:, half], row)

            def gain(to, g):
                return lambda row, half: dve.scalar_tensor_tensor(out=to[:, half], in0=row, scalar=1.0,
                                                                  in1=g[:, half], op0=ALU.add, op1=ALU.mult)

            def gate(to, g):
                return lambda row, half: dve.tensor_tensor(to[:, half], row, g[:, half], ALU.mult)

            def modulated(gain_row, shift_row):
                for tt in range(TT):
                    own(dve.scalar_tensor_tensor(out=htok[:, tt, :], in0=x[:, tt, :], scalar=rstd[:, tt:tt + 1],
                                                 in1=gain_row, op0=ALU.mult, op1=ALU.mult))
                    dve.tensor_tensor(htok[:, tt, :], htok[:, tt, :], shift_row, ALU.add).then_inc(h_ready, 1)

            row_scale()
            ada(0, 2 * [shift(shift_m)] + 2 * [gain(gain_m, gpre_m)])
            await_own("mod1")
            await_own("mod3")
            modulated(gain_m, shift_m)
            await_full("forget")
            leave(dve.tensor_scalar(fz, bank("forget")[0:40, 0:T], bforget[0:40, :], None, ALU.add), "forget")
            await_own("forget")
            dve.scalar_tensor_tensor(out=fa, in0=fz, scalar=-1.0, in1=fz, op0=ALU.mult, op1=ALU.max)\
                .then_inc(log_in, 1)
            own(dve.tensor_scalar(fm, fz, 0.0, None, ALU.min))
            dve.wait_ge(scan_in, 1)
            own(dve.tensor_tensor(fm, fm, fe, ALU.subtract))
            own(dve.tensor_tensor_scan(fcum, ones[0:40, 0:1].broadcast_to([40, T]), fm, 0.0, ALU.mult, ALU.add))
            own(dve.tensor_tensor(fox_rhs[32:40], fox_rhs[32:40], fcum[32:40].unsqueeze(1).broadcast_to([8, HEADS, T]),
                                  ALU.mult))
            dve.memset(fcum[32:40, :], 1.0).then_inc(fox_ready, 1)
            keep_scores("a", lambda tt, h: causal[:, tt, :])
            normalise()
            dve.wait_ge(table_in, 32)
            keep_scores("b", lambda tt, h: tables[:, tt, h, :])
            ada(1, 2 * [gate(gate_m, gpost_m)] + 2 * [shift(shift_f)])
            ada(2, 2 * [gain(gain_f, gpre_f)] + 2 * [gate(gate_f, gpost_f)])
            normalise()
            post_norm([f"mix{j}" for j in range(4)], gate_m, x_mid)
            dve.wait_ge(x_mid, seen(x_mid))
            row_scale()
            modulated(gain_f, shift_f)
            await_full("logits")
            leave(dve.tensor_tensor(logits, by_tile(bank("logits")[:, 0:TT * EXPERTS]),
                                    brt.unsqueeze(1).broadcast_to([P, TT, EXPERTS]), ALU.add), "logits")
            await_own("logits")
            for tt in range(TT):
                own(dve.max(best[:, tt, :], logits[:, tt, :]))
                own(dve.max_index(picked[:, 8 * tt:8 * tt + 8], best[:, tt, :], logits[:, tt, :]))
            own(dve.tensor_copy(bestf.rearrange("p t k -> p (t k)"), picked[:, :]))
            for tt in range(TT):
                last = dve.tensor_scalar(gate4[:, tt, :], best[:, tt, 0:TOPK], best[:, tt, 0:1], None, ALU.subtract)
            last.then_inc(gates_in, 1)
            for tt in range(TT):
                for k in range(TOPK):
                    last = dve.tensor_scalar(equal4[:, k, :], experts, bestf[:, tt, k:k + 1], None, ALU.is_equal)
                own(last)
                last = dve.tensor_reduce(chosen[:, tt, :], equal4.rearrange("p k e -> p e k"), AX_X, ALU.add)
                if tt < TT - 1:
                    own(last)
            last.then_inc(route_ready, 1)
            await_full("counts")
            leave(dve.tensor_copy(starts, bank("counts")[0:EXPERTS, 0:1]), "counts")
            await_own("counts")
            own(dve.tensor_scalar(nblk, starts, float(CAP), 1.0, ALU.is_gt, ALU.add))
            for p in range(2, T // CAP):
                last = dve.scalar_tensor_tensor(out=nblk, in0=starts, scalar=float(CAP * p), in1=nblk, op0=ALU.is_gt,
                                                op1=ALU.add)
                if p < T // CAP - 1:
                    own(last)
            last.then_inc(route_ready, 1)
            dve.wait_ge(gates_exp, 1)
            own(dve.reciprocal(gsum, gsum))
            for tt in range(TT):
                own(dve.tensor_scalar(gate4[:, tt, :], gate4[:, tt, :], gsum[:, tt:tt + 1], None, ALU.mult))
            for tt in range(TT):
                for k in range(TOPK):
                    last = dve.tensor_scalar(equalg[:, k, :], experts, bestf[:, tt, k:k + 1], gate4[:, tt, k:k + 1],
                                             ALU.is_equal, ALU.mult)
                own(last)
                own(dve.tensor_reduce(gates_te[:, tt, :], equalg.rearrange("p k e -> p e k"), AX_X, ALU.add))
            await_full("places")
            leave(dve.scalar_tensor_tensor(out=place, in0=by_tile(bank("places")[:, 0:TT * EXPERTS]), scalar=NOT_CHOSEN,
                                           in1=chosen, op0=ALU.add, op1=ALU.mult), "places")
            await_own("places")
            dve.tensor_scalar(place, place, -NOT_CHOSEN, None, ALU.add).then_inc(route_ready, 1)
            await_full("ends")
            leave(dve.tensor_copy(ends, bank("ends")[0:EXPERTS, 0:1]), "ends")
            await_own("ends")
            own(dve.tensor_tensor(starts, ends, nblk, ALU.subtract))
            dve.tensor_scalar(done_e, blocks[0:EXPERTS, :], ends, None, ALU.is_ge)
            own(dve.tensor_scalar(begun_e, blocks[0:EXPERTS, :], starts, None, ALU.is_ge))
            dve.tensor_tensor(onehot, begun_e, done_e, ALU.subtract).then_inc(route_ready, 1)
            own(dve.tensor_scalar(starts, starts, float(CAP), None, ALU.mult))
            await_full("turned")
            dve.tensor_scalar(posT, bank("turned")[0:EXPERTS, 0:T], starts, None, ALU.add)
            leave(dve.tensor_copy(gateT, bank("turned")[0:EXPERTS, T:2 * T]), "turned")
            await_full("list")
            leave(dve.tensor_copy(lists[0:1, 0:BLOCKS + 1 + EXPERTS], bank("list")[0:1, 0:BLOCKS + 1 + EXPERTS]), "list")
            for tt in range(TT):
                await_full(f"spread{tt}")
                dve.scalar_tensor_tensor(out=blkpos[:, tt, :], in0=blocks, scalar=-float(CAP),
                                         in1=bank(f"spread{tt}")[:, 0:BLOCKS + 1], op0=ALU.mult, op1=ALU.add)
                leave(dve.tensor_copy(blkgate[:, tt, :], bank(f"spread{tt}")[:, 64:64 + BLOCKS + 1]), f"spread{tt}")
            dve.tensor_copy(y_halves.rearrange("p a (b t) -> p (a b) t", t=T), zeros.unsqueeze(1).broadcast_to([P, 4, T]))\
                .then_inc(y_ready, 1)
            for tt in range(TT):
                await_own(f"spread{tt}")

            def select(at):
                for tt in range(TT):
                    last = dve.tensor_scalar(sel[:, tt, :], slots[:, 0:CAP], blkpos[:, tt, at], None, ALU.is_equal)
                last.then_inc(sel_ready, 1)

            select(slice(0, 1))
            await_own("list")
            n_blocks = dve.value_load(lists[0:1, BLOCKS + EXPERTS:BLOCKS + EXPERTS + 1], min_val=EXPERTS, max_val=BLOCKS)
            with dve.Fori(0, n_blocks) as i:
                own.loop(i, 2)
                for tt in range(TT):
                    dve.tensor_scalar(sel2[:, tt, :], slots, blkpos[:, tt, bass.ds(i, 1)], None, ALU.is_equal)
                dve.tensor_copy(gate_now.unsqueeze(2), blkgate[:, :, bass.ds(i, 1)]).then_inc(sel2_ready, 1)
                dve.wait_ge(gathered, i + 1)
                select(bass.ds(i + 1, 1))
                dve.wait_ge(hidden_done, i + 1)
                dve.tensor_scalar(glu, banks[4][:, :], SWIGLU_LIMIT, None, ALU.min).then_inc(clamped, 1)
                own(dve.tensor_scalar(lin, banks[5][:, :], -SWIGLU_LIMIT, SWIGLU_LIMIT, ALU.max, ALU.min))
                dve.wait_ge(clamped, i + 1)
                own(dve.scalar_tensor_tensor(out=lin1, in0=lin, scalar=1.0, in1=glu, op0=ALU.add, op1=ALU.mult))
                dve.wait_ge(sig_ready, i + 1)
                dve.tensor_tensor(act_row, lin1, sig, ALU.mult).then_inc(act_ready, 1)
                dve.wait_ge(y_high, i + 1)
                for half in range(2):
                    here, there = (slice(CAP * a, CAP * a + CAP) for a in (half, 1 - half))
                    last = dve.scalar_tensor_tensor(out=y_halves[there, half, :], in0=banks[6][here, :],
                                                    scalar=slot_gate[here, :], in1=y_halves[here, half, :].bitcast(F32),
                                                    op0=ALU.mult, op1=ALU.subtract)
                last.then_inc(y_ready, 1)
            own.loop_end(n_blocks)
            dve.wait_ge(squares, seen(squares))
            pair = halves.rearrange("p (t a) -> p t a", t=TT)
            dve.tensor_tensor(meansq, pair[:, :, 0], pair[:, :, 1], ALU.add).then_inc(means, 1)
            dve.wait_ge(roots, seen(roots))
            dve.reciprocal(rstd, root).then_inc(bank_free_l[7], 1)
            dve.wait_ge(bank_free_l[7], 1)
            quarters = [(j // 2, slice(512 * (j % 2), 512 * (j % 2) + 512)) for j in range(4)]
            for j, (tt, half) in enumerate(quarters):
                dve.scalar_tensor_tensor(out=htok[:, tt, half], in0=banks[j][:, :], scalar=rstd[:, tt:tt + 1],
                                         in1=gate_f[:, half], op0=ALU.mult, op1=ALU.mult).then_inc(bank_free_l[j], 1)
            for j, (tt, half) in enumerate(quarters):
                dve.wait_ge(bank_free_l[j], 1)
                dve.tensor_tensor(x[:, tt, half], x[:, tt, half], htok[:, tt, half], ALU.add)\
                    .then_inc(bank_free_l[4 + j] if j < 3 else layer_in, 1)

            def take_low(*units):
                for u in units:
                    dve.wait_ge(high_done, state["l"] * len(SPLIT) + (SPLIT.index(u) + 1))
                    high, low = split_halves(u)
                    dve.tensor_tensor(low, unit_at(u % RING_L), high.bitcast(F32), ALU.subtract).then_inc(low_done, 1)

            def hT_low(prefix, column):
                for j in range(4):
                    dve.wait_ge(hT_high, seen(hT_high))
                    for kk in range(2):
                        k = 2 * j + kk
                        last = dve.scalar_tensor_tensor(out=hT_lo[:, k, :], in0=bank(f"{prefix}{j}")[:, kk * T:kk * T + T],
                                                        scalar=column[:, k:k + 1], in1=hT_hi[:, k, :].bitcast(F32),
                                                        op0=ALU.mult, op1=ALU.subtract)
                    leave(last, f"{prefix}{j}")

            with dve.Fori(0, LAYERS) as l:
                state["l"] = l
                own.loop(l, DVE_LAYER)
                seen.loop(l)
                await_full("params")
                leave(dve.tensor_copy(columns[:, 0:220], bank("params")[:, 0:220]), "params")
                dve.wait_ge(layer_in, l + 1)

                def normed():
                    row_scale()
                    for tt in range(TT):
                        dve.tensor_scalar(htok[:, tt, :], x[:, tt, :], rstd[:, tt:tt + 1], None, ALU.mult)\
                            .then_inc(h_ready, 1)

                normed()
                take_low(0)
                hT_low("h", c_pre)
                take_low(1, 2, 3, 4)
                await_own("kv")
                own(dve.tensor_tensor(qksq, qk, qk, ALU.mult))
                dve.tensor_reduce(qkms, qksq.rearrange("p t (h d) -> p (t h) d", d=DH), AX_X, ALU.add)\
                    .then_inc(qk_means, 1)
                dve.wait_ge(roots, seen(roots))
                own(dve.reciprocal(qkr, qkms))
                n_heads = HEADS + A_KV
                qk_heads = qk.rearrange("p t (h d) -> p (t h) d", d=DH)
                own(dve.tensor_tensor(qk_heads, qk_heads, qkr.unsqueeze(2).broadcast_to([P, TT * n_heads, DH]), ALU.mult))
                dve.wait_ge(params_in, 16 * PARAMS_IN * (l + 1))
                own(dve.tensor_tensor(qk, qk, gqk.unsqueeze(1).broadcast_to([P, TT, n_heads * DH]), ALU.mult))
                for tt in range(TT):
                    def heads(a):
                        return a[:, tt, :].rearrange("p (h d) -> p h d", d=DH)

                    def angle(name):
                        return by_tile(const(name))[:, tt, :]

                    dve.tensor_tensor(heads(rope1), heads(qk), angle("cos").unsqueeze(1).broadcast_to([P, n_heads, DH]),
                                      ALU.mult)
                    sin = angle("sin").rearrange("p (a b d) -> p a b d", a=2, b=2)
                    q5 = heads(qk).rearrange("p h (a b d) -> p h a b d", a=2, b=2)
                    r5 = heads(rope2).rearrange("p h (a b d) -> p h a b d", a=2, b=2)
                    for b in range(2):
                        last = dve.tensor_tensor(r5[:, :, :, b, :], q5[:, :, :, 1 - b, :],
                                                 sin[:, :, b, :].unsqueeze(1).broadcast_to([P, n_heads, 2, 16]), ALU.mult)
                own(last)
                dve.tensor_tensor(qk[:, :, 0:MIX], rope1[:, :, 0:MIX], rope2[:, :, 0:MIX], ALU.add)
                for tt in range(TT):
                    for c in range(2):
                        k1, k2 = (r[:, tt, MIX:].rearrange("p (g d) -> p g d", d=DH) for r in (rope1, rope2))
                        last = dve.tensor_tensor(kdup[:, tt, :, c, :], k1, k2, ALU.add)
                last.then_inc(rope_ready, 1)
                keep_scores("a", lambda tt, h: zeros)
                normalise()
                take_low(9, 10, 11, 12)
                dve.wait_ge(bias_masked, l + 1)
                keep_scores("c", lambda tt, h: tables[:, tt, h, :])
                normalise()
                take_low(*range(13, len(IN2)))
                await_own("gl11")
                for u in range(6):
                    for i in range(2):
                        n, c = f"branch{u}{i}", 4 * (u % 2) + 2 * i
                        await_full(n)
                        part = gates[u // 2][:, c:c + 2, :]
                        leave(dve.tensor_tensor(part, bank(n)[:, :].rearrange("p (c t) -> p c t", c=2), part, ALU.mult), n)
                await_own("branch51")
                own(dve.tensor_tensor(merged, gates[0], gates[1], ALU.add))
                dve.tensor_tensor(merged, merged, gates[2], ALU.add).then_inc(branch_ready, 1)
                post_norm([f"mix{j}" for j in range(4)], gpost2[0], x_mid)
                dve.wait_ge(x_mid, seen(x_mid))
                normed()
                take_low(FIRST_UP)
                hT_low("g", c_ffn)
                take_low(FIRST_UP + 1)

                def product(c):
                    dve.wait_ge(gelu_ready, seen(gelu_ready))
                    last = dve.tensor_tensor(gated[:, 2 * c:2 * c + 2, :], conv[2 * (c % 2)], conv[2 * (c % 2) + 1], ALU.mult)
                    last.then_inc(conv_ready if c < UPAIRS - 1 else gated_ready, 1)

                for c in range(UPAIRS):
                    for half, name in enumerate(("val", "gate")):
                        n, cv = f"{name}{c}", conv[2 * (c % 2) + half]
                        up = bank(n)[:, :].rearrange("p (m t) -> p m t", m=2)
                        dve.wait_ge(conv_in, seen(conv_in))
                        for m in range(2):
                            f = FT * half + 2 * c + m
                            last = dve.scalar_tensor_tensor(out=cv[:, m, 1:T], in0=up[:, m, 0:T - 1],
                                                            scalar=c_conv0(f), in1=cv[:, m, 1:T], op0=ALU.mult, op1=ALU.add)
                        own(last)
                        for m in range(2):
                            f = FT * half + 2 * c + m
                            last = dve.scalar_tensor_tensor(out=cv[:, m, 0:T - 1], in0=up[:, m, 1:T],
                                                            scalar=c_conv2(f), in1=cv[:, m, 0:T - 1], op0=ALU.mult, op1=ALU.add)
                        leave(last, n)
                        if c < UPAIRS - 1:
                            take_low(FIRST_UP + 2 * (c + 1) + half)
                    if c:
                        product(c - 1)
                await_own(f"val{UPAIRS - 1}")
                product(UPAIRS - 1)
                post_norm([f"down{j}" for j in range(4)], gpost2[1], layer_in)
                own.loop_end(LAYERS)
                seen.loop_end()

        @block.scalar
        def _(act):
            own, seen = Chain(act, act_own), Seen()
            state = dict(l=None)

            def await_full(name):
                act.wait_ge(*(full(name) if state["l"] is None else full_l(name, state["l"])))

            def bank(name):
                return banks[(JF if state["l"] is None else JL)[name][0]]

            def leave(last, name):
                job, free = (JF, bank_free) if state["l"] is None else (JL, bank_free_l)
                last.then_inc(free[job[name][0]], 1)

            def copy(name, to, scale=1.0, width=512):
                await_full(name)
                source = bank(name)[0:to.shape[0], 0:width]
                if len(to.shape) == 3:
                    source = source.rearrange("p (a b) -> p a b", a=to.shape[1])
                leave(act.activation(to, source, ACT.Copy, scale=scale), name)

            def exps(tables=None):
                for tt in range(TT):
                    act.wait_ge(negmax_ready, seen(negmax_ready))
                    for h in range(HEADS):
                        r = slice(tt * HEADS + h, tt * HEADS + h + 1)
                        last = act.activation(probs[:, tt, h, :], probs[:, tt, h, :], ACT.Exp, bias=negtop[:, r],
                                              accum_out=total[:, r])
                    last.then_inc(exp_done, 1)

            def turn_and_out(s, chunk):
                for h in range(HEADS):
                    copy(f"{s}turn{h}", turned[:, h, :, :])
                for p in range(PAIRS):
                    copy(f"{s}out{p}", mixT[:, chunk + p, :], width=T)

            def take_root():
                act.activation(root, meansq, ACT.Sqrt, bias=eps).then_inc(roots, 1)

            def square_x():
                for tt in range(TT):
                    last = act.activation(htok[:, tt, :], x[:, tt, :], ACT.Square, scale=D ** -0.5,
                                          accum_out=meansq[:, tt:tt + 1])
                own(last)
                take_root()

            def square_banks(sources):
                for j, b in enumerate(sources):
                    last = act.activation(htok[:, j // 2, 512 * (j % 2):512 * (j % 2) + 512], b, ACT.Square,
                                          scale=D ** -0.5, accum_out=halves[:, j:j + 1])
                last.then_inc(squares, 1)
                act.wait_ge(means, seen(means))
                take_root()

            act.dma_start(crow, c_in[0].rearrange("(k p) -> k p", p=P)).then_inc(cond_in, 16)
            act.dma_start(consts[:, :], shape_table).then_inc(consts_in, 16)
            act.wait_ge(cond_in, 16)
            act.activation(crow, crow, ACT.Silu).then_inc(cond_rows, 1)
            act.wait_ge(cleared, 1)
            w_f = w_in[0].rearrange("(k p) n -> p k n", p=P)[:, :, 6 * MIX:6 * MIX + HEADS]
            loads = [(bada, b_ada[0].rearrange("(r n) -> r n", n=512)), (wf, w_f), (rel33[0:BUCKETS, :], rel_bias),
                     (bforget[0:HEADS, :], b_forget[0].rearrange("(h a) -> h a", a=1)),
                     (bforget[32:32 + HEADS, :], b_forget[0].rearrange("(h a) -> h a", a=1)),
                     (side[0:40, :], fox_table), (gpre_m, g_pre_mix[0].partition_broadcast(P)),
                     (gpost_m, g_post_mix[0].partition_broadcast(P)), (gpre_f, g_pre_ffn[0].partition_broadcast(P)),
                     (gpost_f, g_post_ffn[0].partition_broadcast(P)),
                     (wrt, w_router[0].rearrange("(k p) e -> p k e", p=P)), (brt, b_router[0].partition_broadcast(P))]
            assert 16 * len(loads) == SMALL_IN
            for to, source in loads:
                act.dma_start(to, source).then_inc(small_in, 16)
            act.wait_ge(x_in_sem, 16)
            square_x()
            copy("table", trow)
            for j in range(4):
                copy(f"h{j}", hT[:, 2 * j:2 * j + 2, :])
            act.wait_ge(log_in, 1)
            own(act.activation(fe, fa, ACT.Exp, scale=-1.0))
            act.activation(fe, fe, ACT.Ln, bias=ones[0:40, 0:1]).then_inc(scan_in, 1)

            def projections(names, views):
                for n in names:
                    i = int(n[-1])
                    to = views[n[:-1]]
                    if n[0] == "v":
                        copy(n, to[:, :, 256 * i:256 * i + 256])
                    else:
                        copy(n, to[:, 2 * i:2 * i + 2, :], scale=QK_SCALE if n[0] == "q" else 1.0)

            projections(IN1[0:6], proj1)
            exps()
            projections(IN1[6:], proj1)
            turn_and_out("a", 0)
            exps()
            turn_and_out("b", 4)
            await_full("mix3")
            square_banks([bank(f"mix{j}")[:, :] for j in range(4)])
            act.wait_ge(x_mid, seen(x_mid))
            square_x()
            for j in range(4):
                copy(f"g{j}", hT[:, 2 * j:2 * j + 2, :])
            act.wait_ge(gates_in, 1)
            for tt in range(TT):
                last = act.activation(gate4[:, tt, :], gate4[:, tt, :], ACT.Exp, accum_out=gsum[:, tt:tt + 1])
            last.then_inc(gates_exp, 1)
            act.wait_ge(*emptied("list"))
            n_blocks = act.value_load(lists[0:1, BLOCKS + EXPERTS:BLOCKS + EXPERTS + 1], min_val=EXPERTS, max_val=BLOCKS)
            act.activation(selT, zeros, ACT.Copy).then_inc(selT_ready, 1)

            def rows_out(n):
                act.wait_ge(gathered, n)
                act.activation(xrow, banks[6][:, :], ACT.Copy).then_inc(xrow_ready, 1)

            def rows_turned(n):
                act.wait_ge(xg_turned, n)
                act.activation(xgT.rearrange("p b j s -> p (b j s)"), banks[7][:, :], ACT.Copy).then_inc(xg_ready, 1)

            rows_out(1)
            rows_turned(1)
            with act.Fori(0, n_blocks) as i:
                act.wait_ge(clamped, i + 1)
                act.activation(sig, glu, ACT.Sigmoid, scale=SWIGLU_ALPHA).then_inc(sig_ready, 1)
                act.wait_ge(sel2_turned, i + 1)
                act.activation(selT, banks[7][:, 0:T], ACT.Copy)
                act.activation(slot_gate, banks[7][:, T:T + 1], ACT.Copy).then_inc(selT_ready, 1)
                rows_out(i + 2)
                act.wait_ge(act_turned, i + 1)
                act.activation(actT.rearrange("p b j s -> p (b j s)"), banks[7][:, :], ACT.Copy).then_inc(actT_ready, 1)
                rows_turned(i + 2)
                act.wait_ge(down_done, i + 1)
                for half in range(2):
                    here = slice(CAP * half, CAP * half + CAP)
                    last = act.activation(y_halves[here, half, :], banks[6][here, :], ACT.Copy, scale=slot_gate[here, :])
                last.then_inc(y_high, 1)
            act.wait_ge(moe_done, 4)
            square_banks([banks[j][:, :] for j in range(4)])

            with act.Fori(0, LAYERS) as l:
                state["l"] = l
                own.loop(l, 2)
                seen.loop(l)
                act.wait_ge(layer_in, l + 1)
                square_x()
                act.wait_ge(*emptied_l("params", l))

                def turn_h(prefix, column):
                    for j in range(4):
                        await_full(f"{prefix}{j}")
                        for kk in range(2):
                            k = 2 * j + kk
                            last = act.activation(hT_hi[:, k, :], bank(f"{prefix}{j}")[:, kk * T:kk * T + T], ACT.Copy,
                                                  scale=column[:, k:k + 1])
                        last.then_inc(hT_high, 1)

                def take_high(*units):
                    for u in units:
                        act.wait_ge(*landed_unit(u, l))
                        n = SPLIT.index(u)
                        if n >= HALVES:
                            act.wait_ge(unit_done_l, l * N_UNITS + (SPLIT[n - HALVES] + 1 + RING_L))
                        act.activation(split_halves(u)[0], unit_at(u % RING_L), ACT.Copy).then_inc(high_done, 1)

                take_high(0)
                turn_h("h", c_pre)
                take_high(1)
                for i in range(2):
                    copy(f"qa{i}", qk[:, :, 256 * i:256 * i + 256])
                    take_high(2 + i)
                await_full("kv")
                kv = bank("kv")[:, :].rearrange("p (t n) -> p t n", t=TT)
                act.activation(qk[:, :, MIX:MIX + P], kv[:, :, 0:P], ACT.Copy)
                leave(act.activation(va2, kv[:, :, P:2 * P], ACT.Copy), "kv")
                take_high(4)
                copy("pu0", pu[:, :, 0:256])
                take_high(5)
                act.wait_ge(qk_means, seen(qk_means))
                act.activation(qkms, qkms, ACT.Sqrt, scale=1.0 / DH, bias=eps).then_inc(roots, 1)
                copy("pu1", pu[:, :, 256:512])
                take_high(6)
                views = dict(qc=qTc, kc=kTc, vc=vc)
                for u in (5, 6):
                    projections([IN2[u]], views)
                    take_high(u + 2)
                for g in range(4):
                    copy(f"diff{g}", diffT[:, g, :], width=T)
                for g in range(4):
                    n = f"pool{g}"
                    await_full(n)
                    leave(act.activation(mixT[:, 4 + g, :], bank(n)[:, 0:T], ACT.Copy, scale=c_pool[:, g:g + 1]), n)
                for i in range(2):
                    copy(f"qturn{i}", qTa[:, 2 * i:2 * i + 2, :], scale=QK_SCALE)
                copy("kturn", kTa)
                exps()
                for u in range(EARLY, 11):
                    projections([IN2[u]], views)
                    take_high(u + 2)
                turn_and_out("a", 0)
                exps()
                for i in range(12):
                    n = f"gl{i}"
                    await_full(n)
                    for m in range(2):
                        f = 2 * i + m
                        last = act.activation(gates[f // KC][:, f % KC, :], bank(n)[:, m * T:m * T + T], ACT.Sigmoid,
                                              bias=c_gate[:, f:f + 1])
                    leave(last, n)
                    if i < 10:
                        take_high(13 + i)
                turn_and_out("c", 8)
                await_full("mix3")
                square_banks([bank(f"mix{j}")[:, :] for j in range(4)])
                act.wait_ge(x_mid, seen(x_mid))
                square_x()
                take_high(FIRST_UP)
                turn_h("g", c_ffn)
                take_high(FIRST_UP + 1)

                def gelu(c):
                    act.wait_ge(*emptied_l(f"gate{c}", l))
                    cv = conv[2 * (c % 2) + 1]
                    act.activation(cv, cv, ACT.Gelu_apprx_tanh).then_inc(gelu_ready, 1)

                for c in range(UPAIRS):
                    if c >= 2:
                        act.wait_ge(conv_ready, l * (UPAIRS - 1) + (c - 1))
                    for half, name in enumerate(("val", "gate")):
                        n = f"{name}{c}"
                        await_full(n)
                        for m in range(2):
                            f = FT * half + 2 * c + m
                            last = act.activation(conv[2 * (c % 2) + half][:, m, :], bank(n)[:, m * T:m * T + T],
                                                  ACT.Identity, scale=c_conv1(f), bias=c_bias[:, f:f + 1])
                        last.then_inc(conv_in, 1)
                        if c < UPAIRS - 1:
                            take_high(FIRST_UP + 2 * (c + 1) + half)
                    if c:
                        gelu(c - 1)
                gelu(UPAIRS - 1)
                await_full("down3")
                square_banks([bank(f"down{j}")[:, :] for j in range(4)])
                own.loop_end(LAYERS)
                seen.loop_end()

        @block.gpsimd
        def _(pool):
            for layer_ in range(LAYERS):
                pool.dma_start(rpb_copies[layer_], rpb[layer_].rearrange("h r c -> (h r c)").partition_broadcast(GRID_W))\
                    .then_inc(rpb_out, 16)
            pool.wait_ge(*emptied("table"))
            pool.dma_start(distances.rearrange("q h d -> h q d"), trow.unsqueeze(1).broadcast_to([HEADS, P, 2 * T]))\
                .then_inc(table_out, 16)
            pool.wait_ge(table_out, 16)
            for tt in range(TT):
                pitch = HEADS * 2 * T
                shifted = bass.AP(distances.tensor, T - 1 - P * tt, [[pitch - 1, P], [2 * T, HEADS], [1, T]])
                pool.dma_start(tables[:, tt, :, :], shifted).then_inc(table_in, 16)
            pool.wait_ge(rpb_out, 16 * LAYERS)
            pitch = HEADS * RPB_HEAD
            for layer_ in range(LAYERS):
                for r in range(GRID_H):
                    for rk in range(GRID_H):
                        start = layer_ * GRID_W * pitch + (rk - r + NA_ROWS - 1) * RPB_ROW + NA_COLS - 1
                        source = bass.AP(rpb_copies.tensor, start, [[pitch - 1, GRID_W], [RPB_HEAD, HEADS], [1, GRID_W]])
                        to = neighbours[layer_, GRID_W * (r % 2):GRID_W * (r % 2) + GRID_W, r // 2, :,
                                        GRID_W * rk:GRID_W * rk + GRID_W]
                        pool.dma_start(to, source).then_inc(neighbours_out, 16)
            pool.wait_ge(h_ready, 4)
            pool.dma_start(bdown, b_down[0]).then_inc(bdown_in, 16)
            pool.tensor_copy(bias_r[96:100, 1024:1024 + 4 * CAP], pick4)
            with pool.Fori(0, EXPERTS) as e:
                pool.wait_ge(bias_in, 16 * e + 16)
                pool.tensor_tensor(bias_halves[0].rearrange("r (a t) -> r a t", t=T), brows.rearrange("r (a t) -> r a t", t=T),
                                   zeros[96:100, :].unsqueeze(1).broadcast_to([4, 2, T]), ALU.add).then_inc(bias_high, 1)
                pool.wait_ge(bias_high, e + 1)
                pool.tensor_tensor(bias_halves[1], brows, bias_halves[0].bitcast(F32), ALU.subtract).then_inc(bias_ready, 1)
            pool.wait_ge(neighbours_out, 16 * LAYERS * GRID_H * GRID_H)
            with pool.Fori(0, LAYERS) as l:
                one = bass.ds(l, 1)
                pool.wait_ge(layer_in, l + 1)

                def over_heads(a, n):
                    return a[one].rearrange("l d -> (l d)").unsqueeze(0).broadcast_to([n, DH]).partition_broadcast(P)

                conv_rows = conv_w[one].rearrange("l c (f p) -> (l c f) p", p=P)
                loads = [(params[0:88, 0, :], conv_rows[0:88, :]), (params[0:44, 1, :], conv_rows[88:132, :]),
                         (params[88:112, 0, :], b_gate2[one].rearrange("l (f p) -> (l f) p", p=P)),
                         (params[112:120, 0, :], norm_mix_pre[one].rearrange("l (f p) -> (l f) p", p=P)),
                         (params[120:128, 0, :], norm_ffn_pre[one].rearrange("l (f p) -> (l f) p", p=P)),
                         (params[44:88, 1, :], conv_b[one].rearrange("l (f p) -> (l f) p", p=P)),
                         (params[88:92, 1, :], pool_scale[one].rearrange("l (f p) -> (l f) p", p=P)),
                         (gqk[:, 0:MIX].rearrange("p (h d) -> p h d", d=DH), over_heads(qk_q, HEADS)),
                         (gqk[:, MIX:].rearrange("p (h d) -> p h d", d=DH), over_heads(qk_k, A_KV)),
                         (wpool, w_pool[one].rearrange("l g c d -> (l c) g d")),
                         (gpost2[0], norm_mix_post[one].rearrange("l d -> (l d)").partition_broadcast(P)),
                         (gpost2[1], norm_ffn_post[one].rearrange("l d -> (l d)").partition_broadcast(P))]
                assert len(loads) == PARAMS_IN
                for to, source in loads:
                    pool.dma_start(to, source).then_inc(params_in, 16)
                pool.dma_start(tables.rearrange("p t h k -> p (t h k)"),
                               neighbours[one].rearrange("l p t h k -> (l p) (t h k)")).then_inc(bias_l_in, 16)
                pool.wait_ge(bias_l_in, 16 * (l + 1))
                groups = tables.rearrange("p t h (r c) -> p (t h r) c", c=GRID_W)
                pool.tensor_tensor(groups, groups, const("window").unsqueeze(1).broadcast_to(
                    [P, TT * HEADS * GRID_H, GRID_W]), ALU.add).then_inc(bias_masked, 1)
                for u in POOL_LOW:
                    pool.wait_ge(high_done, l * len(SPLIT) + (SPLIT.index(u) + 1))
                    high, low = split_halves(u)
                    pool.tensor_tensor(low, unit_at(u % RING_L), high.bitcast(F32), ALU.subtract).then_inc(low_done_pool, 1)


_INS = ["x", "c", "w_ada", "b_ada", "g_pre_mix", "g_post_mix", "w_in", "b_forget", "rel_bias", "w_out", "g_pre_ffn",
        "g_post_ffn", "w_router", "b_router", "w_gate_up", "b_gate_up", "w_down", "b_down", "norm_mix_pre_2",
        "norm_mix_post_2", "norm_ffn_pre_2", "norm_ffn_post_2", "w_in_2", "b_gate_2", "qk_norm_q_2", "qk_norm_k_2",
        "w_pool_2", "pool_scale_2", "rpb_2", "w_branch_2", "w_out_2", "w_up_2", "conv_w_2", "conv_b_2", "w_down_2"]


def kernel(**inputs):
    import concourse.bacc as bacc
    from concourse.bass_utils import run_bass_kernel_spmd

    nc = bacc.Bacc("TRN2", target_bir_lowering=False, num_devices=1)
    table, table_at, fox = shape_tables()
    arrays, args = {}, []
    for name in _INS:
        arrays[f"in_{name}"] = np.ascontiguousarray(inputs[name])
    arrays["shape_table"], arrays["fox_table"] = table, fox
    for name, a in arrays.items():
        args.append(nc.dram_tensor(name, a.shape, mybir.dt.from_np(a.dtype), kind="ExternalInput").ap())
    args.append(nc.dram_tensor("out_x", (1, T, D), F32, kind="ExternalOutput").ap())
    build(nc, *args, table_at)
    return run_bass_kernel_spmd(nc, [arrays], core_ids=[0]).results[0]["out_x"]
```

```python
import math

import concourse.bass as bass
import numpy as np
from concourse import mybir
from contextlib import ExitStack

F32 = mybir.dt.float32
F32R = mybir.dt.float32r
I32 = mybir.dt.int32
U32 = mybir.dt.uint32
ALU = mybir.AluOpType
ACT = mybir.ActivationFunctionType
AX_X = mybir.AxisListType.X

P = 128
T = 256
TT = T // P
D = 1024
KC = D // P
UNIT = 2048
HEADS, DH = 8, 64
PAIRS = HEADS // 2
MIX = HEADS * DH
EPS = 1e-6
MASKED = -1e30
LEAST = -3e38
QK_SCALE = DH ** -0.5

RING = 6
RING_L = 3
HALVES = 2
MOE_UNITS = 12
EXPERTS, TOPK = 32, 4
CAP = 64
BLOCKS = EXPERTS + T * TOPK // (CAP + 1)
SWIGLU_LIMIT, SWIGLU_ALPHA = 7.0, 1.702
BUCKETS, MAX_DISTANCE = 32, 128
NOT_CHOSEN = 1000.0

LAYERS = 2
A_KV = 2
GRID_W, GRID_H = 64, T // 64
NA_ROWS, NA_COLS = 8, 16
RPB_ROW = 2 * NA_COLS - 1
RPB_HEAD = (2 * NA_ROWS - 1) * RPB_ROW
WINDOWS = (2, 4, 8, 16)
D_FF = 2816
FT = D_FF // P
UPAIRS = D_FF // 256

SMALL_IN = 16 * 11
COLUMNS = 220
COLUMNS_IN = 7
PARAMS_IN = 5
DVE_LAYER = 38


def shape_tables():
    parts = {}
    parts["ident"] = np.eye(P)
    parts["ones"] = np.ones((P, P))
    parts["picks"] = np.zeros((P, 2 * T))
    q, k = np.arange(T)[:, None], np.arange(T)[None, :]
    causal = np.where(k <= q, 0.0, MASKED)
    parts["causal"] = np.concatenate([causal[:P], causal[P:]], 1)
    col = np.arange(P) % GRID_W
    first = np.clip(col - NA_COLS // 2, 0, GRID_W - NA_COLS)
    key = np.arange(GRID_W)[None, :]
    inside = (key >= first[:, None]) & (key < first[:, None] + NA_COLS)
    parts["window"] = np.where(inside, 0.0, MASKED)
    t = np.arange(T)
    bands = []
    for st in range(TT):
        for w in WINDOWS:
            lo, hi = np.clip(t - w // 2, 0, T), np.clip(t + w - w // 2, 0, T)
            s = (st * P + np.arange(P))[:, None]
            mean = np.where((s >= lo) & (s < hi), np.float32(1.0) / (hi - lo).astype(np.float32), 0.0)
            bands.append(mean - (s == t))
    parts["bands"] = np.concatenate(bands, 1)
    freqs = np.float32(10000.0) ** (-np.arange(0, 32, 2, dtype=np.float32) / np.float32(32))
    cos, sin = [], []
    for st in range(TT):
        tok = st * P + np.arange(P)
        for pos in (tok // GRID_W, tok % GRID_W):
            ang = pos.astype(np.float32)[:, None] * freqs[None, :]
            cos += [np.cos(ang), np.cos(ang)]
            sin += [-np.sin(ang), np.sin(ang)]
    parts["cos"], parts["sin"] = np.concatenate(cos, 1), np.concatenate(sin, 1)
    parts["before"] = (np.arange(P)[:, None] < np.arange(P)[None, :])
    parts["upto"] = (np.arange(P)[:, None] <= np.arange(EXPERTS)[None, :])
    parts["slots"] = np.tile(np.arange(CAP), (P, 2))
    parts["blocks"] = np.tile(np.arange(BLOCKS + 1), (P, 1))
    parts["experts"] = np.tile(np.arange(EXPERTS), (P, 1))
    d = T - 1 - np.arange(2 * T)
    exact = BUCKETS // 2
    far = np.maximum(d, 1).astype(np.float32)
    large = exact + (np.log(far / np.float32(exact)) / np.float32(math.log(MAX_DISTANCE / exact))
                     * np.float32(BUCKETS - exact)).astype(np.int32)
    bucket = np.where(d < exact, d, np.minimum(large, BUCKETS - 1))
    onehot = np.zeros((P, 2 * T))
    onehot[:BUCKETS] = (bucket[None, :] == np.arange(BUCKETS)[:, None]) & (d >= 0)
    onehot[BUCKETS] = np.where(d >= 0, 0.0, MASKED)
    onehot[64:76, :12 * 32] = np.arange(12)[:, None] == np.repeat(np.arange(12), 32)[None, :]
    onehot[96:100, :4 * CAP] = np.arange(4)[:, None] == np.repeat(np.arange(4), CAP)[None, :]
    parts["picks"] = onehot
    at, offset = {}, 0
    for name, a in parts.items():
        at[name] = (offset, a.shape[1])
        offset += a.shape[1]
    table = np.concatenate([np.asarray(a, np.float32) for a in parts.values()], 1)
    fox = np.zeros((40, HEADS, T), np.float32)
    for h in range(HEADS):
        fox[h, h], fox[32 + h, h] = 1.0, -1.0
    return np.ascontiguousarray(table), at, fox.reshape(40, HEADS * T)


class Plan:

    def __init__(self):
        self.tiles, self.units, self.jobs, self.uses, self.at = 0, 0, {}, [0] * 8, 0

    def bank(self, name):
        b = self.at % 8
        self.at += 1
        self.jobs[name] = [b, self.uses[b], 0]
        self.uses[b] += 1

    def tile(self, name):
        self.bank(name)
        self.tiles += 1
        self.jobs[name][2] = self.tiles

    def unit(self, *names):
        self.units += 1
        for n in names:
            self.jobs[n][2] = self.units

    def attention(self, s, after_scores, after=None):
        for tt in range(TT):
            for h in range(HEADS):
                self.tile(f"{s}score{tt}{h}")
        after_scores()
        for h in range(HEADS):
            self.tile(f"{s}turn{h}")
        for p in range(PAIRS):
            self.tile(f"{s}out{p}")


IN1 = [f"{n}{i}" for n in ("qa", "ka", "va", "qb", "kb", "vb") for i in range(2)]
IN2 = ["qa0", "qa1", "kv", "pu0", "pu1", "qc0", "qc1", "kc0", "kc1", "vc0", "vc1"] + [f"gl{i}" for i in range(12)]


BRANCH_UNITS, OUT_UNITS = 6, D // 256
FIRST_OUT = len(IN2) + BRANCH_UNITS
FIRST_UP = FIRST_OUT + OUT_UNITS
FIRST_DOWN = FIRST_UP + 2 * UPAIRS
SPLIT = list(range(len(IN2))) + list(range(FIRST_OUT, FIRST_DOWN + FT // 2))
POOL_LOW = [5, 6, 7, 8]
FIRST_OUT_1 = 2 * KC + len(IN1) + KC // 2
SPLIT_1 = list(range(KC, KC + len(IN1))) + list(range(FIRST_OUT_1, FIRST_OUT_1 + OUT_UNITS))
DVE_LOW = [u for u in SPLIT if u not in POOL_LOW]
EARLY = 7


def plan_first():
    p = Plan()
    p.tile("cond")

    def ada_units(r, n):
        p.bank(f"ada{r}")
        for k in range(n):
            p.unit(f"ada{r}")

    def ada_rows(r):
        for j in range(4):
            p.tile(f"mod{4 * r + j}")

    def ada(r):
        ada_units(r, KC)
        ada_rows(r)

    def project(names):
        for n in names:
            p.bank(n)
            p.unit(n)

    ada(0)
    for l in range(LAYERS):
        p.tile(f"columns{l}")
    for j in range(4):
        p.tile(f"h{j}")
    project(IN1[:2])
    p.tile("table")
    p.tile("forget")
    project(IN1[2:6])
    p.attention("a", lambda: project(IN1[6:]))
    p.attention("b", lambda: ada(1))
    ada_units(2, KC // 2)
    for j in range(4):
        p.bank(f"mix{j}")
    for u in range(4):
        p.unit(*[f"mix{j}" for j in range(4)])
    for k in range(KC // 2):
        p.unit("ada2")
    ada_rows(2)
    for j in range(4):
        p.tile(f"g{j}")
    for n in ("logits", "places", "counts", "ends", "turned", "list", "spread0", "spread1"):
        p.tile(n)
    return p


def plan_layer():
    p = Plan()

    def project(names):
        for n in names:
            p.bank(n)
            p.unit(n)

    for j in range(4):
        p.tile(f"h{j}")
    project(IN2[0:EARLY])
    for g in range(4):
        p.tile(f"diff{g}")
    for g in range(4):
        p.tile(f"pool{g}")
    for n in ("qturn0", "qturn1", "kturn"):
        p.tile(n)
    p.attention("a", lambda: project(IN2[EARLY:11]))
    p.attention("c", lambda: project(IN2[11:]))
    for u in range(BRANCH_UNITS):
        p.bank(f"branch{u}0")
        p.bank(f"branch{u}1")
        p.unit(f"branch{u}0", f"branch{u}1")
    for j in range(4):
        p.bank(f"mix{j}")
    for u in range(4):
        p.unit(*[f"mix{j}" for j in range(4)])
    for j in range(4):
        p.tile(f"g{j}")
    for c in range(UPAIRS):
        for n in ("val", "gate"):
            p.bank(f"{n}{c}")
            p.unit(f"{n}{c}")
    for j in range(4):
        p.bank(f"down{j}")
    for u in range(FT // 2):
        p.unit(*[f"down{j}" for j in range(4)])
    return p


class Chain:

    def __init__(self, engine, semaphore):
        self.engine, self.semaphore, self.base, self.n = engine, semaphore, 0, 0

    def __call__(self, instruction):
        self.n += 1
        instruction.then_inc(self.semaphore, 1)
        self.engine.wait_ge(self.semaphore, self.base + self.n)

    def loop(self, i, per_turn):
        self.before, self.per_turn = (self.base + self.n if i is not None else 0), per_turn
        self.base, self.n = self.before + i * per_turn, 0

    def loop_end(self, turns):
        assert self.n == self.per_turn, (self.n, self.per_turn)
        self.base, self.n = self.before + turns * self.per_turn, 0


def build(nc, x_in, c_in, w_ada, b_ada, g_pre_mix, g_post_mix, w_in, b_forget, rel_bias, w_out, g_pre_ffn,
          g_post_ffn, w_router, b_router, w_gate_up, b_gate_up, w_down, b_down, norm_mix_pre, norm_mix_post,
          norm_ffn_pre, norm_ffn_post, w_in2, b_gate2, qk_q, qk_k, w_pool, pool_scale, rpb, w_branch, w_out2,
          w_up, conv_w, conv_b, w_down2, shape_table, fox_table, out, table_at):
    first, layer = plan_first(), plan_layer()
    JF, JL = first.jobs, layer.jobs
    N_UNITS, N_TILES = layer.units, layer.tiles

    with ExitStack() as ctx:
        def sb(name, width, dt=F32, parts=P):
            return ctx.enter_context(nc.sbuf_tensor(name, [parts, width], dt))

        def sem(name):
            return ctx.enter_context(nc.semaphore(name))

        with ExitStack() as over:
            def beside(name, width, dt=F32R):
                return over.enter_context(nc.sbuf_tensor(name, [P, width], dt))

            beside("layer_ring", RING_L * UNIT, F32)
            split_t, hT_lo_t = beside("split", 2 * HALVES * UNIT), beside("hT_lo", KC * T)
            gated_hi_t, gated_lo_t = beside("gated_hi", FT * T), beside("gated_lo", (FT - 12) * T)
        with nc.sbuf_tensor("ring_low", [P, MOE_UNITS * UNIT], F32R) as ring_r:
            pass
        ring = sb("ring", MOE_UNITS * UNIT)
        x = sb("x", TT * D)[:, :].rearrange("p (t d) -> p t d", t=TT)
        with nc.sbuf_tensor("htok_low", [P, TT * D], F32R) as htok_r:
            pass
        htok_t = sb("htok", TT * D)
        htok = htok_t[:, :].rearrange("p (t d) -> p t d", t=TT)
        with nc.sbuf_tensor("hT_hi", [P, KC * T], F32R) as hT_hi_t:
            pass
        hT = sb("hT", KC * T)[:, :].rearrange("p (k t) -> p k t", k=KC)
        probs_t = sb("probs", TT * HEADS * T)
        probs = probs_t[:, :].rearrange("p (t h k) -> p t h k", t=TT, h=HEADS)
        with nc.sbuf_tensor("out_halves", [P, 1024 + T], F32R) as out_r:
            pass
        with nc.sbuf_tensor("gated_lo_rest", [P, 12 * T], F32R) as gated_lo_rest_t:
            pass
        mixT_t = sb("mixT", 12 * T)
        mixT = mixT_t[:, :].rearrange("p (c t) -> p c t", c=12)
        qkv = sb("qkv", 6 * 1024)
        consts = sb("consts", shape_table.shape[1])
        with nc.sbuf_tensor("bias_halves", [P, 1024 + 4 * CAP], F32R) as bias_r:
            pass
        side = sb("side", 2048)
        small = sb("small", 2040)
        lists = sb("lists", 96, I32, parts=1)
        picked = sb("picked", TT * 8, U32)

        def const(name, parts=slice(0, P)):
            a, n = table_at[name]
            return consts[parts, a:a + n]

        def scratch(at, n):
            return ring[:, RING * UNIT + at:RING * UNIT + at + n]

        used = [0]

        def little(n):
            a = used[0]
            used[0] += n
            return small[:, a:a + n]

        def by_tile(a):
            return a.rearrange("p (t e) -> p t e", t=TT)

        ident, ones = const("ident"), const("ones")
        causal, bands = by_tile(const("causal")), const("bands").rearrange("p (s g t) -> p s g t", s=TT, g=4)
        eps, meansq, root, rstd, halves = little(1), little(TT), little(TT), little(TT), little(4)
        top, negtop, total, scale = (little(TT * HEADS) for _ in range(4))
        zeros, spare = little(T), little(1)

        def q4(a):
            return qkv[:, a:a + 1024].rearrange("p (c t) -> p c t", c=4)

        def v2(a, n=512):
            return qkv[:, a:a + TT * n].rearrange("p (t n) -> p t n", t=TT)

        proj1 = dict(qa=q4(0), ka=q4(1024), va=v2(2048), qb=q4(3072), kb=q4(4096), vb=v2(5120))
        gain_m, shift_m = probs_t[:, 0:1024], probs_t[:, 1024:2048]
        modrows = [probs_t[:, 2048:2560], htok_t[:, 0:512], qkv[:, 0:512]]
        tables = scratch(4096, 4096).rearrange("p (t h k) -> p t h k", t=TT, h=HEADS)
        turned = scratch(8192, 4096).rearrange("p (h c q) -> p h c q", h=HEADS, c=TT)
        gpre_m, gpost_m, gpre_f, gpost_f = (scratch(1024 * i, 1024) for i in range(4))
        gate_m, gain_f, shift_f, gate_f = gpost_m, gpre_f, gpre_m, mixT_t[:, 2048:3072]
        hT1_hi, mix_lo = (gated_lo_rest_t[:, 0:KC * T].rearrange("p (k t) -> p k t", k=KC) for _ in range(2))
        hT1_lo = htok_r[:, :].rearrange("p (k t) -> p k t", k=KC)
        mix_hi = hT_hi_t[:, :].rearrange("p (k t) -> p k t", k=KC)
        fox_rhs = side[0:40, :].rearrange("p (h k) -> p h k", h=HEADS)
        bada, trow, crow = side[64:76, 0:512], side[96:96 + HEADS, 0:512], side[96:96 + KC, 512:512 + P]
        pick12 = const("picks", slice(64, 76))[:, 0:12 * 32].rearrange("p (c m) -> p c m", c=12)
        buckets = const("picks", slice(0, BUCKETS + 1))
        condrep = little(KC * 32).rearrange("p (k m) -> p k m", k=KC)
        wf = little(KC * HEADS).rearrange("p (k n) -> p k n", k=KC)
        wfdup = little(KC * 40).rearrange("p (k n) -> p k n", k=KC)
        bforget, rel33 = little(1), little(HEADS)
        fcum = little(T)[0:40, :]
        fz, fa, fe, fm = (probs_t[0:40, 2560 + T * i:2560 + T * i + T] for i in range(4))

        wrt = sb("wrt", KC * EXPERTS)[:, :].rearrange("p (k e) -> p k e", k=KC)
        brt, logits = little(EXPERTS), by_tile(little(TT * EXPERTS))
        best, bestf, gate4 = (by_tile(little(TT * n)) for n in (8, 8, TOPK))
        gsum = little(TT)
        gates_te, chosen, place = (by_tile(little(TT * EXPERTS)) for _ in range(3))
        nblk, ends, starts = (little(1)[0:EXPERTS, :] for _ in range(3))
        blkpos, blkgate = (by_tile(little(TT * (BLOCKS + 1))) for _ in range(2))
        assert used[0] <= 2040, used

        at = [0]

        def moe(n, memory=qkv):
            a = at[0]
            at[0] += n
            return memory[:, a:a + n]

        xgT = moe(512).rearrange("p (b j s) -> p b j s", b=4, j=2)
        actT = moe(512).rearrange("p (b j s) -> p b j s", b=4, j=2)
        xrow, glu, lin, lin1, sig, act_row = (moe(512) for _ in range(6))
        brows = moe(512)[96:100, :]
        assert at[0] <= 6144
        at[0] = 0
        sel, sel2 = by_tile(moe(TT * CAP, probs_t)), by_tile(moe(TT * 2 * CAP, probs_t))
        bdown = moe(D, probs_t)[0:EXPERTS, :]
        slot_gate, gate_now = moe(1, probs_t), moe(TT, probs_t)
        posT, gateT = (moe(T, probs_t)[0:EXPERTS, :] for _ in range(2))
        done_e, begun_e, onehot = (moe(BLOCKS + 1, probs_t)[0:EXPERTS, :] for _ in range(3))
        equal4, equalg = (moe(TOPK * EXPERTS, probs_t).rearrange("p (k e) -> p k e", k=TOPK) for _ in range(2))
        pick4 = const("picks", slice(96, 100))[:, 0:4 * CAP]
        bias_halves = [bias_r[96:100, 512 * i:512 * i + 512] for i in range(2)]
        pick4_r = bias_r[96:100, 1024:1024 + 4 * CAP].rearrange("p (q m) -> p q m", q=2)
        y_halves = out_r[:, 0:2 * 512].rearrange("p (a n) -> p a n", a=2)
        selT = out_r[:, 1024:1024 + T]
        slots, blocks, experts = const("slots"), const("blocks"), const("experts")

        qk = qkv[:, 0:1280].rearrange("p (t n) -> p t n", t=TT)
        qTa, kTa, va2 = q4(1280), qkv[:, 2304:2816].rearrange("p (g t) -> p g t", g=A_KV), v2(2816, P)
        pu = vc = v2(3072)
        qTc, kTc = q4(4096), q4(5120)
        params = mixT_t[:, 0:LAYERS * 256].rearrange("p (l i n) -> p l i n", l=LAYERS, i=2)
        gqk = scratch(8448, 640)
        wpool = scratch(9088, 512).rearrange("p (g d) -> p g d", g=4)
        diffT = scratch(9600, 1024).rearrange("p (c t) -> p c t", c=4)
        qksq = scratch(10624, 1280).rearrange("p (t n) -> p t n", t=TT)
        rope1 = probs_t[:, 0:1280].rearrange("p (t n) -> p t n", t=TT)
        rope2 = probs_t[:, 1280:2560].rearrange("p (t n) -> p t n", t=TT)
        kdup = probs_t[:, 2560:3072].rearrange("p (t g c d) -> p t g c d", t=TT, g=A_KV, c=2)
        gpost2 = [side[:, 0:1024], side[:, 1024:2048]]
        gates = [qkv[:, 4096:6144], qkv[:, 0:2048], htok_t[:, :]]
        gates = [g.rearrange("p (c t) -> p c t", c=KC) for g in gates]
        merged = gates[0]
        gated_hi, low_1, low_2 = (a[:, :].rearrange("p (c t) -> p c t", t=T) for a in (gated_hi_t, gated_lo_t, gated_lo_rest_t))

        def gated_lo(c, n=None):
            part, at_ = (low_1, c) if c < FT - 12 else (low_2, c - (FT - 12))
            return part[:, at_, :] if n is None else part[:, at_:at_ + n, :]
        conv = [probs_t[:, 512 * i:512 * i + 512].rearrange("p (m t) -> p m t", m=2) for i in range(4)]
        hT_hi, hT_lo = (a[:, :].rearrange("p (k t) -> p k t", k=KC) for a in (hT_hi_t, hT_lo_t))
        halves_of = [[split_t[:, (2 * i + j) * UNIT:(2 * i + j + 1) * UNIT] for j in range(2)] for i in range(HALVES)]
        columns, next_columns = sb("columns", COLUMNS), sb("next_columns", COLUMNS)
        qkms, qkr = sb("qkms", TT * (HEADS + A_KV))[:, :], sb("qkr", TT * (HEADS + A_KV))[:, :]

        def tap(first_column):
            return lambda f: columns[:, first_column + f:first_column + f + 1]

        c_conv0, c_conv1, c_conv2 = tap(0), tap(44), tap(128)
        c_gate, c_pre, c_ffn = columns[:, 88:112], columns[:, 112:120], columns[:, 120:128]
        c_bias, c_pool = columns[:, 172:216], columns[:, 216:220]

        distances = nc.dram_tensor("distances", (P, HEADS, 2 * T), F32, kind="Internal").ap()
        rpb_copies = nc.dram_tensor("rpb_copies", (LAYERS, GRID_W, HEADS * RPB_HEAD), F32, kind="Internal").ap()
        neighbours = nc.dram_tensor("neighbours", (LAYERS, P, TT, HEADS, T), F32, kind="Internal").ap()
        banks = [ctx.enter_context(nc.psum_tensor(f"bank{b}", [P, 512], F32)) for b in range(8)]

        consts_in, bada_in, gpre_in, small_in, x_in_sem = sem("consts_in"), sem("bada_in"), sem("gpre_in"), sem("small_in"), sem("x_in")
        columns_in, forget_in = sem("columns_in"), sem("forget_in")
        cleared, cond_rows = sem("cleared"), sem("cond_rows")
        high_first, low_first, out_high, hT_whole = (sem(n) for n in ("high_first", "low_first", "out_high", "hT_whole"))
        landed = [sem(f"landed{s}") for s in range(RING)]
        landed_moe = [sem(f"landed_moe{s}") for s in range(MOE_UNITS)]
        landed_l = [sem(f"landed_l{s}") for s in range(RING_L)]
        high_done, low_done, low_done_pool, hT_high = (sem(n) for n in ("high_done", "low_done", "low_done_pool", "hT_high"))
        unit_done, tile_done = sem("unit_done"), sem("tile_done")
        unit_done_l, tile_done_l = sem("unit_done_l"), sem("tile_done_l")
        bank_free = [sem(f"bank_free{b}") for b in range(8)]
        bank_free_l = [sem(f"bank_free_l{b}") for b in range(8)]
        dve_own, act_own, pool_own = sem("dve_own"), sem("act_own"), sem("pool_own")
        negmax_ready, exp_done, prob_ready = (sem(n) for n in ("negmax_ready", "exp_done", "prob_ready"))
        squares, means, roots = sem("squares"), sem("means"), sem("roots")
        h_ready, fox_ready, scan_in, log_in = sem("h_ready"), sem("fox_ready"), sem("scan_in"), sem("log_in")
        table_out, rpb_out, table_in, x_mid = sem("table_out"), sem("rpb_out"), sem("table_in"), sem("x_mid")
        gates_in, gates_exp, route_ready = sem("gates_in"), sem("gates_exp"), sem("route_ready")
        bias_in = sem("bias_in")
        moe_used = [sem(f"moe_used{s}") for s in range(MOE_UNITS)]
        sel_ready, gathered, xrow_ready, xg_turned, xg_ready = (sem(n) for n in ("sel_ready", "gathered", "xrow_ready", "xg_turned", "xg_ready"))
        sel2_ready, sel2_turned, selT_ready = sem("sel2_ready"), sem("sel2_turned"), sem("selT_ready")
        bias_high, bias_ready, y_high = sem("bias_high"), sem("bias_ready"), sem("y_high")
        clamped, sig_ready, act_ready, act_turned, actT_ready = (sem(n) for n in ("clamped", "sig_ready", "act_ready", "act_turned", "actT_ready"))
        y_ready, moe_done = sem("y_ready"), sem("moe_done")
        layer_in, params_in, bias_l_in, bias_masked = sem("layer_in"), sem("params_in"), sem("bias_l_in"), sem("bias_masked")
        qk_means, rope_ready, branch_ready, gated_ready = sem("qk_means"), sem("rope_ready"), sem("branch_ready"), sem("gated_ready")
        conv_in, conv_ready, gelu_ready = sem("conv_in"), sem("conv_ready"), sem("gelu_ready")
        odd_scores, out_done, cond_in, bdown_in, neighbours_out = (sem(n) for n in ("odd_scores", "out_done", "cond_in", "bdown_in", "neighbours_out"))

        hidden_done, down_done = moe_used[KC - 1], moe_used[MOE_UNITS - 1]
        block = ctx.enter_context(nc.Block())

        per_layer = {id(s): n for s, n in (
            (negmax_ready, 4), (exp_done, 4), (hT_high, 8), (prob_ready, 4), (roots, 5), (squares, 8), (means, 2), (h_ready, 4),
            (x_mid, 2), (qk_means, 1), (rope_ready, 1), (branch_ready, 2), (gated_ready, 1), (conv_in, 2 * UPAIRS),
            (conv_ready, UPAIRS - 1), (gelu_ready, UPAIRS))}

        class Seen:

            def __init__(self):
                self.base, self.n = {}, {}

            def __call__(self, s):
                self.n[id(s)] = self.n.get(id(s), 0) + 1
                return self.base.get(id(s), 0) + self.n[id(s)]

            def loop(self, i):
                self.base = {k: self.n.get(k, 0) + i * per for k, per in per_layer.items()}
                self.n = {}

            def loop_end(self):
                assert all(per_layer[k] == n for k, n in self.n.items()), self.n

        def full(name):
            job = JF[name]
            return (unit_done if name in UNIT_TILES else tile_done), job[2]

        def full_l(name, l):
            job = JL[name]
            if name in UNIT_TILES_L:
                return unit_done_l, l * N_UNITS + (job[2] + RING_L)
            return tile_done_l, l * N_TILES + job[2]

        def emptied(name):
            return bank_free[JF[name][0]], JF[name][1] + 1

        def emptied_l(name, l):
            b, use, _ = JL[name]
            return bank_free_l[b], l * layer.uses[b] + (use + 2)

        UNIT_TILES = {f"ada{r}" for r in range(3)} | set(IN1) | {f"mix{j}" for j in range(4)}
        UNIT_TILES_L = set(IN2) | {f"branch{u}{i}" for u in range(6) for i in range(2)}
        UNIT_TILES_L |= {f"{n}{j}" for n in ("mix", "down") for j in range(4)}
        UNIT_TILES_L |= {f"{n}{c}" for n in ("val", "gate") for c in range(UPAIRS)}

        def unit_at(slot):
            return ring[:, slot * UNIT:(slot + 1) * UNIT]

        def landed_unit(u, l):
            return landed_l[u % RING_L], l * (16 * N_UNITS // RING_L) + 16 * (u // RING_L + 1)

        def low_half_done(u, l):
            mine, done = (POOL_LOW, low_done_pool) if u in POOL_LOW else (DVE_LOW, low_done)
            return done, l * len(mine) + (mine.index(u) + 1)

        def split_halves(u):
            return halves_of[SPLIT.index(u) % HALVES]

        def first_landed(u):
            return landed[u % RING], 16 * (u // RING + 1)

        def first_halves(u):
            n = SPLIT_1.index(u)
            high = MOE_UNITS - HALVES + n % HALVES if n < len(IN1) else MOE_UNITS - OUT_UNITS + n - len(IN1)
            return [ring_r[:, slot * UNIT:(slot + 1) * UNIT] for slot in (high, u % RING)]

        def rows_unit(slot):
            return unit_at(slot).rearrange("p (k n) -> p k n", k=2)

        @block.sync
        def _(sp):
            w_in_v = w_in[0].rearrange("(k p) n -> p k n", p=P)
            w_out_v = w_out[0].rearrange("(k p) n -> p k n", p=P)
            sources = [w_ada[0, P * k:P * k + P, 0:UNIT] for k in range(KC)]
            sources += [w_in_v[:, :, 256 * u:256 * u + 256] for u in range(len(IN1))]
            sources += [w_ada[0, P * k:P * k + P, UNIT:2 * UNIT] for k in range(KC)]
            ada2 = [w_ada[0, P * k:P * k + P, 2 * UNIT:3 * UNIT] for k in range(KC)]
            out_sources = [w_out_v[:, 2 * u:2 * u + 2, :] for u in range(OUT_UNITS)]
            sources += ada2[:KC // 2] + out_sources + ada2[KC // 2:]
            for u, source in enumerate(sources):
                if u == 4:
                    sp.dma_start(x, x_in[0].rearrange("(t p) d -> p t d", p=P)).then_inc(x_in_sem, 16)
                s = u % RING
                if u >= RING:
                    sp.wait_ge(unit_done, u - RING + 1)
                shape = unit_at(s) if len(source.shape) == 2 else unit_at(s).rearrange(
                    "p (k n) -> p k n", k=source.shape[1])
                sp.dma_start(shape, source).then_inc(landed[s], 16)

            def load_expert(e, wait):
                wgu = w_gate_up[0, bass.ds(e, 1)].rearrange("e (k p) n -> (e p) k n", p=P)
                wdn = w_down[0, bass.ds(e, 1)].rearrange("e (k p) n -> (e p) k n", p=P)
                for u in range(MOE_UNITS):
                    wait(u)
                    if u == 0:
                        sp.dma_start(brows, b_gate_up[0, bass.ds(e, 1)].rearrange("e (r n) -> (e r) n", r=4))\
                            .then_inc(bias_in, 16)
                    if u < KC:
                        sp.dma_start(unit_at(u), wgu[:, u, :]).then_inc(landed_moe[u], 16)
                    else:
                        v = u - KC
                        sp.dma_start(rows_unit(u), wdn[:, 2 * v:2 * v + 2, :]).then_inc(landed_moe[u], 16)

            def first_wait(u):
                if u == 0:
                    sp.wait_ge(unit_done, first.units)
                if u == RING:
                    sp.wait_ge(h_ready, 4)
                    sp.wait_ge(*emptied("mod11"))

            load_expert(0, first_wait)
            sp.wait_ge(*emptied("list"))
            with sp.Fori(1, EXPERTS) as e:
                blocks_before = sp.value_load(lists[0:1, bass.ds(BLOCKS + e, 1)], min_val=1, max_val=BLOCKS)
                load_expert(e, lambda u: sp.wait_ge(moe_used[u], blocks_before))

            with sp.Fori(0, LAYERS) as l:
                def w(a, k):
                    return a[bass.ds(l, 1)].rearrange("l (k p) n -> (l p) k n", p=P)

                in_v, out_v = w(w_in2, KC), w(w_out2, KC)
                up_v, down_v = w(w_up, KC), w(w_down2, FT)
                branch_v = w_branch[bass.ds(l, 1)].rearrange("l b (k p) n -> (l p) b k n", p=P)
                order = [in_v[:, :, 256 * u:256 * u + 256] for u in range(len(IN2))]
                order += [branch_v[:, u // 2, :, 512 * (u % 2):512 * (u % 2) + 512] for u in range(6)]
                order += [out_v[:, 2 * u:2 * u + 2, :] for u in range(4)]
                for c in range(UPAIRS):
                    order += [up_v[:, :, D_FF * half + 256 * c:D_FF * half + 256 * c + 256] for half in range(2)]
                order += [down_v[:, 2 * u:2 * u + 2, :] for u in range(FT // 2)]
                assert len(order) == N_UNITS and N_UNITS % RING_L == 0
                for u, source in enumerate(order):
                    if u >= RING_L and u - RING_L in SPLIT:
                        sp.wait_ge(*low_half_done(u - RING_L, l))
                    else:
                        sp.wait_ge(unit_done_l, l * N_UNITS + (u + 1))
                    sp.dma_start(unit_at(u % RING_L).rearrange("p (k n) -> p k n", k=source.shape[1]), source)\
                        .then_inc(landed_l[u % RING_L], 16)
            sp.wait_ge(layer_in, TT * (LAYERS + 1))
            sp.dma_start(out[0].rearrange("(t p) d -> p t d", p=P), x).then_inc(out_done, 16)
            sp.wait_ge(out_done, 16)

        @block.tensor
        def _(pe):
            seen = Seen()
            state = dict(unit=0, l=None, emptied=[0] * 8)

            def bank_emptied(b, times):
                if times > state["emptied"][b]:
                    state["emptied"][b] = times
                    if state["l"] is None:
                        pe.wait_ge(bank_free[b], times)
                    else:
                        pe.wait_ge(bank_free_l[b], state["l"] * layer.uses[b] + (times + 1))

            def take(name):
                b, use, _ = (JF if state["l"] is None else JL)[name]
                bank_emptied(b, use)
                return banks[b]

            def read(*names):
                jobs, last = JF if state["l"] is None else JL, {}
                for n in names:
                    b, use, _ = jobs[n]
                    last[b] = max(use + 1, last.get(b, 0))
                for b, times in last.items():
                    bank_emptied(b, times)

            def tile(last):
                last.then_inc(tile_done if state["l"] is None else tile_done_l, 1)

            def next_unit():
                u = state["unit"]
                state["unit"] += 1
                if state["l"] is None:
                    pe.wait_ge(*first_landed(u))
                    return u % RING
                pe.wait_ge(*landed_unit(u, state["l"]))
                return u % RING_L

            def used(last):
                last.then_inc(unit_done if state["l"] is None else unit_done_l, 1)

            def turn_h(names, src):
                for j, n in enumerate(names):
                    b = take(n)
                    for kk in range(2):
                        for tt in range(TT):
                            c = (2 * j + kk) * P
                            last = pe.transpose(b[:, kk * T + tt * P:kk * T + tt * P + P], src[:, tt, c:c + P], ident)
                    tile(last)

            def next_halves(k):
                u = state["unit"]
                state["unit"] += 1
                if state["l"] is None:
                    pe.wait_ge(low_first, SPLIT_1.index(u) + 1)
                else:
                    pe.wait_ge(*low_half_done(u, state["l"]))
                return [a.rearrange("p (k n) -> p k n", k=k)
                        for a in (first_halves if state["l"] is None else split_halves)(u)]

            def hT_halves():
                return (hT1_hi, hT1_lo) if state["l"] is None else (hT_hi, hT_lo)

            def split_product(out, a, b, start, stop):
                for i, (a_half, b_half) in enumerate(((0, 0), (1, 0), (0, 1))):
                    last = pe.matmul(out, a[a_half], b[b_half], start=start and i == 0, stop=stop and i == 2)
                return last

            def split_project_T(name):
                b, w_halves = take(name), next_halves(KC)
                for i in range(2):
                    for k in range(KC):
                        last = split_product(b[:, i * T:i * T + T], [a[:, k, i * P:i * P + P] for a in w_halves],
                                             [a[:, k, :] for a in hT_halves()], k == 0, k == KC - 1)
                used(last)

            def split_project(name):
                b, w_halves = take(name), next_halves(KC)
                for tt in range(TT):
                    for k in range(KC):
                        last = split_product(b[:, tt * 256:tt * 256 + 256],
                                             [a[:, k, tt * P:tt * P + P] for a in hT_halves()],
                                             [a[:, k, :] for a in w_halves], k == 0, k == KC - 1)
                used(last)

            def split_rows_product(name, rows, chunks, await_rows):
                bs = [take(f"{name}{j}") for j in range(4)]
                for u in range(chunks // 2):
                    await_rows(u)
                    w_halves = next_halves(2)
                    for c in range(2):
                        f = 2 * u + c
                        for j, b in enumerate(bs):
                            tokens, half = slice(j // 2 * P, j // 2 * P + P), slice(j % 2 * 512, j % 2 * 512 + 512)
                            last = split_product(b[:, :], [a[:, tokens] for a in rows(f)],
                                                 [a[:, c, half] for a in w_halves], f == 0, f == chunks - 1)
                    used(last)

            def merged_in(u):
                if u % (OUT_UNITS // 2) == 0:
                    pe.wait_ge(branch_ready, seen(branch_ready))

            def gated_in(u):
                if u < UPAIRS - 1:
                    pe.wait_ge(conv_ready, state["l"] * (UPAIRS - 1) + (u + 1))
                else:
                    pe.wait_ge(gated_ready, seen(gated_ready))

            def scores(s, qT, key, extra=None):
                for tt in range(TT):
                    for h in range(HEADS):
                        b, o = take(f"{s}score{tt}{h}"), DH * (h % 2)
                        last = pe.matmul(b[:, 0:T], qT[o:o + DH, h // 2, tt * P:tt * P + P], key(h, o), start=True,
                                         stop=extra is None)
                        if extra is not None:
                            if o:
                                last.then_inc(odd_scores, 1)
                                pe.wait_ge(odd_scores, tt * PAIRS + h // 2 + 1)
                            last = extra(b, tt, h)
                        tile(last)

            def values(s, value):
                for tt in range(TT):
                    pe.wait_ge(prob_ready, seen(prob_ready))
                for h in range(HEADS):
                    b = take(f"{s}turn{h}")
                    for c in range(TT):
                        for tt in range(TT):
                            last = pe.transpose(b[:, c * T + tt * P:c * T + tt * P + P],
                                                probs[:, tt, h, c * P:c * P + P], ident)
                    tile(last)
                for p in range(PAIRS):
                    b = take(f"{s}out{p}")
                    pair = (2 * p, 2 * p + 1)
                    read(*[f"{s}turn{h}" for h in pair])
                    for c in range(TT):
                        for h in pair:
                            o = DH * (h % 2)
                            last = pe.matmul(b[o:o + DH, 0:T], value(h, c), turned[:, h, c, :], start=(c == 0),
                                             stop=(c == TT - 1))
                    tile(last)

            pe.wait_ge(consts_in, 16)
            pe.wait_ge(cond_rows, 1)
            tile(pe.transpose(take("cond")[:, 0:KC], crow, const("ident", slice(96, 96 + KC))[:, 96:96 + KC]))

            def ada_units(r, ks):
                b = banks[JF[f"ada{r}"][0]]
                if ks[0] == 0:
                    take(f"ada{r}")
                    for j in range(4):
                        pe.matmul(b[32 * j:32 * j + 32, :], pick12[:, 4 * r + j, :], bada, start=True, stop=False)
                for k in ks:
                    s = next_unit()
                    for j in range(4):
                        last = pe.matmul(b[32 * j:32 * j + 32, :], condrep[:, k, :],
                                         unit_at(s)[:, 512 * j:512 * j + 512], start=False, stop=(k == KC - 1))
                    used(last)

            def ada_rows(r):
                read(f"ada{r}")
                for j in range(4):
                    tile(pe.matmul(take(f"mod{4 * r + j}")[:, :], ones[32 * j:32 * j + 1, :],
                                   modrows[r][32 * j:32 * j + 1, :], start=True, stop=True))

            def ada(r):
                ada_units(r, range(KC))
                ada_rows(r)

            read("cond")
            pe.wait_ge(bada_in, 16)
            ada(0)
            pe.wait_ge(columns_in, 16 * LAYERS * COLUMNS_IN)
            for l in range(LAYERS):
                b = take(f"columns{l}")
                pe.transpose(b[:, 0:P], params[:, l, 0, :], ident)
                tile(pe.transpose(b[:, P:COLUMNS], params[0:COLUMNS - P, l, 1, :], ident[0:COLUMNS - P, 0:COLUMNS - P]))
            for tt in range(TT):
                pe.wait_ge(h_ready, seen(h_ready))
            turn_h([f"h{j}" for j in range(4)], htok)
            read(*[f"h{j}" for j in range(4)])
            def project_set(names):
                for n in names:
                    (split_project if n[0] == "v" else split_project_T)(n)

            project_set(IN1[0:2])
            pe.wait_ge(small_in, SMALL_IN)
            pe.wait_ge(cleared, 1)
            tile(pe.matmul(take("table")[0:HEADS, :], rel33[0:BUCKETS + 1, :], buckets, start=True, stop=True))
            pe.wait_ge(forget_in, 1)
            pe.wait_ge(hT_whole, 1)
            b = take("forget")
            for k in range(KC):
                last = pe.matmul(b[0:40, 0:T], wfdup[:, k, :], hT[:, k, :], start=(k == 0), stop=(k == KC - 1))
            tile(last)
            project_set(IN1[2:6])
            read(*IN1[0:6])
            pe.wait_ge(fox_ready, 1)

            def fox_bias(b, tt, h):
                return pe.matmul(b[:, 0:T], fcum[:, tt * P:tt * P + P], fox_rhs[:, h, :], start=False, stop=True)

            scores("a", proj1["qa"], lambda h, o: proj1["ka"][o:o + DH, h // 2, :], fox_bias)
            project_set(IN1[6:])
            values("a", lambda h, c: proj1["va"][:, c, h * DH:h * DH + DH])
            read(*IN1[6:])
            scores("b", proj1["qb"], lambda h, o: proj1["kb"][o:o + DH, h // 2, :])
            ada(1)
            values("b", lambda h, c: proj1["vb"][:, c, h * DH:h * DH + DH])
            ada_units(2, range(KC // 2))

            def mixed_in(u):
                read(*[f"{'ab'[u // 2]}out{2 * (u % 2) + i}" for i in range(2)])

            split_rows_product("mix", lambda f: (mix_hi[:, f, :], mix_lo[:, f, :]), KC, mixed_in)
            ada_units(2, range(KC // 2, KC))
            ada_rows(2)
            for tt in range(TT):
                pe.wait_ge(h_ready, seen(h_ready))
            turn_h([f"g{j}" for j in range(4)], htok)
            read(*[f"g{j}" for j in range(4)])
            b = take("logits")
            for tt in range(TT):
                for k in range(KC):
                    last = pe.matmul(b[:, tt * EXPERTS:tt * EXPERTS + EXPERTS], hT[:, k, tt * P:tt * P + P],
                                     wrt[:, k, :], start=(k == 0), stop=(k == KC - 1))
            tile(last)
            pe.wait_ge(route_ready, 1)
            b = take("places")
            before = const("before")
            pe.matmul(b[:, 0:EXPERTS], before, chosen[:, 0, :], start=True, stop=True)
            pe.matmul(b[:, EXPERTS:2 * EXPERTS], ones, chosen[:, 0, :], start=True, stop=False)
            tile(pe.matmul(b[:, EXPERTS:2 * EXPERTS], before, chosen[:, 1, :], start=False, stop=True))
            b = take("counts")
            for tt in range(TT):
                last = pe.matmul(b[0:EXPERTS, 0:1], chosen[:, tt, :], ones[:, 0:1], start=(tt == 0), stop=(tt == 1))
            tile(last)
            pe.wait_ge(route_ready, 2)
            tile(pe.matmul(take("ends")[0:EXPERTS, 0:1], const("upto", slice(0, EXPERTS)), nblk, start=True, stop=True))
            pe.wait_ge(route_ready, 3)
            b = take("turned")
            for tt in range(TT):
                pe.transpose(b[0:EXPERTS, tt * P:tt * P + P], place[:, tt, :], ident)
            for tt in range(TT):
                last = pe.transpose(b[0:EXPERTS, T + tt * P:T + tt * P + P], gates_te[:, tt, :], ident)
            tile(last)
            pe.wait_ge(route_ready, 4)
            b = take("list")
            pe.matmul(b[0:1, 0:BLOCKS + 1], ones[0:EXPERTS, 0:1], done_e, start=True, stop=True)
            tile(pe.matmul(b[0:1, BLOCKS + 1:BLOCKS + 1 + EXPERTS], nblk, const("upto", slice(0, EXPERTS)), start=True,
                           stop=True))
            read("turned")
            for tt in range(TT):
                b = take(f"spread{tt}")
                pe.matmul(b[:, 0:BLOCKS + 1], posT[:, tt * P:tt * P + P], onehot, start=True, stop=True)
                tile(pe.matmul(b[:, 64:64 + BLOCKS + 1], gateT[:, tt * P:tt * P + P], onehot, start=True, stop=True))

            for b in range(8):
                pe.wait_ge(bank_free[b], first.uses[b])
            sums, hidden, rows_bank, turn_bank = banks[0:4], banks[4:6], banks[6], banks[7]
            def start_sums(*banks_):
                for j in banks_:
                    tt, half = j // 2, j % 2
                    pe.matmul(sums[j][:, :], gateT[:, tt * P:tt * P + P], bdown[:, 512 * half:512 * half + 512], start=True,
                              stop=False, skip_group_check=True)

            def gather():
                for tt in range(TT):
                    for j in range(2):
                        last = pe.matmul(rows_bank[CAP * j:CAP * j + CAP, :], sel[:, tt, :],
                                         htok[:, tt, 512 * j:512 * j + 512], start=(tt == 0), stop=(tt == TT - 1))
                last.then_inc(gathered, 1)

            def turn_rows():
                for b in range(4):
                    last = pe.transpose(turn_bank[:, P * b:P * b + P], xrow[:, P * b:P * b + P], ident)
                last.then_inc(xg_turned, 1)

            def scatter(end):
                for j in range(4):
                    tt, half = j // 2, j % 2
                    last = pe.matmul(sums[j][:, :], selT[:, tt * P:tt * P + P], y_halves[:, half, :], start=False,
                                     stop=end, skip_group_check=True)
                    if end:
                        last.then_inc(unit_done_l if j < RING_L else moe_done, 1)

            pe.wait_ge(sel_ready, 1)
            gather()
            pe.wait_ge(bdown_in, 16)
            start_sums(0, 1)
            pe.wait_ge(xrow_ready, 1)
            turn_rows()
            start_sums(2, 3)
            read("list")
            n_blocks = pe.value_load(lists[0:1, BLOCKS + EXPERTS:BLOCKS + EXPERTS + 1], min_val=EXPERTS, max_val=BLOCKS)
            with pe.Fori(0, n_blocks) as i:
                e = pe.value_load(lists[0:1, bass.ds(i, 1)], min_val=0, max_val=EXPERTS - 1)
                pe.wait_ge(bias_ready, e + 1)
                for q in range(2):
                    for half in range(2):
                        pe.matmul(hidden[q][:, :], pick4_r[:, q, :], bias_halves[half], start=(half == 0), stop=False)
                pe.wait_ge(xg_ready, i + 1)
                for k in range(KC):
                    pe.wait_ge(landed_moe[k], 16 * e + 16)
                    for q in range(2):
                        for j in range(2):
                            c = q * D + j * 512
                            last = pe.matmul(hidden[q][CAP * j:CAP * j + CAP, :], xgT[:, k % 4, k // 4, :],
                                             unit_at(k)[:, c:c + 512], start=False, stop=(k == KC - 1))
                    last.then_inc(moe_used[k], 1)
                pe.wait_ge(selT_ready, i + 1)
                pe.wait_ge(y_ready, i + 1)
                scatter(False)
                pe.wait_ge(sel2_ready, i + 1)
                for tt in range(TT):
                    pe.transpose(turn_bank[:, tt * P:tt * P + P], sel2[:, tt, :], ident)
                for tt in range(TT):
                    last = pe.matmul(turn_bank[:, T:T + 1], sel2[:, tt, :], gate_now[:, tt:tt + 1], start=(tt == 0),
                                     stop=(tt == TT - 1))
                last.then_inc(sel2_turned, 1)
                pe.wait_ge(sel_ready, i + 2)
                gather()
                pe.wait_ge(act_ready, i + 1)
                pe.wait_ge(selT_ready, i + 2)
                for b in range(4):
                    last = pe.transpose(turn_bank[:, P * b:P * b + P], act_row[:, P * b:P * b + P], ident)
                last.then_inc(act_turned, 1)
                pe.wait_ge(xrow_ready, i + 2)
                pe.wait_ge(actT_ready, i + 1)
                for v in range(KC // 2):
                    if v == KC // 2 - 1:
                        turn_rows()
                    pe.wait_ge(landed_moe[KC + v], 16 * e + 16)
                    for c in range(2):
                        f = 2 * v + c
                        for half in range(2):
                            last = pe.matmul(rows_bank[CAP * half:CAP * half + CAP, :], actT[:, f % 4, f // 4, :],
                                             rows_unit(KC + v)[:, c, 512 * half:512 * half + 512], start=(f == 0),
                                             stop=(f == KC - 1))
                    last.then_inc(moe_used[KC + v], 1)
            pe.wait_ge(y_ready, n_blocks + 1)
            pe.wait_ge(selT_ready, n_blocks + 1)
            scatter(True)

            with pe.Fori(0, LAYERS) as l:
                state.update(unit=0, l=l, emptied=[-1] * 8)
                seen.loop(l)
                for tt in range(TT):
                    pe.wait_ge(h_ready, seen(h_ready))
                turn_h([f"h{j}" for j in range(4)], htok)
                read(*[f"h{j}" for j in range(4)])
                for n in IN2[0:EARLY]:
                    (split_project_T if n[0:2] == "qc" else split_project)(n)
                read("pu0", "pu1")
                for g in range(4):
                    b = take(f"diff{g}")
                    for st in range(TT):
                        last = pe.matmul(b[:, 0:T], pu[:, st, g * P:g * P + P], bands[:, st, g, :], start=(st == 0),
                                         stop=(st == TT - 1))
                    tile(last)
                pe.wait_ge(params_in, 16 * PARAMS_IN * (l + 1))
                for g in range(4):
                    b = take(f"pool{g}")
                    read(f"diff{g}")
                    tile(pe.matmul(b[:, 0:T], wpool[:, g, :], diffT[:, g, :], start=True, stop=True))
                pe.wait_ge(rope_ready, seen(rope_ready))
                for i in range(2):
                    b = take(f"qturn{i}")
                    for c in range(2):
                        for tt in range(TT):
                            a = (2 * i + c) * P
                            last = pe.transpose(b[:, c * T + tt * P:c * T + tt * P + P], qk[:, tt, a:a + P], ident)
                    tile(last)
                b = take("kturn")
                for g in range(A_KV):
                    for tt in range(TT):
                        last = pe.transpose(b[:, g * T + tt * P:g * T + tt * P + P],
                                            kdup[:, tt, g, :, :].rearrange("p c d -> p (c d)"), ident)
                tile(last)
                read("qturn0", "qturn1", "kturn")
                group = HEADS // A_KV
                scores("a", qTa, lambda h, o: kTa[o:o + DH, h // group, :])
                for n in IN2[EARLY:11]:
                    (split_project if n[0] == "v" else split_project_T)(n)
                values("a", lambda h, c: va2[:, c, (h // group) * DH:(h // group) * DH + DH])
                read(*IN2[5:11])
                scores("c", qTc, lambda h, o: kTc[o:o + DH, h // 2, :])
                for n in IN2[11:]:
                    split_project_T(n)
                values("c", lambda h, c: vc[:, c, h * DH:h * DH + DH])
                read(*[f"pool{g}" for g in range(4)], *[f"{s}out{p}" for s in "ac" for p in range(PAIRS)])
                for u in range(6):
                    bs = [take(f"branch{u}{i}") for i in range(2)]
                    wv = unit_at(next_unit()).rearrange("p (k n) -> p k n", k=4)
                    for i in range(2):
                        for c in range(2):
                            n0 = (2 * i + c) * P
                            for k in range(4):
                                last = pe.matmul(bs[i][:, c * T:c * T + T], wv[:, k, n0:n0 + P],
                                                 mixT[:, 4 * (u // 2) + k, :], start=(k == 0), stop=(k == 3))
                    used(last)
                split_rows_product("mix", lambda f: (hT_hi[:, f, :], hT_lo[:, f, :]), KC, merged_in)
                for tt in range(TT):
                    pe.wait_ge(h_ready, seen(h_ready))
                turn_h([f"g{j}" for j in range(4)], htok)
                read(*[f"g{j}" for j in range(4)])
                for c in range(UPAIRS):
                    split_project_T(f"val{c}")
                    split_project_T(f"gate{c}")
                split_rows_product("down", lambda f: (gated_hi[:, f, :], gated_lo(f)), FT, gated_in)
                seen.loop_end()

        @block.vector
        def _(dve):
            own, seen = Chain(dve, dve_own), Seen()
            state = dict(l=None)

            def await_full(name):
                dve.wait_ge(*(full(name) if state["l"] is None else full_l(name, state["l"])))

            def await_own(name):
                dve.wait_ge(*(emptied(name) if state["l"] is None else emptied_l(name, state["l"])))

            def leave(last, name):
                job, free = (JF, bank_free) if state["l"] is None else (JL, bank_free_l)
                last.then_inc(free[job[name][0]], 1)

            def bank(name):
                return banks[(JF if state["l"] is None else JL)[name][0]]

            def keep_scores(s, table):
                for tt in range(TT):
                    for h in range(HEADS):
                        n, r = f"{s}score{tt}{h}", tt * HEADS + h
                        await_full(n)
                        if state["l"] is not None:
                            dve.memset(negtop[:, r:r + 1], 0.0)
                        leave(dve.tensor_tensor_reduce(probs[:, tt, h, :], bank(n)[:, 0:T], table(tt, h), 1.0, LEAST,
                                                       ALU.add, ALU.max, top[:, r:r + 1]), n)
                    await_own(n)
                    r = slice(tt * HEADS, (tt + 1) * HEADS)
                    dve.tensor_scalar(negtop[:, r], top[:, r], -1.0, None, ALU.mult).then_inc(negmax_ready, 1)

            def normalise():
                for tt in range(TT):
                    dve.wait_ge(exp_done, seen(exp_done))
                    r = slice(tt * HEADS, (tt + 1) * HEADS)
                    own(dve.reciprocal(scale[:, r], total[:, r]))
                    for h in range(HEADS):
                        a = tt * HEADS + h
                        last = dve.tensor_scalar(probs[:, tt, h, :], probs[:, tt, h, :], scale[:, a:a + 1], None,
                                                 ALU.mult)
                    last.then_inc(prob_ready, 1)

            def row_scale():
                dve.wait_ge(roots, seen(roots))
                own(dve.reciprocal(rstd, root))

            def post_norm(names, gate, signal):
                mean_squares(names, gate, lambda last, j: leave(last, names[j]), bank)
                row_scale()
                await_own(names[-1])
                for tt in range(TT):
                    scaled(tt).then_inc(signal, 1)

            def mean_squares(names, gate, done, bank_of):
                for j, n in enumerate(names):
                    tt, half = j // 2, slice(512 * (j % 2), 512 * (j % 2) + 512)
                    dve.wait_ge(squares, seen(squares))
                    if j == 3:
                        pair = halves.rearrange("p (t a) -> p t a", t=TT)
                        dve.tensor_tensor(meansq, pair[:, :, 0], pair[:, :, 1], ALU.add).then_inc(means, 1)
                    done(dve.tensor_tensor(htok[:, tt, half], bank_of(n)[:, :], gate[:, half], ALU.mult), j)

            def scaled(tt, half=slice(0, D)):
                return dve.scalar_tensor_tensor(out=x[:, tt, half], in0=htok[:, tt, half], scalar=rstd[:, tt:tt + 1],
                                                in1=x[:, tt, half], op0=ALU.mult, op1=ALU.add)

            def await_x_mid():
                seen(x_mid)
                dve.wait_ge(x_mid, seen(x_mid))

            dve.memset(eps, EPS)
            dve.memset(zeros, 0.0)
            dve.memset(wfdup, 0.0)
            dve.memset(bforget, 0.0)
            dve.memset(rel33[BUCKETS:BUCKETS + 1, :], 1.0).then_inc(cleared, 1)
            await_full("cond")
            leave(dve.tensor_copy(condrep, bank("cond")[:, 0:KC].unsqueeze(2).broadcast_to([P, KC, 32])), "cond")
            dve.wait_ge(gpre_in, 16)

            def ada(r, takes):
                await_full(f"ada{r}")
                leave(dve.tensor_copy(modrows[r], bank(f"ada{r}")[:, :]), f"ada{r}")
                ada_rows(r, 0, takes)

            def ada_rows(r, first_row, takes):
                for j, what in enumerate(takes, first_row):
                    n, half = f"mod{4 * r + j}", slice(512 * (j % 2), 512 * (j % 2) + 512)
                    await_full(n)
                    leave(what(bank(n)[:, :], half), n)

            def shift(to):
                return lambda row, half: dve.tensor_copy(to[:, half], row)

            def gain(to, g):
                return lambda row, half: dve.scalar_tensor_tensor(out=to[:, half], in0=row, scalar=1.0,
                                                                  in1=g[:, half], op0=ALU.add, op1=ALU.mult)

            def gate(to, g):
                return lambda row, half: dve.tensor_tensor(to[:, half], row, g[:, half], ALU.mult)

            def modulated(gain_row, shift_row):
                for tt in range(TT):
                    own(dve.scalar_tensor_tensor(out=htok[:, tt, :], in0=x[:, tt, :], scalar=rstd[:, tt:tt + 1],
                                                 in1=gain_row, op0=ALU.mult, op1=ALU.mult))
                    dve.tensor_tensor(htok[:, tt, :], htok[:, tt, :], shift_row, ALU.add).then_inc(h_ready, 1)

            row_scale()
            ada(0, 2 * [shift(shift_m)] + 2 * [gain(gain_m, gpre_m)])
            await_own("mod1")
            await_own("mod3")
            modulated(gain_m, shift_m)

            def first_low(*numbers):
                for n in numbers:
                    dve.wait_ge(high_first, n + 1)
                    u = SPLIT_1[n]
                    high, low = first_halves(u)
                    dve.tensor_tensor(low, unit_at(u % RING), high.bitcast(F32), ALU.subtract).then_inc(low_first, 1)

            first_low(0)
            await_full("h3")
            for j in range(4):
                dve.wait_ge(hT_high, seen(hT_high))
                ks = slice(2 * j, 2 * j + 2)
                last = dve.tensor_tensor(hT1_lo[:, ks, :], bank(f"h{j}")[:, :].rearrange("p (k t) -> p k t", k=2),
                                         hT1_hi[:, ks, :].bitcast(F32), ALU.subtract)
                leave(last, f"h{j}")
            first_low(1)
            for l, to in enumerate((columns, next_columns)):
                await_full(f"columns{l}")
                leave(dve.tensor_copy(to[:, :], bank(f"columns{l}")[:, 0:COLUMNS]), f"columns{l}")
            dve.wait_ge(small_in, SMALL_IN)
            dve.wait_ge(cleared, 1)
            for a in (0, 32):
                last = dve.tensor_copy(wfdup[:, :, a:a + HEADS], wf)
            last.then_inc(forget_in, 1)
            first_low(2, 3)
            await_full("forget")
            leave(dve.tensor_scalar(fz, bank("forget")[0:40, 0:T], bforget[0:40, :], None, ALU.add), "forget")
            await_own("forget")
            dve.scalar_tensor_tensor(out=fa, in0=fz, scalar=-1.0, in1=fz, op0=ALU.mult, op1=ALU.max)\
                .then_inc(log_in, 1)
            own(dve.tensor_scalar(fm, fz, 0.0, None, ALU.min))
            dve.wait_ge(scan_in, 1)
            own(dve.tensor_tensor(fm, fm, fe, ALU.subtract))
            own(dve.tensor_tensor_scan(fcum, ones[0:40, 0:1].broadcast_to([40, T]), fm, 0.0, ALU.mult, ALU.add))
            own(dve.tensor_tensor(fox_rhs[32:40], fox_rhs[32:40], fcum[32:40].unsqueeze(1).broadcast_to([8, HEADS, T]),
                                  ALU.mult))
            dve.memset(fcum[32:40, :], 1.0).then_inc(fox_ready, 1)
            first_low(4, 5, 6)
            keep_scores("a", lambda tt, h: causal[:, tt, :])
            first_low(7)
            normalise()
            first_low(8, 9, 10, 11)

            def out_low(s):
                for p in range(PAIRS):
                    c = PAIRS * "ab".index(s) + p
                    dve.wait_ge(out_high, c + 1)
                    leave(dve.tensor_tensor(mix_lo[:, c, :], bank(f"{s}out{p}")[:, 0:T], mix_hi[:, c, :].bitcast(F32),
                                            ALU.subtract), f"{s}out{p}")

            out_low("a")
            dve.wait_ge(table_in, 32)
            keep_scores("b", lambda tt, h: tables[:, tt, h, :])
            normalise()
            ada(1, 2 * [gate(gate_m, gpost_m)] + 2 * [shift(shift_f)])
            first_low(len(IN1), len(IN1) + 1)
            out_low("b")
            first_low(len(IN1) + 2, len(IN1) + 3)
            post_norm([f"mix{j}" for j in range(4)], gate_m, x_mid)
            ada(2, 2 * [gain(gain_f, gpre_f)])
            await_own("mod9")
            await_x_mid()
            row_scale()
            modulated(gain_f, shift_f)
            ada_rows(2, 2, 2 * [gate(gate_f, gpost_f)])
            await_full("logits")
            leave(dve.tensor_tensor(logits, by_tile(bank("logits")[:, 0:TT * EXPERTS]),
                                    brt.unsqueeze(1).broadcast_to([P, TT, EXPERTS]), ALU.add), "logits")
            await_own("logits")
            for tt in range(TT):
                own(dve.max(best[:, tt, :], logits[:, tt, :]))
                own(dve.max_index(picked[:, 8 * tt:8 * tt + 8], best[:, tt, :], logits[:, tt, :]))
            own(dve.tensor_copy(bestf.rearrange("p t k -> p (t k)"), picked[:, :]))
            for tt in range(TT):
                last = dve.tensor_scalar(gate4[:, tt, :], best[:, tt, 0:TOPK], best[:, tt, 0:1], None, ALU.subtract)
            last.then_inc(gates_in, 1)
            for tt in range(TT):
                for k in range(TOPK):
                    last = dve.tensor_scalar(equal4[:, k, :], experts, bestf[:, tt, k:k + 1], None, ALU.is_equal)
                own(last)
                last = dve.tensor_reduce(chosen[:, tt, :], equal4.rearrange("p k e -> p e k"), AX_X, ALU.add)
                if tt < TT - 1:
                    own(last)
            last.then_inc(route_ready, 1)
            await_full("counts")
            leave(dve.tensor_copy(starts, bank("counts")[0:EXPERTS, 0:1]), "counts")
            await_own("counts")
            own(dve.tensor_scalar(nblk, starts, float(CAP), 1.0, ALU.is_gt, ALU.add))
            for p in range(2, T // CAP):
                last = dve.scalar_tensor_tensor(out=nblk, in0=starts, scalar=float(CAP * p), in1=nblk, op0=ALU.is_gt,
                                                op1=ALU.add)
                if p < T // CAP - 1:
                    own(last)
            last.then_inc(route_ready, 1)
            dve.wait_ge(gates_exp, 1)
            own(dve.reciprocal(gsum, gsum))
            for tt in range(TT):
                own(dve.tensor_scalar(gate4[:, tt, :], gate4[:, tt, :], gsum[:, tt:tt + 1], None, ALU.mult))
            for tt in range(TT):
                for k in range(TOPK):
                    last = dve.tensor_scalar(equalg[:, k, :], experts, bestf[:, tt, k:k + 1], gate4[:, tt, k:k + 1],
                                             ALU.is_equal, ALU.mult)
                own(last)
                own(dve.tensor_reduce(gates_te[:, tt, :], equalg.rearrange("p k e -> p e k"), AX_X, ALU.add))
            await_full("places")
            leave(dve.scalar_tensor_tensor(out=place, in0=by_tile(bank("places")[:, 0:TT * EXPERTS]), scalar=NOT_CHOSEN,
                                           in1=chosen, op0=ALU.add, op1=ALU.mult), "places")
            await_own("places")
            dve.tensor_scalar(place, place, -NOT_CHOSEN, None, ALU.add).then_inc(route_ready, 1)
            await_full("ends")
            leave(dve.tensor_copy(ends, bank("ends")[0:EXPERTS, 0:1]), "ends")
            await_own("ends")
            own(dve.tensor_tensor(starts, ends, nblk, ALU.subtract))
            dve.tensor_scalar(done_e, blocks[0:EXPERTS, :], ends, None, ALU.is_ge)
            own(dve.tensor_scalar(begun_e, blocks[0:EXPERTS, :], starts, None, ALU.is_ge))
            dve.tensor_tensor(onehot, begun_e, done_e, ALU.subtract).then_inc(route_ready, 1)
            own(dve.tensor_scalar(starts, starts, float(CAP), None, ALU.mult))
            await_full("turned")
            dve.tensor_scalar(posT, bank("turned")[0:EXPERTS, 0:T], starts, None, ALU.add)
            leave(dve.tensor_copy(gateT, bank("turned")[0:EXPERTS, T:2 * T]), "turned")
            await_full("list")
            leave(dve.tensor_copy(lists[0:1, 0:BLOCKS + 1 + EXPERTS], bank("list")[0:1, 0:BLOCKS + 1 + EXPERTS]), "list")
            for tt in range(TT):
                await_full(f"spread{tt}")
                dve.scalar_tensor_tensor(out=blkpos[:, tt, :], in0=blocks, scalar=-float(CAP),
                                         in1=bank(f"spread{tt}")[:, 0:BLOCKS + 1], op0=ALU.mult, op1=ALU.add)
                leave(dve.tensor_copy(blkgate[:, tt, :], bank(f"spread{tt}")[:, 64:64 + BLOCKS + 1]), f"spread{tt}")
            dve.tensor_copy(y_halves.rearrange("p a (b t) -> p (a b) t", t=T), zeros.unsqueeze(1).broadcast_to([P, 4, T]))\
                .then_inc(y_ready, 1)
            for tt in range(TT):
                await_own(f"spread{tt}")

            def select(at):
                for tt in range(TT):
                    last = dve.tensor_scalar(sel[:, tt, :], slots[:, 0:CAP], blkpos[:, tt, at], None, ALU.is_equal)
                last.then_inc(sel_ready, 1)

            select(slice(0, 1))
            await_own("list")
            n_blocks = dve.value_load(lists[0:1, BLOCKS + EXPERTS:BLOCKS + EXPERTS + 1], min_val=EXPERTS, max_val=BLOCKS)
            with dve.Fori(0, n_blocks) as i:
                own.loop(i, 2)
                for tt in range(TT):
                    dve.tensor_scalar(sel2[:, tt, :], slots, blkpos[:, tt, bass.ds(i, 1)], None, ALU.is_equal)
                dve.tensor_copy(gate_now.unsqueeze(2), blkgate[:, :, bass.ds(i, 1)]).then_inc(sel2_ready, 1)
                dve.wait_ge(gathered, i + 1)
                select(bass.ds(i + 1, 1))
                dve.wait_ge(hidden_done, i + 1)
                dve.tensor_scalar(glu, banks[4][:, :], SWIGLU_LIMIT, None, ALU.min).then_inc(clamped, 1)
                own(dve.tensor_scalar(lin, banks[5][:, :], -SWIGLU_LIMIT, SWIGLU_LIMIT, ALU.max, ALU.min))
                dve.wait_ge(clamped, i + 1)
                own(dve.scalar_tensor_tensor(out=lin1, in0=lin, scalar=1.0, in1=glu, op0=ALU.add, op1=ALU.mult))
                dve.wait_ge(sig_ready, i + 1)
                dve.tensor_tensor(act_row, lin1, sig, ALU.mult).then_inc(act_ready, 1)
                dve.wait_ge(y_high, i + 1)
                for half in range(2):
                    here, there = (slice(CAP * a, CAP * a + CAP) for a in (half, 1 - half))
                    last = dve.scalar_tensor_tensor(out=y_halves[there, half, :], in0=banks[6][here, :],
                                                    scalar=slot_gate[here, :], in1=y_halves[here, half, :].bitcast(F32),
                                                    op0=ALU.mult, op1=ALU.subtract)
                last.then_inc(y_ready, 1)
            own.loop_end(n_blocks)
            mean_squares(range(4), gate_f, lambda last, j: last.then_inc(bank_free_l[j], 1), lambda j: banks[j])
            dve.wait_ge(roots, seen(roots))
            for tt in range(TT):
                dve.reciprocal(rstd[:, tt:tt + 1], root[:, tt:tt + 1]).then_inc(bank_free_l[6 + tt], 1)
            dve.wait_ge(bank_free_l[7], 1)
            dve.wait_ge(bank_free_l[3], 1)
            for tt in range(TT):
                scaled(tt, slice(0, 512)).then_inc(bank_free_l[4 + tt], 1)
                scaled(tt, slice(512, D)).then_inc(layer_in, 1)

            def take_low(*units):
                for u in units:
                    dve.wait_ge(high_done, state["l"] * len(SPLIT) + (SPLIT.index(u) + 1))
                    high, low = split_halves(u)
                    dve.tensor_tensor(low, unit_at(u % RING_L), high.bitcast(F32), ALU.subtract).then_inc(low_done, 1)

            def hT_low(prefix, column):
                for j in range(4):
                    dve.wait_ge(hT_high, seen(hT_high))
                    for kk in range(2):
                        k = 2 * j + kk
                        last = dve.scalar_tensor_tensor(out=hT_lo[:, k, :], in0=bank(f"{prefix}{j}")[:, kk * T:kk * T + T],
                                                        scalar=column[:, k:k + 1], in1=hT_hi[:, k, :].bitcast(F32),
                                                        op0=ALU.mult, op1=ALU.subtract)
                    leave(last, f"{prefix}{j}")

            with dve.Fori(0, LAYERS) as l:
                state["l"] = l
                own.loop(l, DVE_LAYER)
                seen.loop(l)
                take_low(0)
                dve.wait_ge(layer_in, TT * l + TT)

                def normed():
                    row_scale()
                    for tt in range(TT):
                        dve.tensor_scalar(htok[:, tt, :], x[:, tt, :], rstd[:, tt:tt + 1], None, ALU.mult)\
                            .then_inc(h_ready, 1)

                normed()
                hT_low("h", c_pre)
                take_low(1, 2, 3, 4)
                await_own("kv")
                own(dve.tensor_tensor(qksq, qk, qk, ALU.mult))
                dve.tensor_reduce(qkms, qksq.rearrange("p t (h d) -> p (t h) d", d=DH), AX_X, ALU.add)\
                    .then_inc(qk_means, 1)
                dve.wait_ge(roots, seen(roots))
                own(dve.reciprocal(qkr, qkms))
                n_heads = HEADS + A_KV
                qk_heads = qk.rearrange("p t (h d) -> p (t h) d", d=DH)
                own(dve.tensor_tensor(qk_heads, qk_heads, qkr.unsqueeze(2).broadcast_to([P, TT * n_heads, DH]), ALU.mult))
                dve.wait_ge(params_in, 16 * PARAMS_IN * (l + 1))
                own(dve.tensor_tensor(qk, qk, gqk.unsqueeze(1).broadcast_to([P, TT, n_heads * DH]), ALU.mult))
                for tt in range(TT):
                    def heads(a):
                        return a[:, tt, :].rearrange("p (h d) -> p h d", d=DH)

                    def angle(name):
                        return by_tile(const(name))[:, tt, :]

                    dve.tensor_tensor(heads(rope1), heads(qk), angle("cos").unsqueeze(1).broadcast_to([P, n_heads, DH]),
                                      ALU.mult)
                    sin = angle("sin").rearrange("p (a b d) -> p a b d", a=2, b=2)
                    q5 = heads(qk).rearrange("p h (a b d) -> p h a b d", a=2, b=2)
                    r5 = heads(rope2).rearrange("p h (a b d) -> p h a b d", a=2, b=2)
                    for b in range(2):
                        last = dve.tensor_tensor(r5[:, :, :, b, :], q5[:, :, :, 1 - b, :],
                                                 sin[:, :, b, :].unsqueeze(1).broadcast_to([P, n_heads, 2, 16]), ALU.mult)
                own(last)
                dve.tensor_tensor(qk[:, :, 0:MIX], rope1[:, :, 0:MIX], rope2[:, :, 0:MIX], ALU.add)
                for tt in range(TT):
                    for c in range(2):
                        k1, k2 = (r[:, tt, MIX:].rearrange("p (g d) -> p g d", d=DH) for r in (rope1, rope2))
                        last = dve.tensor_tensor(kdup[:, tt, :, c, :], k1, k2, ALU.add)
                last.then_inc(rope_ready, 1)
                keep_scores("a", lambda tt, h: zeros)
                normalise()
                take_low(9, 10, 11, 12)
                dve.wait_ge(bias_masked, l + 1)
                keep_scores("c", lambda tt, h: tables[:, tt, h, :])
                normalise()
                take_low(*range(13, len(IN2)))
                await_own("gl11")
                for u in range(BRANCH_UNITS):
                    for i in range(2):
                        n, c = f"branch{u}{i}", 4 * (u % 2) + 2 * i
                        await_full(n)
                        part = gates[u // 2][:, c:c + 2, :]
                        leave(dve.tensor_tensor(part, bank(n)[:, :].rearrange("p (c t) -> p c t", c=2), part, ALU.mult), n)
                    if u == 3:
                        await_own("branch31")
                        own(dve.tensor_tensor(merged, gates[0], gates[1], ALU.add))
                    if u == 5:
                        take_low(FIRST_OUT + 1)
                    if u >= 4:
                        await_own(f"branch{u}1")
                        half = slice(KC // 2 * (u - 4), KC // 2 * (u - 3))
                        dve.tensor_tensor(hT_hi[:, half, :], merged[:, half, :], gates[2][:, half, :], ALU.add)
                        own(dve.tensor_tensor(merged[:, half, :], merged[:, half, :], gates[2][:, half, :], ALU.add))
                        dve.tensor_tensor(hT_lo[:, half, :], merged[:, half, :], hT_hi[:, half, :].bitcast(F32), ALU.subtract)\
                            .then_inc(branch_ready, 1)
                    if u == 4:
                        take_low(FIRST_OUT)
                take_low(FIRST_OUT + 2, FIRST_OUT + 3)
                post_norm([f"mix{j}" for j in range(4)], gpost2[0], x_mid)
                take_low(FIRST_UP)
                await_x_mid()
                normed()
                hT_low("g", c_ffn)
                take_low(FIRST_UP + 1)

                for c in range(UPAIRS):
                    for half, name in enumerate(("val", "gate")):
                        n, cv = f"{name}{c}", conv[2 * (c % 2) + half]
                        up = bank(n)[:, :].rearrange("p (m t) -> p m t", m=2)
                        take_low(FIRST_UP + 2 * (c + 1) + half)
                        dve.wait_ge(conv_in, seen(conv_in))
                        for m in range(2):
                            f = FT * half + 2 * c + m
                            last = dve.scalar_tensor_tensor(out=cv[:, m, 1:T], in0=up[:, m, 0:T - 1],
                                                            scalar=c_conv0(f), in1=cv[:, m, 1:T], op0=ALU.mult, op1=ALU.add)
                        own(last)
                        for m in range(2):
                            f = FT * half + 2 * c + m
                            last = dve.scalar_tensor_tensor(out=cv[:, m, 0:T - 1], in0=up[:, m, 1:T],
                                                            scalar=c_conv2(f), in1=cv[:, m, 0:T - 1], op0=ALU.mult, op1=ALU.add)
                        leave(last, n)
                take_low(*range(FIRST_DOWN + HALVES, N_UNITS))
                dve.tensor_copy(columns[:, :], next_columns[:, :])
                post_norm([f"down{j}" for j in range(4)], gpost2[1], layer_in)
                own.loop_end(LAYERS)
                seen.loop_end()

        @block.scalar
        def _(act):
            own, seen = Chain(act, act_own), Seen()
            state = dict(l=None)

            def await_full(name):
                act.wait_ge(*(full(name) if state["l"] is None else full_l(name, state["l"])))

            def bank(name):
                return banks[(JF if state["l"] is None else JL)[name][0]]

            def leave(last, name):
                job, free = (JF, bank_free) if state["l"] is None else (JL, bank_free_l)
                last.then_inc(free[job[name][0]], 1)

            def copy(name, to, scale=1.0, width=512):
                await_full(name)
                source = bank(name)[0:to.shape[0], 0:width]
                if len(to.shape) == 3:
                    source = source.rearrange("p (a b) -> p a b", a=to.shape[1])
                leave(act.activation(to, source, ACT.Copy, scale=scale), name)

            def exps():
                for tt in range(TT):
                    act.wait_ge(negmax_ready, seen(negmax_ready))
                    for h in range(HEADS):
                        r = slice(tt * HEADS + h, tt * HEADS + h + 1)
                        last = act.activation(probs[:, tt, h, :], probs[:, tt, h, :], ACT.Exp, bias=negtop[:, r],
                                              accum_out=total[:, r])
                    last.then_inc(exp_done, 1)

            def turn_and_out(s, chunk):
                for h in range(HEADS):
                    copy(f"{s}turn{h}", turned[:, h, :, :])
                for p in range(PAIRS):
                    copy(f"{s}out{p}", mixT[:, chunk + p, :], width=T)

            def take_root():
                act.activation(root, meansq, ACT.Sqrt, bias=eps).then_inc(roots, 1)

            def square_x(ready=None):
                for tt in range(TT):
                    if ready is not None:
                        ready(tt)
                    last = act.activation(htok[:, tt, :], x[:, tt, :], ACT.Square, scale=D ** -0.5,
                                          accum_out=meansq[:, tt:tt + 1])
                own(last)
                take_root()

            def x_mid_ready(tt):
                act.wait_ge(x_mid, seen(x_mid))

            def square_banks(sources, wait):
                act.activation(spare, eps, ACT.Sqrt)
                wait()
                for j, b in enumerate(sources):
                    act.activation(htok[:, j // 2, 512 * (j % 2):512 * (j % 2) + 512], b, ACT.Square, scale=D ** -0.5,
                                   accum_out=halves[:, j:j + 1]).then_inc(squares, 1)
                act.wait_ge(means, seen(means))
                take_root()

            act.dma_start(crow, c_in[0].rearrange("(k p) -> k p", p=P)).then_inc(cond_in, 16)
            act.dma_start(bada, b_ada[0].rearrange("(r n) -> r n", n=512)).then_inc(bada_in, 16)
            early = sum(table_at[n][1] for n in ("ident", "ones", "picks"))
            act.dma_start(consts[:, 0:early], shape_table[:, 0:early]).then_inc(consts_in, 16)
            act.dma_start(gpre_m, g_pre_mix[0].partition_broadcast(P)).then_inc(gpre_in, 16)
            act.wait_ge(cond_in, 16)
            act.activation(crow, crow, ACT.Silu).then_inc(cond_rows, 1)
            act.wait_ge(x_in_sem, 16)
            act.wait_ge(cleared, 1)
            square_x()
            act.wait_ge(unit_done, KC - 2)
            w_f = w_in[0].rearrange("(k p) n -> p k n", p=P)[:, :, 6 * MIX:6 * MIX + HEADS]
            loads = [(consts[:, early:], shape_table[:, early:]), (wf, w_f), (rel33[0:BUCKETS, :], rel_bias),
                     (bforget[0:HEADS, :], b_forget[0].rearrange("(h a) -> h a", a=1)),
                     (bforget[32:32 + HEADS, :], b_forget[0].rearrange("(h a) -> h a", a=1)),
                     (side[0:40, :], fox_table),
                     (gpost_m, g_post_mix[0].partition_broadcast(P)), (gpre_f, g_pre_ffn[0].partition_broadcast(P)),
                     (gpost_f, g_post_ffn[0].partition_broadcast(P)),
                     (wrt, w_router[0].rearrange("(k p) e -> p k e", p=P)), (brt, b_router[0].partition_broadcast(P))]
            assert 16 * len(loads) == SMALL_IN
            for to, source in loads:
                act.dma_start(to, source).then_inc(small_in, 16)

            def first_high(*numbers):
                for n in numbers:
                    u = SPLIT_1[n]
                    if HALVES <= n < len(IN1):
                        act.wait_ge(unit_done, SPLIT_1[n - HALVES] + 1)
                    act.wait_ge(*first_landed(u))
                    act.activation(first_halves(u)[0], unit_at(u % RING), ACT.Copy).then_inc(high_first, 1)

            first_high(0)
            for j in range(4):
                await_full(f"h{j}")
                act.activation(hT1_hi[:, 2 * j:2 * j + 2, :], bank(f"h{j}")[:, :].rearrange("p (k t) -> p k t", k=2),
                               ACT.Copy).then_inc(hT_high, 1)
            first_high(1)

            def projections(names, views):
                for n in names:
                    i = int(n[-1])
                    to = views[n[:-1]]
                    if n[0] == "v":
                        copy(n, to[:, :, 256 * i:256 * i + 256])
                    else:
                        copy(n, to[:, 2 * i:2 * i + 2, :], scale=QK_SCALE if n[0] == "q" else 1.0)

            for i in range(2):
                first_high(i + HALVES)
                projections([IN1[i]], proj1)
            copy("table", trow)
            act.wait_ge(log_in, 1)
            own(act.activation(fe, fa, ACT.Exp, scale=-1.0))
            act.activation(fe, fe, ACT.Ln, bias=ones[0:40, 0:1]).then_inc(scan_in, 1)
            for i in range(2, 6):
                first_high(i + HALVES)
                projections([IN1[i]], proj1)
            exps()
            for i in range(6, len(IN1)):
                if i + HALVES < len(IN1):
                    first_high(i + HALVES)
                projections([IN1[i]], proj1)

            def turn_and_out_high(s, between=()):
                for h in range(HEADS):
                    copy(f"{s}turn{h}", turned[:, h, :, :])
                first_high(*between)
                for p in range(PAIRS):
                    await_full(f"{s}out{p}")
                    act.activation(mix_hi[:, PAIRS * "ab".index(s) + p, :], bank(f"{s}out{p}")[:, 0:T], ACT.Copy)\
                        .then_inc(out_high, 1)

            turn_and_out_high("a")
            exps()
            turn_and_out_high("b", (len(IN1), len(IN1) + 1))
            first_high(len(IN1) + 2, len(IN1) + 3)
            square_banks([bank(f"mix{j}")[:, :] for j in range(4)], lambda: await_full("mix3"))
            square_x(x_mid_ready)
            for j in range(4):
                copy(f"g{j}", hT[:, 2 * j:2 * j + 2, :])
            act.wait_ge(gates_in, 1)
            for tt in range(TT):
                last = act.activation(gate4[:, tt, :], gate4[:, tt, :], ACT.Exp, accum_out=gsum[:, tt:tt + 1])
            last.then_inc(gates_exp, 1)
            act.wait_ge(*emptied("list"))
            n_blocks = act.value_load(lists[0:1, BLOCKS + EXPERTS:BLOCKS + EXPERTS + 1], min_val=EXPERTS, max_val=BLOCKS)
            act.activation(selT, zeros, ACT.Copy).then_inc(selT_ready, 1)

            def rows_out(n):
                act.wait_ge(gathered, n)
                act.activation(xrow, banks[6][:, :], ACT.Copy).then_inc(xrow_ready, 1)

            def rows_turned(n):
                act.wait_ge(xg_turned, n)
                act.activation(xgT.rearrange("p b j s -> p (b j s)"), banks[7][:, :], ACT.Copy).then_inc(xg_ready, 1)

            rows_out(1)
            rows_turned(1)
            with act.Fori(0, n_blocks) as i:
                act.wait_ge(clamped, i + 1)
                act.activation(sig, glu, ACT.Sigmoid, scale=SWIGLU_ALPHA).then_inc(sig_ready, 1)
                act.wait_ge(sel2_turned, i + 1)
                act.activation(selT, banks[7][:, 0:T], ACT.Copy)
                act.activation(slot_gate, banks[7][:, T:T + 1], ACT.Copy).then_inc(selT_ready, 1)
                rows_out(i + 2)
                act.wait_ge(act_turned, i + 1)
                act.activation(actT.rearrange("p b j s -> p (b j s)"), banks[7][:, :], ACT.Copy).then_inc(actT_ready, 1)
                rows_turned(i + 2)
                act.wait_ge(down_done, i + 1)
                for half in range(2):
                    here = slice(CAP * half, CAP * half + CAP)
                    last = act.activation(y_halves[here, half, :], banks[6][here, :], ACT.Copy, scale=slot_gate[here, :])
                last.then_inc(y_high, 1)
            square_banks([banks[j][:, :] for j in range(4)], lambda: act.wait_ge(moe_done, 1))

            with act.Fori(0, LAYERS) as l:
                state["l"] = l
                own.loop(l, 2)
                seen.loop(l)
                def take_high(*units):
                    for u in units:
                        act.wait_ge(*landed_unit(u, l))
                        n = SPLIT.index(u)
                        if n >= HALVES:
                            act.wait_ge(unit_done_l, l * N_UNITS + (SPLIT[n - HALVES] + 1 + RING_L))
                        act.activation(split_halves(u)[0], unit_at(u % RING_L), ACT.Copy).then_inc(high_done, 1)

                take_high(0)
                square_x(lambda tt: act.wait_ge(layer_in, TT * l + tt + 1))

                def turn_h(prefix, column):
                    for j in range(4):
                        await_full(f"{prefix}{j}")
                        for kk in range(2):
                            k = 2 * j + kk
                            last = act.activation(hT_hi[:, k, :], bank(f"{prefix}{j}")[:, kk * T:kk * T + T], ACT.Copy,
                                                  scale=column[:, k:k + 1])
                        last.then_inc(hT_high, 1)

                turn_h("h", c_pre)
                take_high(1)
                for i in range(2):
                    take_high(2 + i)
                    copy(f"qa{i}", qk[:, :, 256 * i:256 * i + 256])
                take_high(4)
                await_full("kv")
                kv = bank("kv")[:, :].rearrange("p (t n) -> p t n", t=TT)
                act.activation(qk[:, :, MIX:MIX + P], kv[:, :, 0:P], ACT.Copy)
                leave(act.activation(va2, kv[:, :, P:2 * P], ACT.Copy), "kv")
                take_high(5)
                copy("pu0", pu[:, :, 0:256])
                act.wait_ge(qk_means, seen(qk_means))
                act.activation(qkms, qkms, ACT.Sqrt, scale=1.0 / DH, bias=eps).then_inc(roots, 1)
                take_high(6)
                copy("pu1", pu[:, :, 256:512])
                views = dict(qc=qTc, kc=kTc, vc=vc)
                for u in (5, 6):
                    take_high(u + 2)
                    projections([IN2[u]], views)
                for g in range(4):
                    copy(f"diff{g}", diffT[:, g, :], width=T)
                for g in range(4):
                    n = f"pool{g}"
                    await_full(n)
                    leave(act.activation(mixT[:, 4 + g, :], bank(n)[:, 0:T], ACT.Copy, scale=c_pool[:, g:g + 1]), n)
                for i in range(2):
                    copy(f"qturn{i}", qTa[:, 2 * i:2 * i + 2, :], scale=QK_SCALE)
                copy("kturn", kTa)
                exps()
                for u in range(EARLY, 11):
                    take_high(u + 2)
                    projections([IN2[u]], views)
                turn_and_out("a", 0)
                exps()
                for i in range(12):
                    n = f"gl{i}"
                    if i < 10:
                        take_high(13 + i)
                    await_full(n)
                    for m in range(2):
                        f = 2 * i + m
                        last = act.activation(gates[f // KC][:, f % KC, :], bank(n)[:, m * T:m * T + T], ACT.Sigmoid,
                                              bias=c_gate[:, f:f + 1])
                    leave(last, n)
                turn_and_out("c", 8)
                take_high(*range(FIRST_OUT, FIRST_UP))
                square_banks([bank(f"mix{j}")[:, :] for j in range(4)], lambda: await_full("mix3"))
                take_high(FIRST_UP)
                square_x(x_mid_ready)
                turn_h("g", c_ffn)
                take_high(FIRST_UP + 1)

                def gelu(c):
                    act.wait_ge(*emptied_l(f"gate{c}", l))
                    cv = conv[2 * (c % 2) + 1]
                    act.activation(cv, cv, ACT.Gelu_apprx_tanh).then_inc(gelu_ready, 1)

                for c in range(UPAIRS):
                    if c >= 2:
                        act.wait_ge(conv_ready, l * (UPAIRS - 1) + (c - 1))
                    for half, name in enumerate(("val", "gate")):
                        n = f"{name}{c}"
                        take_high(FIRST_UP + 2 * (c + 1) + half)
                        await_full(n)
                        for m in range(2):
                            f = FT * half + 2 * c + m
                            last = act.activation(conv[2 * (c % 2) + half][:, m, :], bank(n)[:, m * T:m * T + T],
                                                  ACT.Identity, scale=c_conv1(f), bias=c_bias[:, f:f + 1])
                        last.then_inc(conv_in, 1)
                        if c and half == 0:
                            gelu(c - 1)
                gelu(UPAIRS - 1)
                take_high(*range(FIRST_DOWN + HALVES, N_UNITS))
                square_banks([bank(f"down{j}")[:, :] for j in range(4)], lambda: await_full("down3"))
                own.loop_end(LAYERS)
                seen.loop_end()

        @block.gpsimd
        def _(pool):
            own = Chain(pool, pool_own)
            def along(a, layer_):
                return a[layer_].rearrange("(f p) -> f p", p=P)

            for layer_ in range(LAYERS):
                conv_rows = conv_w[layer_].rearrange("c (f p) -> (c f) p", p=P)
                loads = [((0, 88), 0, conv_rows[0:88, :]), ((88, 112), 0, along(b_gate2, layer_)),
                         ((112, 120), 0, along(norm_mix_pre, layer_)), ((120, 128), 0, along(norm_ffn_pre, layer_)),
                         ((0, 44), 1, conv_rows[88:132, :]), ((44, 88), 1, along(conv_b, layer_)),
                         ((88, 92), 1, along(pool_scale, layer_))]
                assert len(loads) == COLUMNS_IN
                for rows, i, source in loads:
                    pool.dma_start(params[slice(*rows), layer_, i, :], source).then_inc(columns_in, 16)
            pool.wait_ge(h_ready, 1)
            for layer_ in range(LAYERS):
                pool.dma_start(rpb_copies[layer_], rpb[layer_].rearrange("h r c -> (h r c)").partition_broadcast(GRID_W))\
                    .then_inc(rpb_out, 16)
            for j in range(4):
                pool.wait_ge(*emptied(f"h{j}"))
            pool.tensor_tensor(hT, hT1_hi.bitcast(F32), hT1_lo.bitcast(F32), ALU.add).then_inc(hT_whole, 1)
            pool.wait_ge(*emptied("table"))
            pool.dma_start(distances.rearrange("q h d -> h q d"), trow.unsqueeze(1).broadcast_to([HEADS, P, 2 * T]))\
                .then_inc(table_out, 16)
            pool.wait_ge(table_out, 16)
            for tt in range(TT):
                pitch = HEADS * 2 * T
                shifted = bass.AP(distances.tensor, T - 1 - P * tt, [[pitch - 1, P], [2 * T, HEADS], [1, T]])
                pool.dma_start(tables[:, tt, :, :], shifted).then_inc(table_in, 16)
            pool.wait_ge(rpb_out, 16 * LAYERS)
            pitch = HEADS * RPB_HEAD
            for layer_ in range(LAYERS):
                for r in range(GRID_H):
                    for rk in range(GRID_H):
                        start = layer_ * GRID_W * pitch + (rk - r + NA_ROWS - 1) * RPB_ROW + NA_COLS - 1
                        source = bass.AP(rpb_copies.tensor, start, [[pitch - 1, GRID_W], [RPB_HEAD, HEADS], [1, GRID_W]])
                        to = neighbours[layer_, GRID_W * (r % 2):GRID_W * (r % 2) + GRID_W, r // 2, :,
                                        GRID_W * rk:GRID_W * rk + GRID_W]
                        pool.dma_start(to, source).then_inc(neighbours_out, 16)
            pool.wait_ge(h_ready, 4)
            pool.dma_start(bdown, b_down[0]).then_inc(bdown_in, 16)
            pool.tensor_copy(bias_r[96:100, 1024:1024 + 4 * CAP], pick4)
            with pool.Fori(0, EXPERTS) as e:
                pool.wait_ge(bias_in, 16 * e + 16)
                pool.tensor_tensor(bias_halves[0].rearrange("r (a t) -> r a t", t=T), brows.rearrange("r (a t) -> r a t", t=T),
                                   zeros[96:100, :].unsqueeze(1).broadcast_to([4, 2, T]), ALU.add).then_inc(bias_high, 1)
                pool.wait_ge(bias_high, e + 1)
                pool.tensor_tensor(bias_halves[1], brows, bias_halves[0].bitcast(F32), ALU.subtract).then_inc(bias_ready, 1)
            pool.wait_ge(neighbours_out, 16 * LAYERS * GRID_H * GRID_H)
            with pool.Fori(0, LAYERS) as l:
                one = bass.ds(l, 1)
                pool.wait_ge(layer_in, TT * l + TT)

                def over_heads(a, n):
                    return a[one].rearrange("l d -> (l d)").unsqueeze(0).broadcast_to([n, DH]).partition_broadcast(P)

                loads = [(gqk[:, 0:MIX].rearrange("p (h d) -> p h d", d=DH), over_heads(qk_q, HEADS)),
                         (gqk[:, MIX:].rearrange("p (h d) -> p h d", d=DH), over_heads(qk_k, A_KV)),
                         (wpool, w_pool[one].rearrange("l g c d -> (l c) g d")),
                         (gpost2[0], norm_mix_post[one].rearrange("l d -> (l d)").partition_broadcast(P)),
                         (gpost2[1], norm_ffn_post[one].rearrange("l d -> (l d)").partition_broadcast(P))]
                assert len(loads) == PARAMS_IN
                for to, source in loads:
                    pool.dma_start(to, source).then_inc(params_in, 16)
                pool.dma_start(tables.rearrange("p t h k -> p (t h k)"),
                               neighbours[one].rearrange("l p t h k -> (l p) (t h k)")).then_inc(bias_l_in, 16)
                pool.wait_ge(bias_l_in, 16 * (l + 1))
                groups = tables.rearrange("p t h (r c) -> p (t h r) c", c=GRID_W)
                pool.tensor_tensor(groups, groups, const("window").unsqueeze(1).broadcast_to(
                    [P, TT * HEADS * GRID_H, GRID_W]), ALU.add).then_inc(bias_masked, 1)
                for u in POOL_LOW:
                    pool.wait_ge(high_done, l * len(SPLIT) + (SPLIT.index(u) + 1))
                    high, low = split_halves(u)
                    pool.tensor_tensor(low, unit_at(u % RING_L), high.bitcast(F32), ALU.subtract).then_inc(low_done_pool, 1)
                own.loop(l, 2 * UPAIRS)
                for c in range(UPAIRS):
                    pool.wait_ge(gelu_ready, l * UPAIRS + (c + 1))
                    value, gate = conv[2 * (c % 2)], conv[2 * (c % 2) + 1]
                    high = gated_hi[:, 2 * c:2 * c + 2, :]
                    own(pool.tensor_tensor(high, value, gate, ALU.mult))
                    own(pool.tensor_tensor(value, value, gate, ALU.mult))
                    pool.tensor_tensor(gated_lo(2 * c, 2), value, high.bitcast(F32), ALU.subtract)\
                        .then_inc(conv_ready if c < UPAIRS - 1 else gated_ready, 1)
                own.loop_end(LAYERS)


_INS = ["x", "c", "w_ada", "b_ada", "g_pre_mix", "g_post_mix", "w_in", "b_forget", "rel_bias", "w_out", "g_pre_ffn",
        "g_post_ffn", "w_router", "b_router", "w_gate_up", "b_gate_up", "w_down", "b_down", "norm_mix_pre_2",
        "norm_mix_post_2", "norm_ffn_pre_2", "norm_ffn_post_2", "w_in_2", "b_gate_2", "qk_norm_q_2", "qk_norm_k_2",
        "w_pool_2", "pool_scale_2", "rpb_2", "w_branch_2", "w_out_2", "w_up_2", "conv_w_2", "conv_b_2", "w_down_2"]


def kernel(**inputs):
    import concourse.bacc as bacc
    from concourse.bass_utils import run_bass_kernel_spmd

    nc = bacc.Bacc("TRN2", target_bir_lowering=False, num_devices=1)
    table, table_at, fox = shape_tables()
    arrays, args = {}, []
    for name in _INS:
        arrays[f"in_{name}"] = np.ascontiguousarray(inputs[name])
    arrays["shape_table"], arrays["fox_table"] = table, fox
    for name, a in arrays.items():
        args.append(nc.dram_tensor(name, a.shape, mybir.dt.from_np(a.dtype), kind="ExternalInput").ap())
    args.append(nc.dram_tensor("out_x", (1, T, D), F32, kind="ExternalOutput").ap())
    build(nc, *args, table_at)
    return run_bass_kernel_spmd(nc, [arrays], core_ids=[0]).results[0]["out_x"]
```
